# Optimizing a Trainium2 kernel written in Bass

```python
import jax, jax.numpy as jnp
from jax import lax
import numpy as np

D_MODEL = 2048
BATCH = 1
SEQ = 256
DEPTH = 1

N_HEADS = 16
N_KV_HEADS = 4
HEAD_DIM = 128
Q_PER_KV = N_HEADS // N_KV_HEADS
Q_BLOCK = 128
ROPE_THETA = 10000.0
GRID_W = 64
ATTN_Q_DIM = N_HEADS * HEAD_DIM
ATTN_KV_DIM = N_KV_HEADS * HEAD_DIM
N_FOURIER_GROUPS = 4
FOURIER_GROUP_DIM = 256
FOURIER_DIM = N_FOURIER_GROUPS * FOURIER_GROUP_DIM
IN_PROJ_DIM = ATTN_Q_DIM + 2 * ATTN_KV_DIM + FOURIER_DIM + 2 * D_MODEL
N_GROUPS = 4
EXPERTS_PER_GROUP = 8
N_EXPERTS = N_GROUPS * EXPERTS_PER_GROUP
TOP_K_IN_GROUP = 2
EXPERT_FF = 512
NORM_EPS = 1e-6

kernel_name = "hybrid_gqa_fnet_hmoe_block"

def rmsnorm(x, g):
    xf = x.astype(jnp.float32)
    y = xf * lax.rsqrt(jnp.mean(xf * xf, axis=-1, keepdims=True) + NORM_EPS)
    return (y * g.astype(jnp.float32)).astype(x.dtype)

def axial_rope_tables(seq):
    rows = seq // GRID_W
    row = jnp.repeat(jnp.arange(rows, dtype=jnp.float32), GRID_W)
    col = jnp.tile(jnp.arange(GRID_W, dtype=jnp.float32), rows)
    n_freq = HEAD_DIM // 4
    inv = ROPE_THETA ** (-jnp.arange(n_freq, dtype=jnp.float32) / n_freq)
    ang_r = row[:, None] * inv
    ang_c = col[:, None] * inv
    ang = jnp.concatenate([ang_r, ang_r, ang_c, ang_c], axis=-1)
    return jnp.cos(ang), jnp.sin(ang)

def apply_axial_rope(x, cos, sin):
    xs = x.reshape(x.shape[:-1] + (2, 2, HEAD_DIM // 4))
    rot = jnp.stack([-xs[..., 1, :], xs[..., 0, :]], axis=-2).reshape(x.shape)
    return (x.astype(jnp.float32) * cos + rot.astype(jnp.float32) * sin).astype(x.dtype)

def blocked_gqa(q, k, v):
    b, kvh, g, s, d = q.shape
    nb = s // Q_BLOCK
    scale = HEAD_DIM ** -0.5
    qb = jnp.moveaxis(q.reshape(b, kvh, g, nb, Q_BLOCK, d), 3, 0)

    def attend(qblk):
        sc = jnp.einsum('bkgqd,bksd->bkgqs', qblk, k).astype(jnp.float32) * scale
        p = jax.nn.softmax(sc, axis=-1).astype(v.dtype)
        return jnp.einsum('bkgqs,bksd->bkgqd', p, v)

    o = lax.map(attend, qb)
    o = jnp.transpose(o, (1, 0, 4, 2, 3, 5))
    return o.reshape(b, s, kvh * g * d)

def fourier_mix(f):
    b, s, _ = f.shape
    fg = f.astype(jnp.float32).reshape(b, s, N_FOURIER_GROUPS, FOURIER_GROUP_DIM)
    out = jnp.real(jnp.fft.fft2(fg, axes=(1, 3), norm="ortho"))
    return out.reshape(b, s, FOURIER_DIM).astype(f.dtype)

def hierarchical_moe(h, w_group_router, b_group_router, w_expert_router, b_expert_router,
                     w_exp_gate, w_exp_up, w_exp_down):
    b, s, d = h.shape
    ht = h.reshape(b * s, d)
    gl = (ht @ w_group_router + b_group_router).astype(jnp.float32)
    gp = jax.nn.softmax(gl, axis=-1)
    g_idx = jnp.argmax(gp, axis=-1)
    g_w = jnp.max(gp, axis=-1)
    el = (ht @ w_expert_router + b_expert_router).astype(jnp.float32)
    el = el.reshape(-1, N_GROUPS, EXPERTS_PER_GROUP)
    sel = jnp.take_along_axis(el, g_idx[:, None, None], axis=1)[:, 0]
    ep = jax.nn.softmax(sel, axis=-1)
    top_v, top_i = lax.top_k(ep, TOP_K_IN_GROUP)
    top_v = top_v / jnp.sum(top_v, axis=-1, keepdims=True)
    e_idx = g_idx[:, None] * EXPERTS_PER_GROUP + top_i
    combine = g_w[:, None] * jnp.sum(top_v[..., None] * jax.nn.one_hot(e_idx, N_EXPERTS, dtype=jnp.float32), axis=1)
    combine = combine.astype(h.dtype)
    out = jnp.zeros_like(ht)
    for e in range(N_EXPERTS):
        y = (jax.nn.silu(ht @ w_exp_gate[e]) * (ht @ w_exp_up[e])) @ w_exp_down[e]
        out = out + combine[:, e:e + 1] * y
    return out.reshape(b, s, d)

def setup_inputs(seed: int = 0) -> dict:
    key = jax.random.key(seed)
    ks = jax.random.split(key, 24)
    f32 = jnp.float32

    def w(k, shape, fan_in, mult=1.0):
        return jax.random.normal(k, shape, f32) * (mult * fan_in ** -0.5)

    def gain(k, shape):
        return 1.0 + 0.05 * jax.random.normal(k, shape, f32)

    return {
        "x": jax.random.normal(ks[0], (BATCH, SEQ, D_MODEL), f32),
        "c": jax.random.normal(ks[1], (BATCH, D_MODEL), f32),
        "w_ada": w(ks[2], (D_MODEL, 6 * D_MODEL), D_MODEL, 0.5),
        "b_ada": 0.02 * jax.random.normal(ks[3], (6 * D_MODEL,), f32),
        "g_pre_mix": gain(ks[4], (D_MODEL,)),
        "g_post_mix": gain(ks[5], (D_MODEL,)),
        "w_in": w(ks[6], (D_MODEL, IN_PROJ_DIM), D_MODEL),
        "q_norm_g": gain(ks[7], (HEAD_DIM,)),
        "k_norm_g": gain(ks[8], (HEAD_DIM,)),
        "w_attn_out": w(ks[9], (ATTN_Q_DIM, D_MODEL), ATTN_Q_DIM),
        "w_fourier_out": w(ks[10], (FOURIER_DIM, D_MODEL), FOURIER_DIM),
        "w_mix_out": w(ks[11], (D_MODEL, D_MODEL), D_MODEL),
        "g_pre_ffn": gain(ks[12], (D_MODEL,)),
        "g_post_ffn": gain(ks[13], (D_MODEL,)),
        "w_group_router": w(ks[14], (D_MODEL, N_GROUPS), D_MODEL),
        "b_group_router": 0.01 * jax.random.normal(ks[15], (N_GROUPS,), f32),
        "w_expert_router": w(ks[16], (D_MODEL, N_EXPERTS), D_MODEL),
        "b_expert_router": 0.01 * jax.random.normal(ks[17], (N_EXPERTS,), f32),
        "w_exp_gate": w(ks[18], (N_EXPERTS, D_MODEL, EXPERT_FF), D_MODEL),
        "w_exp_up": w(ks[19], (N_EXPERTS, D_MODEL, EXPERT_FF), D_MODEL),
        "w_exp_down": w(ks[20], (N_EXPERTS, EXPERT_FF, D_MODEL), EXPERT_FF),
    }

def reference(x, c, w_ada, b_ada, g_pre_mix, g_post_mix, w_in, q_norm_g, k_norm_g,
              w_attn_out, w_fourier_out, w_mix_out, g_pre_ffn, g_post_ffn,
              w_group_router, b_group_router, w_expert_router, b_expert_router,
              w_exp_gate, w_exp_up, w_exp_down):
    b, s, d = x.shape
    cos, sin = axial_rope_tables(s)

    for _ in range(DEPTH):
        mod = jax.nn.silu(c) @ w_ada + b_ada
        sh1, sc1, gt1, sh2, sc2, gt2 = [m[:, None, :] for m in jnp.split(mod, 6, axis=-1)]

        h = rmsnorm(x, g_pre_mix) * (1.0 + sc1) + sh1
        proj = h @ w_in
        o1 = ATTN_Q_DIM
        o2 = o1 + ATTN_KV_DIM
        o3 = o2 + ATTN_KV_DIM
        o4 = o3 + FOURIER_DIM
        o5 = o4 + D_MODEL
        q = proj[..., :o1].reshape(b, s, N_KV_HEADS, Q_PER_KV, HEAD_DIM)
        k = proj[..., o1:o2].reshape(b, s, N_KV_HEADS, HEAD_DIM)
        v = proj[..., o2:o3].reshape(b, s, N_KV_HEADS, HEAD_DIM)
        f_in = proj[..., o3:o4]
        gate_attn = jax.nn.sigmoid(proj[..., o4:o5])
        gate_four = jax.nn.sigmoid(proj[..., o5:])

        q = apply_axial_rope(rmsnorm(jnp.transpose(q, (0, 2, 3, 1, 4)), q_norm_g), cos, sin)
        k = apply_axial_rope(rmsnorm(jnp.transpose(k, (0, 2, 1, 3)), k_norm_g), cos, sin)
        v = jnp.transpose(v, (0, 2, 1, 3))
        attn = blocked_gqa(q, k, v) @ w_attn_out

        four = fourier_mix(f_in) @ w_fourier_out

        mixed = (gate_attn * attn + gate_four * four) @ w_mix_out
        x = x + gt1 * rmsnorm(mixed, g_post_mix)

        h2 = rmsnorm(x, g_pre_ffn) * (1.0 + sc2) + sh2
        ffn = hierarchical_moe(h2, w_group_router, b_group_router, w_expert_router, b_expert_router,
                               w_exp_gate, w_exp_up, w_exp_down)
        x = x + gt2 * rmsnorm(ffn, g_post_ffn)
    return x


_drawn_inputs = setup_inputs


def setup_inputs(seed=0):
    import zlib

    import numpy as np

    out = dict(_drawn_inputs(seed))
    spreads = {}
    factors = {'q_norm_g': 2.812,
     'k_norm_g': 3.137,
     'g_post_ffn': 3.921,
     'b_group_router': 8.0,
     'b_expert_router': 5.041}
    for name, (base, spread) in spreads.items():
        noise = np.random.default_rng([zlib.crc32(name.encode()), seed]).standard_normal(out[name].shape)
        drawn = base * np.exp(spread * noise) if base else spread * noise
        out[name] = __import__('jax').numpy.asarray(drawn.astype(out[name].dtype))
    for name, factor in factors.items():
        out[name] = (out[name] * factor).astype(out[name].dtype)
    return out
```

```python
from contextlib import ExitStack

import concourse.bass as bass
from concourse import mybir

ALU = mybir.AluOpType
ACT = mybir.ActivationFunctionType
F32 = mybir.dt.float32
I32 = mybir.dt.int32
AX_X = mybir.AxisListType.X

P = 128
D = 2048
SEQ = 256
TT = SEQ // P
KD = D // P
CW = 512
ND = D // CW
HD = 128
NH = 16
NKV = 4
HPC = CW // HD
FD = 1024
FG = 256
KF = FD // P
Q_CHUNKS = NH * HD // CW
NE = 32
NG = 4
EG = NE // NG
FF = 512
KFF = FF // P
NR = NG + NE
SLOTS = 64
CAP = 64
BMAX = (SEQ - 1) // CAP
NCAND = BMAX * NE
NOVER = 8
NBLK = NE + NOVER
EPS = 1e-6
SCALE = float(HD) ** -0.5
FAR = 1e37
MIX_SLOTS = 4
RING = 6
HK = 8
ADA_SLOTS = 4
ADA_K = KD // ADA_SLOTS
N_ADA = 6 * ND


class Order:

    def __init__(self, eng, sem, base=0):
        self.eng, self.sem, self.base, self.n = eng, sem, base, 0

    def __call__(self, ins):
        ins.then_inc(self.sem, 1)
        self.n += 1
        self.eng.wait_ge(self.sem, self.base + self.n)


def build(nc, x, c, w_ada, b_ada, g_pre_mix, g_post_mix, w_in, q_norm_g, k_norm_g, w_attn_out, w_fourier_out,
          w_mix_out, g_pre_ffn, g_post_ffn, w_group_router, b_group_router, w_expert_router, b_expert_router,
          w_exp_gate, w_exp_up, w_exp_down, k_cos, k_sin, k_dft_tok, k_dft_ch, k_ident, k_upper, k_row, out):
    mods_dram = nc.dram_tensor("mods_scratch", (N_ADA, CW), F32, kind="Internal").ap()
    with ExitStack() as ctx:
        def sb(name, n, dt=F32):
            return ctx.enter_context(nc.sbuf_tensor(name, [P, n], dt))

        def sem(name):
            return ctx.enter_context(nc.semaphore(name))

        ring = [sb(f"ring{s}", HK * CW) for s in range(RING)]
        ada_w = sb("ada_w", ADA_SLOTS * ADA_K * CW)
        x_sb = sb("x_sb", TT * D)
        r_h = sb("r_h", KD * SEQ)
        r_q = sb("r_q", KD * SEQ)
        r_kvf = sb("r_kvf", KD * SEQ)
        gate = sb("gate", TT * CW)
        acc = sb("acc", 2 * CW)
        b_all = sb("b_all", CW)
        ident = sb("ident", P)
        ones = sb("ones", P)
        cos_t = sb("cos_t", TT * HD)
        sin_t = sb("sin_t", TT * HD)
        small = sb("small", 160)
        meta = sb("meta", 16, I32)
        bank = [ctx.enter_context(nc.psum_tensor(f"bank{b}", [P, CW], F32)) for b in range(8)]

        x3 = x_sb[:, :].rearrange("p (t d) -> p t d", t=TT)
        hT = r_h[:, :].rearrange("p (k s) -> p k s", k=KD)
        y1 = r_h[:, :].rearrange("p (t d) -> p t d", t=TT)
        h_tok = r_q[:, :].rearrange("p (t d) -> p t d", t=TT)
        qT = r_q[:, :].rearrange("p (h s) -> p h s", h=NH)
        kT = r_kvf[:, 0:NKV * SEQ].rearrange("p (h s) -> p h s", h=NKV)
        v_sb = r_kvf[:, 1024:2048].rearrange("p (t d) -> p t d", t=TT)
        f_sb = r_kvf[:, 2048:4096].rearrange("p (t d) -> p t d", t=TT)
        fT = r_kvf[:, 2048:4096].rearrange("p (k s) -> p k s", k=KF)
        g_pre = r_kvf[:, 0:D]
        h2T = r_kvf[:, :].rearrange("p (k s) -> p k s", k=KD)
        gate3 = gate[:, :].rearrange("p (t d) -> p t d", t=TT)
        a_row = gate[:, 0:CW]
        accs = [acc[:, j * CW:(j + 1) * CW] for j in range(2)]
        cos3 = cos_t[:, :].rearrange("p (t d) -> p t d", t=TT)
        sin3 = sin_t[:, :].rearrange("p (t d) -> p t d", t=TT)
        ada3 = [ada_w[:, s * ADA_K * CW:(s + 1) * ADA_K * CW].rearrange("p (k n) -> p k n", k=ADA_K)
                for s in range(ADA_SLOTS)]
        rows = [ada_w[:, s * D:(s + 1) * D] for s in range(4)]
        ring3 = [r[:, :].rearrange("p (k n) -> p k n", k=HK) for r in ring]
        raw = ring[4][:, 0:1024].rearrange("p (t n) -> p t n", t=TT)
        qr = ring[4][:, 1024:2048].rearrange("p (t n) -> p t n", t=TT)
        rope_tmp = ring[4][:, 2048:2560]
        rope_junk = ring[4][:, 2560:2560 + CW]
        ab = ring[4][:, :].rearrange("p (i n) -> p i n", i=KF)
        dft_tok = ring[5][:, 0:1024].rearrange("p (t n) -> p t n", t=TT)
        dft_ch = ring[5][:, 1024:2048].rearrange("p (t n) -> p t n", t=TT)
        cosg = [ring[5][:, 2048 + 256 * a:2304 + 256 * a].rearrange("p (t n) -> p t n", t=TT) for a in range(2)]
        sing = [ring[5][:, 2560 + 256 * a:2816 + 256 * a].rearrange("p (t n) -> p t n", t=TT) for a in range(2)]
        g_qk = ring[5][:, 3072:3072 + 2 * HD].rearrange("p (a n) -> p a n", a=2)
        probs = [ring[5][:, 2048 + 512 * b:2560 + 512 * b].rearrange("p (t s) -> p t s", t=TT) for b in range(2)]
        pT = [ring[5][:, 3072 + 512 * b:3584 + 512 * b].rearrange("p (s q) -> p s q", s=TT) for b in range(2)]
        mixed = ring[5][:, :].rearrange("p (t d) -> p t d", t=TT)
        mT = qT
        wr = gate[:, 0:KD * NR].rearrange("p (k n) -> p k n", k=KD)
        upper = gate[:, 576:704]
        krow = gate[:, 704:704 + k_row.shape[0]]

        cs = small[:, 0:KD]
        s_col = small[:, 16:32]
        ss = small[:, 32:40]
        rstd = small[:, 40:48]
        mx = small[:, 48:52]
        nmx = small[:, 52:56]
        rs = small[:, 56:60]
        rinv = small[:, 60:64]
        rms_q = small[:, 64:64 + TT * HPC]
        eps = small[:, 72:73]
        junk4 = small[:, 74:74 + TT * ND]
        rb = small[0:1, 96:96 + NR]

        w_ada_v = w_ada.rearrange("(k p) n -> p k n", p=P)
        w_in_v = w_in.rearrange("(k p) n -> p k n", p=P)
        ao_v = w_attn_out.rearrange("(k p) n -> p k n", p=P)
        fo_v = w_fourier_out.rearrange("(k p) n -> p k n", p=P)
        mo_v = w_mix_out.rearrange("(k p) n -> p k n", p=P)
        x_v = x.rearrange("b (t p) d -> p (b t) d", p=P)
        out_v = out.rearrange("b (t p) d -> p (b t) d", p=P)

        def bc_row(v):
            return v.rearrange("(a n) -> a n", a=1).partition_broadcast(P) if len(v.shape) == 1 else v.partition_broadcast(P)

        def row_of(v):
            return v.rearrange("(a n) -> a n", a=1)

        x_ready = sem("x_ready")
        c_ready = sem("c_ready")
        mod_consts = sem("mod_consts")
        rope_consts = sem("rope_consts")
        dft_ready = sem("dft_ready")
        ones_ready = sem("ones_ready")
        silu_c_ready = sem("silu_c_ready")
        ada_ready = [sem(f"ada_ready{s}") for s in range(ADA_SLOTS)]
        ada_late = [sem(f"ada_late{s}") for s in range(ADA_SLOTS)]
        ada_free = [sem(f"ada_free{s}") for s in range(ADA_SLOTS)]
        ada_sum_ready = sem("ada_sum_ready")
        ada_reduced = sem("ada_reduced")
        ada_row_out = sem("ada_row_out")
        row_stored = [sem(f"row_stored{s}") for s in range(2)]
        sumsq_ready = sem("sumsq_ready")
        root_x, root_qk, root_y, root_x1, root_out = (sem(f"root_{v}") for v in ("x", "qk", "y", "x1", "out"))
        eps_ready = sem("eps_ready")
        y1_sum = sem("y1_sum")
        h_ready = sem("h_ready")
        tr_done = sem("tr_done")
        tr_out = sem("tr_out")
        slot_ready = [sem(f"slot_ready{s}") for s in range(RING)]
        slot_free = [sem(f"slot_free{s}") for s in range(RING)]
        mm_done = sem("mm_done")
        mm_out = [sem(f"mm_out{s}") for s in range(2)]
        rope_done = sem("rope_done")
        score_done = sem("score_done")
        nmx_ready = sem("nmx_ready")
        exp_done = sem("exp_done")
        probs_ready = sem("probs_ready")
        pt_done = sem("pt_done")
        pt_ready = sem("pt_ready")
        pv_done = sem("pv_done")
        attn_ready = sem("attn_ready")
        f1_done = sem("f1_done")
        ab_ready = [sem("ab_ready_act"), sem("ab_ready_dve")]
        f2_done = sem("f2_done")
        fT_ready = [sem("fT_ready_act"), sem("fT_ready_dve")]
        mixed_ready = sem("mixed_ready")
        y1_ready = sem("y1_ready")
        gg1_ready = sem("gg1_ready")
        rows_a = sem("rows_a")
        rows_b = sem("rows_b")
        rows_c = sem("rows_c")
        x1_ready = sem("x1_ready")
        x1_sumsq = sem("x1_sumsq")
        h2_ready = sem("h2_ready")
        route_consts = sem("route_consts")
        logits_done = sem("logits_done")
        shifted_ready = sem("shifted_ready")
        route_exp = sem("route_exp")
        member_ready = sem("member_ready")
        ranks_done = sem("ranks_done")
        flags_ready = sem("flags_ready")
        flagsT_done = sem("flagsT_done")
        flagsT_ready = sem("flagsT_ready")
        prefix_done = sem("prefix_done")
        meta_ready = sem("meta_ready")
        p_ready = sem("p_ready")
        pw_ready = sem("pw_ready")
        gather_done = sem("gather_done")
        xg_ready = sem("xg_ready")
        st_done = sem("st_done")
        s_ready = sem("s_ready")
        gu_done = sem("gu_done")
        gu_ready = sem("gu_ready")
        gut_done = sem("gut_done")
        silu_ready = sem("silu_ready")
        act_ready = sem("act_ready")
        down_done = sem("down_done")
        y_ready = sem("y_ready")
        scat_done = sem("scat_done")
        scat_out = [sem("scat_out_even"), sem("scat_out_odd")]
        acc_sumsq = sem("acc_sumsq")
        out_ready = sem("out_ready")
        out_stored = sem("out_stored")
        o_dve = sem("o_dve")

        halves = []
        for n in range(8):
            halves += [(w_in_v, k, n) for k in (0, HK)]
        for n in range(ND):
            halves += [(w_in_v, k, 8 + n) for k in (0, HK)] + [(ao_v, k, n) for k in (0, HK)]
        for n in range(ND):
            halves += [(w_in_v, k, 12 + n) for k in (0, HK)] + [(fo_v, 0, n)]
        for n in range(ND):
            halves += [(mo_v, k, n) for k in (0, HK)]
        N_HALVES = len(halves)
        assert N_HALVES % MIX_SLOTS == 0
        MIX_USES = N_HALVES // MIX_SLOTS

        owner = []
        for g in range(8):
            owner += [(g, False), (g, True)]
        for n in range(ND):
            owner += [(8 + 2 * n, False), (8 + 2 * n, True), (9 + 2 * n, False), (9 + 2 * n, True)]
        for n in range(ND):
            owner += [(16 + 2 * n, False), (16 + 2 * n, True), (17 + 2 * n, True)]
        for n in range(ND):
            owner += [(24 + n, False), (24 + n, True)]

        def frees(s, upto):
            return sum(1 for r in range(s, upto + 1, MIX_SLOTS) if not owner[r][1])

        def half_used(r):
            g, last = owner[r]
            return (mm_done, g + 1) if last else (slot_free[r % MIX_SLOTS], frees(r % MIX_SLOTS, r))

        def ada_col(j):
            return (j % 2) * D + (j // 2) * CW if j < 2 * ND else j * CW

        def ada_load(eng, j, ready):
            for s in range(ADA_SLOTS):
                if j >= 1 and s < ADA_SLOTS - 1:
                    eng.wait_ge(ada_free[s], j)
                elif j >= 1:
                    eng.wait_ge(ada_sum_ready, j)
                eng.dma_start(ada3[s], w_ada_v[:, s * ADA_K:(s + 1) * ADA_K, ada_col(j):ada_col(j) + CW])\
                   .then_inc(ready[s], 16)

        M_H, M_Q, M_MIX, M_H2 = 0, 2 * ND, 2 * ND + 2 * (Q_CHUNKS + 1), 4 * ND + 2 * (Q_CHUNKS + 1)
        G_S4, G_S5, G_S6 = 8, 16, 24

        block = ctx.enter_context(nc.Block())

        @block.sync
        def _(sp):
            sp.dma_start(x3, x_v).then_inc(x_ready, 16)
            sp.dma_start(cs, c.rearrange("b (k p) -> p (b k)", p=P), allow_slow_non_contiguous=True).then_inc(c_ready, 16)
            sp.dma_start(ident[:, :], k_ident).then_inc(mod_consts, 16)
            sp.dma_start(b_all[0:N_ADA, :], b_ada.rearrange("(j n) -> j n", n=CW)).then_inc(mod_consts, 16)
            sp.dma_start(g_pre, bc_row(g_pre_mix)).then_inc(mod_consts, 16)
            for j in range(2 * ND):
                ada_load(sp, j, ada_ready)
            sp.dma_start(cos3, k_cos.rearrange("(t p) d -> p t d", p=P)).then_inc(rope_consts, 16)
            sp.dma_start(sin3, k_sin.rearrange("(t p) d -> p t d", p=P)).then_inc(rope_consts, 16)
            sp.dma_start(g_qk[:, 0, :], bc_row(q_norm_g)).then_inc(rope_consts, 16)
            sp.dma_start(g_qk[:, 1, :], bc_row(k_norm_g)).then_inc(rope_consts, 16)
            sp.dma_start(dft_tok, k_dft_tok.rearrange("(t p) n -> p t n", p=P)).then_inc(dft_ready, 16)
            sp.dma_start(dft_ch, k_dft_ch.rearrange("(t p) n -> p t n", p=P)).then_inc(dft_ready, 16)
            for r, (src, k0, n) in enumerate(halves):
                s = r % MIX_SLOTS
                if r >= MIX_SLOTS:
                    sp.wait_ge(*half_used(r - MIX_SLOTS))
                sp.dma_start(ring3[s], src[:, k0:k0 + HK, n * CW:(n + 1) * CW]).then_inc(slot_ready[s], 16)

            def expert_load(e, i):
                for s in range(RING):
                    if i is None:
                        if s < MIX_SLOTS:
                            sp.wait_ge(*half_used(N_HALVES - MIX_SLOTS + s))
                        elif s == MIX_SLOTS:
                            sp.wait_ge(tr_done, M_H2)
                    elif s < 2:
                        sp.wait_ge(slot_free[s], i + frees(s, N_HALVES - 1))
                    elif s < MIX_SLOTS:
                        sp.wait_ge(gu_done, i)
                    else:
                        sp.wait_ge(down_done, 2 * i + s - MIX_SLOTS - 1)
                    if s < MIX_SLOTS:
                        src = (w_exp_gate, w_exp_up)[s % 2]
                        half = s // 2
                        sp.dma_start(ring3[s], src[e, half * HK * P:(half + 1) * HK * P, :]
                                     .rearrange("(k p) n -> p k n", p=P)).then_inc(slot_ready[s], 16)
                    else:
                        n = s - MIX_SLOTS
                        for g in range(2):
                            sp.dma_start(ring3[s][:, g * KFF:(g + 1) * KFF, :],
                                         w_exp_down[e, :, (2 * g + n) * CW:(2 * g + n + 1) * CW]
                                         .rearrange("(k p) n -> p k n", p=P)).then_inc(slot_ready[s], 16)

            expert_load(0, None)
            with sp.Fori(1, NE) as i:
                expert_load(i, i)
            sp.wait_ge(meta_ready, 1)
            n_over = sp.value_load(meta[0:1, 1:2], min_val=0, max_val=NOVER - 1)
            with sp.If(n_over > 0):
                with sp.Fori(0, n_over) as j:
                    e = sp.value_load(meta[0:1, bass.ds(j + 2, 1)], min_val=0, max_val=NE - 1)
                    expert_load(e, j + NE)
            sp.wait_ge(out_stored, 32)

        @block.gpsimd
        def _(pool):
            pool.memset(ones[:, :], 1.0).then_inc(ones_ready, 1)
            pool.memset(eps, EPS).then_inc(eps_ready, 1)
            for j in range(2 * ND, N_ADA):
                ada_load(pool, j, ada_late)
            pool.wait_ge(ada_sum_ready, N_ADA)
            for s in range(2):
                pool.wait_ge(row_stored[s], 16 * (N_ADA - 2 * ND) // 2)

            def mod_row(m):
                return mods_dram[m * ND:(m + 1) * ND, :].rearrange("(a j) n -> a (j n)", a=1)
            pool.dma_start(rows[0], bc_row(mod_row(2))).then_inc(rows_a, 16)
            pool.dma_start(rows[1], bc_row(g_post_mix)).then_inc(rows_a, 16)
            pool.dma_start(rows[2], bc_row(mod_row(4))).then_inc(rows_a, 16)
            pool.dma_start(rows[3], bc_row(g_pre_ffn)).then_inc(rows_a, 16)
            pool.wait_ge(gg1_ready, 1)
            pool.dma_start(rows[1], bc_row(mod_row(3))).then_inc(rows_b, 16)
            pool.wait_ge(mixed_ready, 2 * ND)
            pool.dma_start(wr[:, :, 0:NG], w_group_router.rearrange("(k p) n -> p k n", p=P)).then_inc(route_consts, 16)
            pool.dma_start(wr[:, :, NG:NR], w_expert_router.rearrange("(k p) n -> p k n", p=P)).then_inc(route_consts, 16)
            pool.dma_start(rb[:, 0:NG], row_of(b_group_router)).then_inc(route_consts, 16)
            pool.dma_start(rb[:, NG:NR], row_of(b_expert_router)).then_inc(route_consts, 16)
            pool.dma_start(upper, k_upper).then_inc(route_consts, 16)
            pool.dma_start(krow, bc_row(k_row)).then_inc(route_consts, 16)
            pool.wait_ge(h2_ready, 2)
            pool.dma_start(rows[2], bc_row(mod_row(5))).then_inc(rows_c, 16)
            pool.dma_start(rows[3], bc_row(g_post_ffn)).then_inc(rows_c, 16)

        acc_out = y1
        h2 = h_tok
        o = [0]

        def take(n):
            o[0] += n
            return r_kvf[:, o[0] - n:o[0]]
        xg = take(KD * SLOTS).rearrange("p (k s) -> p k s", k=KD)
        y_sb = take(2 * CW).rearrange("p (n c) -> p n c", n=2)
        gu = take(FF)
        act_sb = take(KFF * SLOTS).rearrange("p (f s) -> p f s", f=KFF)
        silu_sb = take(KFF * SLOTS).rearrange("p (f s) -> p f s", f=KFF)
        s_mat = take(SEQ)
        p_mat = take(TT * SLOTS).rearrange("p (t s) -> p t s", t=TT)
        pw = take(TT * 2 * SLOTS).rearrange("p (t g s) -> p t g s", t=TT, g=2)
        o[0] = 0

        def tmp(n, *dims):
            o[0] += n
            return ada_w[:, o[0] - n:o[0]]
        lg = tmp(TT * NR).rearrange("p (t n) -> p t n", t=TT)
        gm = tmp(TT)
        ga = tmp(TT * NG).rearrange("p (t n) -> p t n", t=TT)
        oh_g = tmp(TT * NG).rearrange("p (t n) -> p t n", t=TT)
        gsh = tmp(TT * NG).rearrange("p (t n) -> p t n", t=TT)
        gex = tmp(TT * NG).rearrange("p (t n) -> p t n", t=TT)
        gmin = tmp(TT)
        elm = tmp(TT * NE).rearrange("p (t n) -> p t n", t=TT)
        e_tmp = tmp(TT * NE).rearrange("p (t n) -> p t n", t=TT)
        oh1 = tmp(TT * NE).rearrange("p (t n) -> p t n", t=TT)
        oh2 = tmp(TT * NE).rearrange("p (t n) -> p t n", t=TT)
        member = tmp(TT * NE).rearrange("p (t n) -> p t n", t=TT)
        comb = tmp(TT * NE).rearrange("p (t n) -> p t n", t=TT)
        rank_m = tmp(TT * NE).rearrange("p (t n) -> p t n", t=TT)
        m1, m2, i1, gw, de, w1, w2 = (tmp(TT) for _ in range(7))
        cnt = tmp(NE)
        flags = tmp(NCAND)
        flagsT = tmp(P)
        rank_c = tmp(TT * NCAND).rearrange("p (t n) -> p t n", t=TT)
        sel = tmp(NOVER * NCAND).rearrange("p (j n) -> p j n", j=NOVER)
        selx = tmp(NOVER * NCAND).rearrange("p (j n) -> p j n", j=NOVER)
        eblk = tmp(NOVER)
        nover = tmp(1)
        rank_b = tmp(TT * NBLK).rearrange("p (t n) -> p t n", t=TT)
        w_b = tmp(TT * NBLK).rearrange("p (t n) -> p t n", t=TT)
        assert o[0] <= 2 * D
        r0 = 0
        k_slot = krow[:, 0:SLOTS]
        k_g4 = krow[:, 64:68]
        k_e32 = krow[:, 68:100]
        k_j8 = krow[:, 100:108]
        k_ec = krow[:, 108:108 + NCAND]

        @block.tensor
        def _(pe):
            def gemm(g, r, lhsT, n_halves):
                pair = g % 2
                if g >= 2:
                    pe.wait_ge(mm_out[pair], 2 * (g // 2))
                for hh in range(n_halves):
                    s, u = (r + hh) % MIX_SLOTS, (r + hh) // MIX_SLOTS
                    pe.wait_ge(slot_ready[s], 16 * (u + 1))
                    for k in range(HK):
                        kk = hh * HK + k
                        for t in range(TT):
                            last = pe.matmul(bank[2 * pair + t][:, :], lhsT[:, kk, t * P:(t + 1) * P], ring3[s][:, k, :],
                                             start=(kk == 0), stop=(kk == n_halves * HK - 1))
                    if hh < n_halves - 1:
                        last.then_inc(slot_free[s], 1)
                last.then_inc(mm_done, 1)

            def transposes(m, src, ready, value):
                pe.wait_ge(ready, value)
                if m >= 2:
                    pe.wait_ge(tr_out, m - 1)
                for b in range(4):
                    last = pe.transpose(bank[6 + m % 2][:, b * P:(b + 1) * P], src[:, b * P:(b + 1) * P], ident[:, :])
                last.then_inc(tr_done, 1)

            def reduce_row(j):
                pe.wait_ge(ada_sum_ready, j + 1)
                if j < 2 * ND + 2:
                    pe.wait_ge(h_ready, 2 * ND)
                else:
                    pe.wait_ge(ada_row_out, j - 2 * ND - 1)
                b = bank[4 + j % 2]
                cc = ada_col(j) // CW
                pe.matmul(b[0:1, :], ones[:, 0:1], accs[j % 2], start=True, stop=False)
                pe.matmul(b[0:1, :], ident[0:N_ADA, cc:cc + 1], b_all[0:N_ADA, :], start=False, stop=True)\
                  .then_inc(ada_reduced, 1)

            pe.wait_ge(ones_ready, 1)
            pe.wait_ge(mod_consts, 48)
            for n in range(ND):
                for j in (2 * n, 2 * n + 1):
                    pe.wait_ge(ada_sum_ready, j + 1)
                    if n:
                        pe.wait_ge(h_ready, 2 * n)
                    b = bank[4 + j % 2]
                    cc = ada_col(j) // CW
                    pe.matmul(b[:, :], ones[:, :], accs[j % 2], start=True, stop=False)
                    pe.matmul(b[:, :], ident[0:N_ADA, cc:cc + 1].to_broadcast([N_ADA, P]), b_all[0:N_ADA, :],
                              start=False, stop=True).then_inc(ada_reduced, 1)
                for t in range(TT):
                    transposes(M_H + 2 * n + t, h_tok[:, t, n * CW:(n + 1) * CW], h_ready, 2 * n + t + 1)
            pe.wait_ge(tr_out, M_Q)
            r = 0
            for g in range(8):
                gemm(g, r, hT, 2)
                r += 2
                reduce_row(2 * ND + g)
                if 1 <= g <= Q_CHUNKS + 1:
                    for t in range(TT):
                        transposes(M_Q + 2 * (g - 1) + t, qr[:, t, :], rope_done, 2 * (g - 1) + t + 1)

            pe.wait_ge(tr_out, M_MIX)
            for pair in range(2):
                pe.wait_ge(mm_out[pair], 8)

            def scores(h):
                if h >= 2:
                    pe.wait_ge(exp_done, 2 * (h - 1))
                for t in range(TT):
                    last = pe.matmul(bank[h % 2][:, t * SEQ:(t + 1) * SEQ], qT[:, h, t * P:(t + 1) * P], kT[:, h // 4, :],
                                     start=True, stop=True)
                last.then_inc(score_done, 1)

            def probs_t(h):
                pe.wait_ge(probs_ready, h + 1)
                if h >= 2:
                    pe.wait_ge(pt_ready, h - 1)
                for s in range(TT):
                    for t in range(TT):
                        last = pe.transpose(bank[2 + h % 2][:, s * SEQ + t * P:s * SEQ + (t + 1) * P],
                                            probs[h % 2][:, t, s * P:(s + 1) * P], ident[:, :])
                last.then_inc(pt_done, 1)

            def pv(h):
                pe.wait_ge(pt_ready, h + 1)
                if h >= 2:
                    pe.wait_ge(attn_ready, h - 1)
                for s in range(TT):
                    last = pe.matmul(bank[6 + h % 2][:, 0:SEQ], v_sb[:, s, (h // 4) * HD:(h // 4 + 1) * HD], pT[h % 2][:, s, :],
                                     start=(s == 0), stop=(s == TT - 1))
                last.then_inc(pv_done, 1)

            scores(0)
            for h in range(NH):
                if h + 1 < NH:
                    scores(h + 1)
                probs_t(h)
                if h >= 1:
                    pv(h - 1)
            pv(NH - 1)

            pe.wait_ge(dft_ready, 32)
            pe.wait_ge(exp_done, 2 * NH)
            pe.wait_ge(pt_ready, NH)
            for i in range(KF):
                if i >= 4:
                    pe.wait_ge(ab_ready[i % 2], (i - 4) // 2 + 1)
                for t in range(TT):
                    last = pe.matmul(bank[i % 4][:, :], f_sb[:, t, i * P:(i + 1) * P], dft_tok[:, t, :],
                                     start=(t == 0), stop=(t == TT - 1))
                last.then_inc(f1_done, 1)
            for i in range(KF):
                grp, cc = i // 2, i % 2
                for a in range(2):
                    pe.wait_ge(ab_ready[a], i // 2 + 1)
                if i < 4:
                    pe.wait_ge(ab_ready[i % 2], (i + 4) // 2 + 1)
                else:
                    pe.wait_ge(fT_ready[i % 2], (i - 4) // 2 + 1)
                for kc in range(2):
                    for part in range(2):
                        last = pe.matmul(bank[i % 4][:, 0:SEQ], dft_ch[:, kc, part * FG + cc * P:part * FG + (cc + 1) * P],
                                         ab[:, 2 * grp + kc, part * SEQ:(part + 1) * SEQ],
                                         start=(kc == 0 and part == 0), stop=(kc == 1 and part == 1))
                last.then_inc(f2_done, 1)
            pe.wait_ge(attn_ready, NH)
            for a in range(2):
                pe.wait_ge(fT_ready[a], KF // 2)

            for n in range(ND):
                gemm(G_S4 + 2 * n, r, hT, 2)
                gemm(G_S4 + 2 * n + 1, r + 2, qT, 2)
                r += 4
                reduce_row(4 * ND + n)
            for n in range(ND):
                gemm(G_S5 + 2 * n, r, hT, 2)
                gemm(G_S5 + 2 * n + 1, r + 2, fT, 1)
                r += 3
                reduce_row(5 * ND + n)
                if n:
                    for t in range(TT):
                        transposes(M_MIX + 2 * (n - 1) + t, mixed[:, t, (n - 1) * CW:n * CW], mixed_ready, 2 * (n - 1) + t + 1)
            for t in range(TT):
                transposes(M_MIX + 2 * (ND - 1) + t, mixed[:, t, (ND - 1) * CW:D], mixed_ready, 2 * (ND - 1) + t + 1)
            pe.wait_ge(tr_out, M_H2)
            for n in range(ND):
                gemm(G_S6 + n, r, mT, 2)
                r += 2
            assert r == N_HALVES

            for t in range(TT):
                for n in range(ND):
                    transposes(M_H2 + t * ND + n, h2[:, t, n * CW:(n + 1) * CW], h2_ready, t + 1)
            pe.wait_ge(tr_out, M_H2 + 2 * ND)
            pe.wait_ge(ada_row_out, N_ADA - 2 * ND)
            pe.wait_ge(route_consts, 96)
            for t in range(TT):
                for k in range(KD):
                    pe.matmul(bank[4][:, t * 64:t * 64 + NR], h2T[:, k, t * P:(t + 1) * P], wr[:, k, :], start=(k == 0), stop=False)
                last = pe.matmul(bank[4][:, t * 64:t * 64 + NR], ones[0:1, :], rb, start=False, stop=True)
            last.then_inc(logits_done, 1)
            pe.wait_ge(member_ready, 1)
            pe.matmul(bank[5][:, 0:NE], upper, member[:, 0, :], start=True, stop=True)
            pe.matmul(bank[5][:, NE:2 * NE], ones[:, :], member[:, 0, :], start=True, stop=False)
            pe.matmul(bank[5][:, NE:2 * NE], upper, member[:, 1, :], start=False, stop=True)
            pe.matmul(bank[5][:, 2 * NE:3 * NE], ones[:, :], member[:, 0, :], start=True, stop=False)
            pe.matmul(bank[5][:, 2 * NE:3 * NE], ones[:, :], member[:, 1, :], start=False, stop=True).then_inc(ranks_done, 1)
            pe.wait_ge(flags_ready, 1)
            pe.transpose(bank[4][0:NCAND, 128:256], flags, ident[:, :]).then_inc(flagsT_done, 1)
            pe.wait_ge(flagsT_ready, 1)
            pe.matmul(bank[4][:, 256:256 + NCAND], flagsT[0:NCAND, :], upper[0:NCAND, 0:NCAND], start=True, stop=True)\
              .then_inc(prefix_done, 1)

            def gather():
                for k in range(KD):
                    for t in range(TT):
                        last = pe.matmul(bank[2 + k // HK][:, (k % HK) * SLOTS:(k % HK + 1) * SLOTS], h2[:, t, k * P:(k + 1) * P],
                                         p_mat[:, t, :], start=(t == 0), stop=(t == TT - 1))
                last.then_inc(gather_done, 1)

            pe.wait_ge(meta_ready, 1)
            n_blk = pe.value_load(meta[0:1, 0:1], min_val=NE, max_val=NBLK - 1)
            pe.wait_ge(p_ready, 1)
            gather()
            with pe.Fori(0, n_blk) as i:
                pe.wait_ge(xg_ready, i + 1)
                for half in range(2):
                    for a in range(2):
                        pe.wait_ge(slot_ready[2 * half + a], 16 * (i + 1 + MIX_USES))
                    for k in range(HK):
                        kk = half * HK + k
                        for a in range(2):
                            last = pe.matmul(bank[0][a * SLOTS:(a + 1) * SLOTS, :], xg[:, kk, :], ring3[2 * half + a][:, k, :],
                                             start=(kk == 0), stop=(kk == KD - 1), skip_group_check=True)
                            if kk == HK - 1:
                                last.then_inc(slot_free[a], 1)
                last.then_inc(gu_done, 1)
                pe.wait_ge(p_ready, i + 2)
                gather()
                pe.wait_ge(pw_ready, i + 1)
                pe.wait_ge(scat_out[0], 2 * i + 1)
                for t in range(TT):
                    last = pe.transpose(bank[4][:, t * P:(t + 1) * P], pw[:, t, :, :].rearrange("p g s -> p (g s)"), ident[:, :])
                last.then_inc(st_done, 1)
                pe.wait_ge(gu_ready, i + 1)
                for f in range(KFF):
                    last = pe.transpose(bank[1][:, f * P:(f + 1) * P], gu[:, f * P:(f + 1) * P], ident[:, :])
                last.then_inc(gut_done, 1)
                pe.wait_ge(act_ready, i + 1)
                pe.wait_ge(xg_ready, i + 2)
                for n in range(2):
                    pe.wait_ge(slot_ready[MIX_SLOTS + n], 32 * (i + 1))
                    for f in range(KFF):
                        for g in range(2):
                            last = pe.matmul(bank[2 + n][g * SLOTS:(g + 1) * SLOTS, :], act_sb[:, f, :],
                                             ring3[MIX_SLOTS + n][:, g * KFF + f, :], start=(f == 0), stop=(f == KFF - 1),
                                             skip_group_check=True)
                    last.then_inc(down_done, 1)
                pe.wait_ge(s_ready, i + 1)
                for n in range(2):
                    pe.wait_ge(y_ready, 2 * i + n + 1)
                    for t in range(TT):
                        if n:
                            pe.wait_ge(scat_out[t], 2 * i + 2)
                        elif t:
                            pe.wait_ge(scat_out[1], 2 * i + 1)
                        for g in range(2):
                            last = pe.matmul(bank[4 + 2 * t + g][:, :], s_mat[g * SLOTS:(g + 1) * SLOTS, t * P:(t + 1) * P],
                                             y_sb[g * SLOTS:(g + 1) * SLOTS, n, :], start=True, stop=True)
                        last.then_inc(scat_done, 1)

        @block.scalar
        def _(act):
            act.wait_ge(c_ready, 16)
            act.activation(s_col, cs, ACT.Silu).then_inc(silu_c_ready, 1)
            act.wait_ge(x_ready, 16)
            for t in range(TT):
                act.activation(h_tok[:, t, :], x3[:, t, :], ACT.Square, accum_out=ss[:, t:t + 1]).then_inc(sumsq_ready, 1)

            def root(dst, src, count, signal):
                act.activation(dst, src, ACT.Sqrt, bias=eps, scale=1.0 / count).then_inc(signal, 1)

            act.wait_ge(eps_ready, 1)
            act.wait_ge(sumsq_ready, TT)
            root(rstd[:, 0:TT], ss[:, 0:TT], D, root_x)

            def tr_copy(m, dst):
                act.wait_ge(tr_done, m + 1)
                act.activation(dst, bank[6 + m % 2][:, :].rearrange("p (b s) -> p b s", b=4), ACT.Copy).then_inc(tr_out, 1)

            def store_row(j):
                act.wait_ge(ada_reduced, j + 1)
                act.activation(accs[j % 2][0:1, :], bank[4 + j % 2][0:1, :], ACT.Copy).then_inc(ada_row_out, 1)
                act.wait_ge(ada_row_out, j - 2 * ND + 1)
                act.dma_start(mods_dram[j:j + 1, :], accs[j % 2][0:1, :]).then_inc(row_stored[j % 2], 16)

            for n in range(ND):
                for t in range(TT):
                    tr_copy(M_H + 2 * n + t, hT[:, 4 * n:4 * n + 4, t * P:(t + 1) * P])
            for g in range(8):
                act.wait_ge(mm_done, g + 1)
                for t in range(TT):
                    src = bank[2 * (g % 2) + t][:, :]
                    if g <= Q_CHUNKS:
                        if g:
                            act.wait_ge(rope_done, 2 * (g - 1) + t + 1)
                        for hh in range(HPC):
                            act.activation(rope_junk[:, hh * HD:(hh + 1) * HD], src[:, hh * HD:(hh + 1) * HD], ACT.Square,
                                           accum_out=rms_q[:, t * HPC + hh:t * HPC + hh + 1])
                        dst = raw[:, t, :]
                    else:
                        dst = v_sb[:, t, :] if g == Q_CHUNKS + 1 else f_sb[:, t, (g - Q_CHUNKS - 2) * CW:(g - Q_CHUNKS - 1) * CW]
                    act.activation(dst, src, ACT.Copy).then_inc(mm_out[g % 2], 1)
                    if g <= Q_CHUNKS:
                        act.wait_ge(mm_out[g % 2], 2 * (g // 2) + t + 1)
                        rq = rms_q[:, t * HPC:(t + 1) * HPC]
                        root(rq, rq, HD, root_qk)
                store_row(2 * ND + g)
                if 1 <= g <= Q_CHUNKS + 1:
                    for t in range(TT):
                        dst = qT[:, 4 * (g - 1):4 * g, t * P:(t + 1) * P] if g <= Q_CHUNKS else kT[:, :, t * P:(t + 1) * P]
                        tr_copy(M_Q + 2 * (g - 1) + t, dst)

            def attn_copy(h):
                act.wait_ge(pv_done, h + 1)
                act.activation(qT[:, h, :], bank[6 + h % 2][:, 0:SEQ], ACT.Copy).then_inc(attn_ready, 1)

            for h in range(NH):
                act.wait_ge(nmx_ready, h + 1)
                if h >= 2:
                    act.wait_ge(pt_done, h - 1)
                for t in range(TT):
                    b = 2 * (h % 2) + t
                    act.activation(probs[h % 2][:, t, :], bank[h % 2][:, t * SEQ:(t + 1) * SEQ], ACT.Exp,
                                   bias=nmx[:, b:b + 1], scale=SCALE, accum_out=rs[:, b:b + 1]).then_inc(exp_done, 1)
                if h >= 2:
                    attn_copy(h - 2)
            attn_copy(NH - 2)
            attn_copy(NH - 1)
            for i in range(0, KF, 2):
                act.wait_ge(f1_done, i + 1)
                act.activation(ab[:, i, :], bank[i % 4][:, :], ACT.Copy).then_inc(ab_ready[0], 1)
            for i in range(0, KF, 2):
                act.wait_ge(f2_done, i + 1)
                act.activation(fT[:, i, :], bank[i % 4][:, 0:SEQ], ACT.Copy).then_inc(fT_ready[0], 1)
            for st in range(2):
                for n in range(ND):
                    g = G_S4 + 2 * ND * st + 2 * n
                    act.wait_ge(mm_done, g + 1)
                    for t in range(TT):
                        if st and n:
                            act.wait_ge(mixed_ready, 2 * (n - 1) + t + 1)
                        elif g > G_S4:
                            act.wait_ge(mm_out[1], 2 * ((g - 1) // 2) + t + 1)
                        act.activation(gate3[:, t, :], bank[t][:, :], ACT.Sigmoid).then_inc(mm_out[0], 1)
                    store_row(4 * ND + ND * st + n)
                    if st and n:
                        for t in range(TT):
                            tr_copy(M_MIX + 2 * (n - 1) + t, mT[:, 4 * (n - 1):4 * n, t * P:(t + 1) * P])
            for t in range(TT):
                tr_copy(M_MIX + 2 * (ND - 1) + t, mT[:, 4 * (ND - 1):4 * ND, t * P:(t + 1) * P])
            for n in range(ND):
                act.wait_ge(mm_done, G_S6 + n + 1)
                for t in range(TT):
                    b = bank[2 * (n % 2) + t][:, :]
                    y = y1[:, t, n * CW:(n + 1) * CW]
                    act.activation(y, b, ACT.Copy).then_inc(mm_out[n % 2], 1)
                    act.wait_ge(mm_out[n % 2], 2 * ((G_S6 + n) // 2) + t + 1)
                    act.activation(bank[6 + t][:, :], y, ACT.Square, accum_out=ss[:, t * ND + n:t * ND + n + 1]).then_inc(y1_ready, 1)
            act.wait_ge(y1_ready, 2 * ND)
            for t in range(TT):
                act.activation(junk4[:, t * ND:(t + 1) * ND], ss[:, t * ND:(t + 1) * ND], ACT.Copy, accum_out=rs[:, t:t + 1]).then_inc(y1_sum, 1)
            act.wait_ge(y1_sum, TT)
            root(rstd[:, 0:TT], rs[:, 0:TT], D, root_y)
            for t in range(TT):
                act.wait_ge(x1_ready, t + 1)
                act.activation(y1[:, t, :], x3[:, t, :], ACT.Square, accum_out=rs[:, t:t + 1]).then_inc(x1_sumsq, 1)
                act.wait_ge(x1_sumsq, t + 1)
                root(rinv[:, t:t + 1], rs[:, t:t + 1], D, root_x1)
            for t in range(TT):
                for n in range(ND):
                    tr_copy(M_H2 + t * ND + n, h2T[:, 4 * n:4 * n + 4, t * P:(t + 1) * P])
            act.wait_ge(shifted_ready, 1)
            act.activation(gex, gsh, ACT.Exp).then_inc(route_exp, 1)
            act.wait_ge(shifted_ready, 2)
            act.activation(w2, de, ACT.Exp).then_inc(route_exp, 1)

            act.wait_ge(meta_ready, 1)
            n_blk = act.value_load(meta[0:1, 0:1], min_val=NE, max_val=NBLK - 1)

            def gather_copy(v):
                act.wait_ge(gather_done, v)
                act.activation(xg[:, 0:HK, :], bank[2][:, :].rearrange("p (k s) -> p k s", k=HK), ACT.Copy)
                act.activation(xg[:, HK:KD, :], bank[3][:, :].rearrange("p (k s) -> p k s", k=HK), ACT.Copy).then_inc(xg_ready, 1)

            gather_copy(1)
            with act.Fori(0, n_blk) as i:
                gather_copy(i + 2)
                act.wait_ge(st_done, i + 1)
                act.activation(s_mat, bank[4][:, 0:SEQ], ACT.Copy).then_inc(s_ready, 1)
                act.wait_ge(gut_done, i + 1)
                act.activation(silu_sb, bank[1][:, :].rearrange("p (f s) -> p f s", f=KFF)[:, :, 0:SLOTS], ACT.Silu)\
                   .then_inc(silu_ready, 1)
                for n in range(2):
                    act.wait_ge(down_done, 2 * i + n + 1)
                    act.activation(y_sb[:, n, :], bank[2 + n][:, :], ACT.Copy).then_inc(y_ready, 1)
            for t in range(TT):
                act.wait_ge(scat_out[t], 2 * n_blk + 1)
            for t in range(TT):
                act.activation(r_q[:, t * D:(t + 1) * D], acc_out[:, t, :], ACT.Square, accum_out=ss[:, t:t + 1]).then_inc(acc_sumsq, 1)
                act.wait_ge(acc_sumsq, t + 1)
                root(rstd[:, t:t + 1], ss[:, t:t + 1], D, root_out)
            for t in range(TT):
                act.wait_ge(out_ready, t + 1)
                act.dma_start(out_v[:, t, :], x3[:, t, :]).then_inc(out_stored, 16)
            act.wait_ge(out_stored, 32)

        @block.vector
        def _(dve):
            order = Order(dve, o_dve)

            def signal(ins, s, value):
                ins.then_inc(s, 1)
                dve.wait_ge(s, value)

            def ada_chunk(j):
                a = accs[j % 2]
                if j >= 2 * ND + 2:
                    dve.wait_ge(row_stored[j % 2], 16 * ((j - 2 * ND) // 2))
                elif j >= 2:
                    dve.wait_ge(ada_reduced, j - 1)
                for s in range(ADA_SLOTS):
                    dve.wait_ge(*((ada_ready[s], 16 * (j + 1)) if j < 2 * ND else (ada_late[s], 16 * (j + 1 - 2 * ND))))
                    for k in range(ADA_K):
                        kk = s * ADA_K + k
                        if kk == 0:
                            ins = dve.tensor_scalar(a, ada3[s][:, k, :], s_col[:, kk:kk + 1], None, ALU.mult)
                        else:
                            ins = dve.scalar_tensor_tensor(a, ada3[s][:, k, :], s_col[:, kk:kk + 1], a, ALU.mult, ALU.add)
                        if k < ADA_K - 1:
                            order(ins)
                        elif s < ADA_SLOTS - 1:
                            signal(ins, ada_free[s], j + 1)
                        else:
                            ins.then_inc(ada_sum_ready, 1)

            dve.wait_ge(root_x, 1)
            order(dve.reciprocal(rstd[:, 0:TT], rstd[:, 0:TT]))
            for t in range(TT):
                order(dve.tensor_scalar(h_tok[:, t, :], x3[:, t, :], rstd[:, t:t + 1], None, ALU.mult))
            dve.wait_ge(silu_c_ready, 1)
            dve.wait_ge(mod_consts, 48)
            for n in range(ND):
                ada_chunk(2 * n)
                ada_chunk(2 * n + 1)
                cols = slice(n * CW, (n + 1) * CW)
                dve.wait_ge(ada_reduced, 2 * n + 2)
                order(dve.scalar_tensor_tensor(a_row, bank[5][:, :], 1.0, g_pre[:, cols], ALU.add, ALU.mult))
                for t in range(TT):
                    order(dve.tensor_tensor(h_tok[:, t, cols], h_tok[:, t, cols], a_row, ALU.mult))
                    dve.tensor_tensor(h_tok[:, t, cols], h_tok[:, t, cols], bank[4][:, :], ALU.add).then_inc(h_ready, 1)

            dve.wait_ge(rope_consts, 64)
            for a in range(2):
                for t in range(TT):
                    order(dve.tensor_tensor(cosg[a][:, t, :], cos3[:, t, :], g_qk[:, a, :], ALU.mult))
                    sv = sin3[:, t, :].rearrange("p (a b c) -> p a b c", a=2, b=2)
                    gv = g_qk[:, a, :].rearrange("p (a b c) -> p a b c", a=2, b=2)
                    dv = sing[a][:, t, :].rearrange("p (a b c) -> p a b c", a=2, b=2)
                    for b in range(2):
                        order(dve.tensor_tensor(dv[:, :, b, :], sv[:, :, b, :], gv[:, :, 1 - b, :], ALU.mult))

            def rope(g, t):
                a = 0 if g < Q_CHUNKS else 1
                v = raw[:, t, :]
                v3 = v.rearrange("p (h d) -> p h d", h=HPC)
                dve.wait_ge(mm_out[g % 2], 2 * (g // 2) + t + 1)
                if g or t:
                    dve.wait_ge(rope_done, 2 * g + t)
                dve.wait_ge(root_qk, 2 * g + t + 1)
                rq = rms_q[:, t * HPC:(t + 1) * HPC]
                order(dve.reciprocal(rq, rq))
                order(dve.tensor_tensor(v3, v3, rq.unsqueeze(2).to_broadcast([P, HPC, HD]), ALU.mult))
                if g:
                    dve.wait_ge(tr_done, M_Q + 2 * (g - 1) + t + 1)
                q3 = qr[:, t, :].rearrange("p (h d) -> p h d", h=HPC)
                order(dve.tensor_tensor(q3, v3, cosg[a][:, t, :].unsqueeze(1).to_broadcast([P, HPC, HD]), ALU.mult))
                v5 = v.rearrange("p (h a b c) -> p h a b c", h=HPC, a=2, b=2)
                r5 = rope_tmp.rearrange("p (h a b c) -> p h a b c", h=HPC, a=2, b=2)
                s4 = sing[a][:, t, :].rearrange("p (a b c) -> p a b c", a=2, b=2)
                for b in range(2):
                    order(dve.tensor_tensor(r5[:, :, :, b, :], v5[:, :, :, 1 - b, :],
                                            s4[:, :, b, :].unsqueeze(1).to_broadcast([P, HPC, 2, HD // 4]), ALU.mult))
                dve.tensor_tensor(qr[:, t, :], qr[:, t, :], rope_tmp, ALU.add).then_inc(rope_done, 1)

            for g in range(8):
                ada_chunk(2 * ND + g)
                if g <= Q_CHUNKS:
                    for t in range(TT):
                        rope(g, t)

            def row_max(h):
                b = 2 * (h % 2)
                dve.wait_ge(score_done, h + 1)
                if h >= 2:
                    dve.wait_ge(exp_done, 2 * (h - 1))
                order(dve.tensor_reduce(mx[:, b:b + 2], bank[h % 2][:, :].rearrange("p (t s) -> p t s", t=TT), AX_X, ALU.max))
                dve.tensor_scalar(nmx[:, b:b + 2], mx[:, b:b + 2], -SCALE, None, ALU.mult).then_inc(nmx_ready, 1)

            def normalise(h):
                b = 2 * (h % 2)
                dve.wait_ge(exp_done, 2 * (h + 1))
                order(dve.reciprocal(rinv[:, b:b + 2], rs[:, b:b + 2]))
                for t in range(TT):
                    last = dve.tensor_scalar(probs[h % 2][:, t, :], probs[h % 2][:, t, :], rinv[:, b + t:b + t + 1], None, ALU.mult)
                last.then_inc(probs_ready, 1)

            def pt_copy(h):
                dve.wait_ge(pt_done, h + 1)
                if h >= 2:
                    dve.wait_ge(pv_done, h - 1)
                dve.tensor_copy(pT[h % 2], bank[2 + h % 2][:, :].rearrange("p (s q) -> p s q", s=TT)).then_inc(pt_ready, 1)

            dve.wait_ge(tr_done, M_MIX)
            row_max(0)
            for h in range(NH):
                if h + 1 < NH:
                    row_max(h + 1)
                normalise(h)
                if h >= 1:
                    pt_copy(h - 1)
            pt_copy(NH - 1)
            for i in range(1, KF, 2):
                dve.wait_ge(f1_done, i + 1)
                dve.tensor_copy(ab[:, i, :], bank[i % 4][:, :]).then_inc(ab_ready[1], 1)
            for i in range(1, KF, 2):
                dve.wait_ge(f2_done, i + 1)
                dve.tensor_copy(fT[:, i, :], bank[i % 4][:, 0:SEQ]).then_inc(fT_ready[1], 1)
            for st in range(2):
                for n in range(ND):
                    ada_chunk(4 * ND + ND * st + n)
                    g = G_S4 + 2 * ND * st + 2 * n
                    cols = slice(n * CW, (n + 1) * CW)
                    dve.wait_ge(mm_done, g + 2)
                    for t in range(TT):
                        count = 2 * (g // 2) + t + 1
                        dve.wait_ge(mm_out[0], count)
                        if st == 0:
                            dve.tensor_tensor(mixed[:, t, cols], gate3[:, t, :], bank[2 + t][:, :], ALU.mult).then_inc(mm_out[1], 1)
                        else:
                            signal(dve.tensor_tensor(gate3[:, t, :], gate3[:, t, :], bank[2 + t][:, :], ALU.mult), mm_out[1], count)
                            dve.tensor_tensor(mixed[:, t, cols], mixed[:, t, cols], gate3[:, t, :], ALU.add).then_inc(mixed_ready, 1)

            dve.wait_ge(rows_a, 64)
            signal(dve.tensor_tensor(rows[0], rows[0], rows[1], ALU.mult), gg1_ready, 1)
            order(dve.scalar_tensor_tensor(rows[2], rows[2], 1.0, rows[3], ALU.add, ALU.mult))
            dve.wait_ge(root_y, 1)
            order(dve.reciprocal(rstd[:, 0:TT], rstd[:, 0:TT]))
            for t in range(TT):
                order(dve.scalar_tensor_tensor(y1[:, t, :], y1[:, t, :], rstd[:, t:t + 1], rows[0], ALU.mult, ALU.mult))
                dve.tensor_tensor(x3[:, t, :], x3[:, t, :], y1[:, t, :], ALU.add).then_inc(x1_ready, 1)
            dve.wait_ge(rows_b, 16)
            dve.wait_ge(mm_done, G_S6 + ND)
            for t in range(TT):
                dve.wait_ge(root_x1, t + 1)
                order(dve.reciprocal(rinv[:, t:t + 1], rinv[:, t:t + 1]))
                order(dve.scalar_tensor_tensor(h2[:, t, :], x3[:, t, :], rinv[:, t:t + 1], rows[2], ALU.mult, ALU.mult))
                dve.tensor_tensor(h2[:, t, :], h2[:, t, :], rows[1], ALU.add).then_inc(h2_ready, 1)
            for t in range(TT):
                signal(dve.memset(acc_out[:, t, :], 0.0), scat_out[t], 1)

            dve.wait_ge(logits_done, 1)
            order(dve.tensor_copy(lg, bank[4][:, 0:128].rearrange("p (t n) -> p t n", t=TT)[:, :, 0:NR]))

            def bc(v, n):
                return v.unsqueeze(2).to_broadcast([P, TT, n])

            def kbc(v, n):
                return v.unsqueeze(1).to_broadcast([P, TT, n])

            def first_max(oh, vals, top, work, low, k_idx, n):
                order(dve.tensor_reduce(top, vals, AX_X, ALU.max))
                order(dve.tensor_tensor(work, vals, bc(top, n), ALU.is_equal))
                order(dve.tensor_tensor(work, work, kbc(k_idx, n), ALU.mult))
                order(dve.tensor_reduce(low, work, AX_X, ALU.min))
                order(dve.tensor_tensor(oh, kbc(k_idx, n), bc(low, n), ALU.is_equal))

            gl = lg[:, :, 0:NG]
            first_max(oh_g, gl, gm, ga, gmin, k_g4, NG)
            signal(dve.tensor_tensor(gsh, gl, bc(gm, NG), ALU.subtract), shifted_ready, 1)
            order(dve.tensor_scalar(ga, oh_g, -1.0, FAR, ALU.add, ALU.mult))
            for t in range(TT):
                order(dve.tensor_tensor(elm[:, t, :].rearrange("p (g e) -> p g e", g=NG),
                                        lg[:, t, NG:NR].rearrange("p (g e) -> p g e", g=NG),
                                        ga[:, t, :].unsqueeze(2).to_broadcast([P, NG, EG]), ALU.add))
            first_max(oh1, elm, m1, e_tmp, i1, k_e32, NE)
            order(dve.scalar_tensor_tensor(elm, oh1, -2 * FAR, elm, ALU.mult, ALU.add))
            first_max(oh2, elm, m2, e_tmp, i1, k_e32, NE)
            signal(dve.tensor_tensor(de, m2, m1, ALU.subtract), shifted_ready, 2)
            signal(dve.tensor_tensor(member, oh1, oh2, ALU.add), member_ready, 1)
            dve.wait_ge(route_exp, 2)
            order(dve.tensor_reduce(gw, gex, AX_X, ALU.add))
            order(dve.tensor_scalar(w1, w2, 1.0, None, ALU.add))
            order(dve.tensor_tensor(w1, w1, gw, ALU.mult))
            order(dve.reciprocal(w1, w1))
            order(dve.tensor_tensor(w2, w2, w1, ALU.mult))
            order(dve.tensor_tensor(comb, oh1, bc(w1, NE), ALU.mult))
            order(dve.tensor_tensor(e_tmp, oh2, bc(w2, NE), ALU.mult))
            order(dve.tensor_tensor(comb, comb, e_tmp, ALU.add))
            dve.wait_ge(ranks_done, 1)
            order(dve.scalar_tensor_tensor(rank_m, bank[5][:, 0:2 * NE].rearrange("p (t n) -> p t n", t=TT), 1.0, member,
                                           ALU.add, ALU.mult))
            order(dve.tensor_scalar(rank_m, rank_m, -1.0, None, ALU.add))
            for b in range(BMAX):
                order(dve.tensor_scalar(rank_c[:, :, b * NE:(b + 1) * NE], rank_m, -float(CAP * (b + 1)), None, ALU.add))
                last = dve.tensor_scalar(flags[:, b * NE:(b + 1) * NE], bank[5][:, 2 * NE:3 * NE], CAP * (b + 1) + 0.5, None, ALU.is_gt)
            signal(last, flags_ready, 1)
            dve.wait_ge(flagsT_done, 1)
            dve.tensor_copy(flagsT[0:NCAND, :], bank[4][0:NCAND, 128:256]).then_inc(flagsT_ready, 1)
            order(dve.tensor_copy(rank_b[:, :, 0:NE], rank_m))
            order(dve.tensor_copy(w_b[:, :, 0:NE], comb))
            order(dve.tensor_reduce(nover, flags, AX_X, ALU.add))
            dve.wait_ge(prefix_done, 1)
            order(dve.tensor_tensor(sel, bank[4][:, 256:256 + NCAND].unsqueeze(1).to_broadcast([P, NOVER, NCAND]),
                                    k_j8.unsqueeze(2).to_broadcast([P, NOVER, NCAND]), ALU.is_equal))
            order(dve.tensor_tensor(sel, sel, flags.unsqueeze(1).to_broadcast([P, NOVER, NCAND]), ALU.mult))
            for t in range(TT):
                order(dve.tensor_tensor(selx, sel, rank_c[:, t, :].unsqueeze(1).to_broadcast([P, NOVER, NCAND]), ALU.mult))
                order(dve.tensor_reduce(rank_b[:, t, NE:NBLK], selx, AX_X, ALU.add))
                for b in range(BMAX):
                    order(dve.tensor_tensor(selx[:, :, b * NE:(b + 1) * NE], sel[:, :, b * NE:(b + 1) * NE],
                                            comb[:, t, :].unsqueeze(1).to_broadcast([P, NOVER, NE]), ALU.mult))
                order(dve.tensor_reduce(w_b[:, t, NE:NBLK], selx, AX_X, ALU.add))
            order(dve.tensor_tensor(selx, sel, k_ec.unsqueeze(1).to_broadcast([P, NOVER, NCAND]), ALU.mult))
            order(dve.tensor_reduce(eblk, selx, AX_X, ALU.add))
            order(dve.tensor_scalar(meta[:, 0:1], nover, float(NE), None, ALU.add))
            order(dve.tensor_copy(meta[:, 1:2], nover))
            signal(dve.tensor_copy(meta[:, 2:2 + NOVER], eblk), meta_ready, 1)
            n_blk = dve.value_load(meta[0:1, 0:1], min_val=NE, max_val=NBLK - 1)
            dve.wait_ge(rows_c, 32)
            order(dve.tensor_tensor(rows[2], rows[2], rows[3], ALU.mult))

            def select(col):
                for t in range(TT):
                    last = dve.tensor_scalar(p_mat[:, t, :], k_slot, rank_b[:, t, col], None, ALU.is_equal)
                last.then_inc(p_ready, 1)

            dve.wait_ge(tr_out, M_H2 + 2 * ND)
            select(slice(0, 1))
            with dve.Fori(0, n_blk) as i:
                dve.wait_ge(p_ready, i + 1)
                for t in range(TT):
                    last = dve.tensor_scalar(pw[:, t, :, :], p_mat[:, t, :].unsqueeze(1).to_broadcast([P, 2, SLOTS]),
                                             w_b[:, t, bass.ds(i, 1)], None, ALU.mult)
                last.then_inc(pw_ready, 1)
                dve.wait_ge(gather_done, i + 1)
                dve.wait_ge(pw_ready, i + 1)
                select(bass.ds(i + 1, 1))
                dve.wait_ge(gu_done, i + 1)
                dve.tensor_copy(gu, bank[0][:, :]).then_inc(gu_ready, 1)
                dve.wait_ge(silu_ready, i + 1)
                dve.tensor_tensor(act_sb, silu_sb, bank[1][:, :].rearrange("p (f s) -> p f s", f=KFF)[:, :, SLOTS:2 * SLOTS],
                                  ALU.mult).then_inc(act_ready, 1)
                for n in range(2):
                    for t in range(TT):
                        dve.wait_ge(scat_done, 4 * i + 2 * n + t + 1)
                        for g in range(2):
                            cols = slice((2 * g + n) * CW, (2 * g + n + 1) * CW)
                            last = dve.tensor_tensor(acc_out[:, t, cols], acc_out[:, t, cols], bank[4 + 2 * t + g][:, :], ALU.add)
                        last.then_inc(scat_out[t], 1)
                for t in range(TT):
                    dve.wait_ge(scat_out[t], 2 * i + 3)
            for t in range(TT):
                dve.wait_ge(root_out, t + 1)
                order(dve.reciprocal(rstd[:, t:t + 1], rstd[:, t:t + 1]))
                order(dve.scalar_tensor_tensor(acc_out[:, t, :], acc_out[:, t, :], rstd[:, t:t + 1], rows[2], ALU.mult, ALU.mult))
                dve.tensor_tensor(x3[:, t, :], x3[:, t, :], acc_out[:, t, :], ALU.add).then_inc(out_ready, 1)


_INS = ["x", "c", "w_ada", "b_ada", "g_pre_mix", "g_post_mix", "w_in", "q_norm_g", "k_norm_g", "w_attn_out", "w_fourier_out",
        "w_mix_out", "g_pre_ffn", "g_post_ffn", "w_group_router", "b_group_router", "w_expert_router", "b_expert_router",
        "w_exp_gate", "w_exp_up", "w_exp_down"]


def shape_constants():
    import numpy as np
    grid_w, theta = 64, 10000.0
    pos = np.arange(SEQ)
    n_freq = HD // 4
    inv = theta ** (-np.arange(n_freq) / n_freq)
    row = (pos // grid_w)[:, None] * inv
    col = (pos % grid_w)[:, None] * inv
    ang = np.concatenate([row, row, col, col], axis=-1)
    sign = np.tile(np.repeat([-1.0, 1.0], n_freq), 2)
    w = 2 * np.pi * (np.outer(np.arange(SEQ), np.arange(SEQ)) % SEQ) / SEQ
    row_k = np.zeros(108 + NCAND)
    row_k[0:SLOTS] = np.where(np.arange(SLOTS) < CAP, np.arange(SLOTS), 1e6)
    row_k[64:68] = np.arange(NG) - NG
    row_k[68:100] = np.arange(NE) - NE
    row_k[100:108] = np.arange(NOVER)
    row_k[108:] = np.tile(np.arange(NE), BMAX)
    tables = {
        "k_cos": np.cos(ang), "k_sin": np.sin(ang) * sign,
        "k_dft_tok": np.concatenate([np.cos(w), np.sin(w)], axis=1) / 16,
        "k_dft_ch": np.concatenate([np.cos(w), -np.sin(w)], axis=1) / 16,
        "k_ident": np.eye(P), "k_upper": np.triu(np.ones((P, P)), 1), "k_row": row_k,
    }
    return {k: np.ascontiguousarray(v.astype(np.float32)) for k, v in tables.items()}


def kernel(**inputs):
    import numpy as np
    import concourse.bacc as bacc
    from concourse.bass_utils import run_bass_kernel_spmd

    nc = bacc.Bacc("TRN2", target_bir_lowering=False, num_devices=1)
    arrays, args = {}, []
    for name, a in [(n, inputs[n]) for n in _INS] + list(shape_constants().items()):
        a = np.ascontiguousarray(a)
        arrays[f"in_{name}"] = a
        args.append(nc.dram_tensor(f"in_{name}", a.shape, mybir.dt.from_np(a.dtype), kind="ExternalInput").ap())
    args.append(nc.dram_tensor("out_x", (1, SEQ, D), F32, kind="ExternalOutput").ap())
    build(nc, *args)
    r = run_bass_kernel_spmd(nc, [arrays], core_ids=[0])
    return r.results[0]["out_x"]
```

```python
from contextlib import ExitStack

import concourse.bass as bass
from concourse import mybir

ALU = mybir.AluOpType
ACT = mybir.ActivationFunctionType
F32 = mybir.dt.float32
I32 = mybir.dt.int32
AX_X = mybir.AxisListType.X

P = 128
D = 2048
SEQ = 256
TT = SEQ // P
KD = D // P
CW = 512
ND = D // CW
HD = 128
NH = 16
NKV = 4
HPC = CW // HD
FD = 1024
FG = 256
KF = FD // P
Q_CHUNKS = NH * HD // CW
NE = 32
NG = 4
EG = NE // NG
FF = 512
KFF = FF // P
NR = NG + NE
SLOTS = 64
CAP = 64
BMAX = (SEQ - 1) // CAP
NCAND = BMAX * NE
NOVER = 8
NBLK = NE + NOVER
EPS = 1e-6
SCALE = float(HD) ** -0.5
FAR = 1e37
MIX_SLOTS = 4
RING = 6
HK = 8
ADA_SLOTS = 4
ADA_K = KD // ADA_SLOTS
N_ADA = 6 * ND


class Order:

    def __init__(self, eng, sem, base=0):
        self.eng, self.sem, self.base, self.n = eng, sem, base, 0

    def __call__(self, ins):
        ins.then_inc(self.sem, 1)
        self.n += 1
        self.eng.wait_ge(self.sem, self.base + self.n)


def build(nc, x, c, w_ada, b_ada, g_pre_mix, g_post_mix, w_in, q_norm_g, k_norm_g, w_attn_out, w_fourier_out,
          w_mix_out, g_pre_ffn, g_post_ffn, w_group_router, b_group_router, w_expert_router, b_expert_router,
          w_exp_gate, w_exp_up, w_exp_down, k_cos, k_sin, k_dft_tok, k_dft_ch, k_ident, k_upper, k_row, out):
    mods_dram = nc.dram_tensor("mods_scratch", (N_ADA, CW), F32, kind="Internal").ap()
    with ExitStack() as ctx:
        def sb(name, n, dt=F32):
            return ctx.enter_context(nc.sbuf_tensor(name, [P, n], dt))

        def sem(name):
            return ctx.enter_context(nc.semaphore(name))

        ring = [sb(f"ring{s}", HK * CW) for s in range(RING)]
        ada_w = sb("ada_w", ADA_SLOTS * ADA_K * CW)
        x_sb = sb("x_sb", TT * D)
        r_h = sb("r_h", KD * SEQ)
        r_q = sb("r_q", KD * SEQ)
        r_kvf = sb("r_kvf", KD * SEQ)
        gate = sb("gate", TT * CW)
        acc = sb("acc", 2 * CW)
        b_all = sb("b_all", CW)
        ident = sb("ident", P)
        ones = sb("ones", SEQ)
        ones_row = ones[0:1, :]
        cos_t = sb("cos_t", TT * HD)
        sin_t = sb("sin_t", TT * HD)
        small = sb("small", 160)
        meta = sb("meta", 16, I32)
        bank = [ctx.enter_context(nc.psum_tensor(f"bank{b}", [P, CW], F32)) for b in range(8)]

        x3 = x_sb[:, :].rearrange("p (t d) -> p t d", t=TT)
        hT = r_h[:, :].rearrange("p (k s) -> p k s", k=KD)
        y1 = r_h[:, :].rearrange("p (t d) -> p t d", t=TT)
        h_tok = r_q[:, :].rearrange("p (t d) -> p t d", t=TT)
        qT = r_q[:, :].rearrange("p (h s) -> p h s", h=NH)
        kT = r_kvf[:, 0:NKV * SEQ].rearrange("p (h s) -> p h s", h=NKV)
        v_sb = r_kvf[:, 1024:2048].rearrange("p (t d) -> p t d", t=TT)
        f_sb = r_kvf[:, 2048:4096].rearrange("p (t d) -> p t d", t=TT)
        fT = r_kvf[:, 2048:4096].rearrange("p (k s) -> p k s", k=KF)
        g_pre = r_kvf[:, 0:D]
        h2T = r_kvf[:, :].rearrange("p (k s) -> p k s", k=KD)
        gate3 = gate[:, :].rearrange("p (t d) -> p t d", t=TT)
        a_row = gate[:, 0:CW]
        accs = [acc[:, j * CW:(j + 1) * CW] for j in range(2)]
        cos3 = cos_t[:, :].rearrange("p (t d) -> p t d", t=TT)
        sin3 = sin_t[:, :].rearrange("p (t d) -> p t d", t=TT)
        ada3 = [ada_w[:, s * ADA_K * CW:(s + 1) * ADA_K * CW].rearrange("p (k n) -> p k n", k=ADA_K)
                for s in range(ADA_SLOTS)]
        rows = [ada_w[:, s * D:(s + 1) * D] for s in range(4)]
        ring3 = [r[:, :].rearrange("p (k n) -> p k n", k=HK) for r in ring]
        raw = ring[4][:, 0:1024].rearrange("p (t n) -> p t n", t=TT)
        qr = ring[4][:, 1024:2048].rearrange("p (t n) -> p t n", t=TT)
        rope_tmp = ring[4][:, 2048:2560]
        rope_junk = ring[4][:, 2560:2560 + CW]
        ab = ring[4][:, :].rearrange("p (i n) -> p i n", i=KF)
        dft_tok = ring[5][:, 0:1024].rearrange("p (t n) -> p t n", t=TT)
        dft_ch = ring[5][:, 1024:2048].rearrange("p (t n) -> p t n", t=TT)
        cosg = [ring[5][:, 2048 + 256 * a:2304 + 256 * a].rearrange("p (t n) -> p t n", t=TT) for a in range(2)]
        sing = [ring[5][:, 2560 + 256 * a:2816 + 256 * a].rearrange("p (t n) -> p t n", t=TT) for a in range(2)]
        g_qk = ring[5][:, 3072:3072 + 2 * HD].rearrange("p (a n) -> p a n", a=2)
        probs = [ring[5][:, 2048 + 512 * b:2560 + 512 * b].rearrange("p (t s) -> p t s", t=TT) for b in range(2)]
        pT = [ring[5][:, 3072 + 512 * b:3584 + 512 * b].rearrange("p (s q) -> p s q", s=TT) for b in range(2)]
        ga_sb = ring[4][:, :].rearrange("p (t d) -> p t d", t=TT)
        mixed = ring[5][:, :].rearrange("p (t d) -> p t d", t=TT)
        mT = qT
        wr = gate[:, 0:KD * NR].rearrange("p (k n) -> p k n", k=KD)
        upper = gate[:, 576:704]
        krow = gate[:, 704:704 + k_row.shape[0]]

        cs = small[:, 0:KD]
        s_col = small[:, 16:32]
        ss = small[:, 32:40]
        rstd = small[:, 40:48]
        mx = small[:, 48:52]
        nmx = small[:, 52:56]
        rs = small[:, 56:60]
        rinv = small[:, 60:64]
        rms_q = small[:, 64:64 + TT * HPC]
        eps = small[:, 72:73]
        junk4 = small[:, 74:74 + TT * ND]
        rb = small[0:1, 96:96 + NR]

        w_ada_v = w_ada.rearrange("(k p) n -> p k n", p=P)
        w_in_v = w_in.rearrange("(k p) n -> p k n", p=P)
        ao_v = w_attn_out.rearrange("(k p) n -> p k n", p=P)
        fo_v = w_fourier_out.rearrange("(k p) n -> p k n", p=P)
        mo_v = w_mix_out.rearrange("(k p) n -> p k n", p=P)
        x_v = x.rearrange("b (t p) d -> p (b t) d", p=P)
        out_v = out.rearrange("b (t p) d -> p (b t) d", p=P)

        def bc_row(v):
            return v.rearrange("(a n) -> a n", a=1).partition_broadcast(P) if len(v.shape) == 1 else v.partition_broadcast(P)

        def row_of(v):
            return v.rearrange("(a n) -> a n", a=1)

        x_ready = sem("x_ready")
        c_ready = sem("c_ready")
        mod_consts = sem("mod_consts")
        rope_consts = sem("rope_consts")
        dft_ready = sem("dft_ready")
        ones_ready = sem("ones_ready")
        silu_c_ready = sem("silu_c_ready")
        ada_ready = [sem(f"ada_ready{s}") for s in range(ADA_SLOTS)]
        ga_ready = sem("ga_ready")
        table_ready = sem("table_ready")
        ada_late = [sem(f"ada_late{s}") for s in range(ADA_SLOTS)]
        ada_free = [sem(f"ada_free{s}") for s in range(ADA_SLOTS)]
        ada_sum_ready = sem("ada_sum_ready")
        ada_reduced = sem("ada_reduced")
        ada_row_out = sem("ada_row_out")
        row_stored = [sem(f"row_stored{s}") for s in range(2)]
        sumsq_ready = sem("sumsq_ready")
        root_x, root_qk, root_y, root_x1, root_out = (sem(f"root_{v}") for v in ("x", "qk", "y", "x1", "out"))
        eps_ready = sem("eps_ready")
        y1_sum = sem("y1_sum")
        h_ready = sem("h_ready")
        tr_done = sem("tr_done")
        tr_out = sem("tr_out")
        slot_ready = [sem(f"slot_ready{s}") for s in range(RING)]
        slot_free = [sem(f"slot_free{s}") for s in range(RING)]
        mm_done = sem("mm_done")
        mm_out = [sem(f"mm_out{s}") for s in range(3)]
        rope_done = sem("rope_done")
        score_done = sem("score_done")
        nmx_ready = sem("nmx_ready")
        exp_done = sem("exp_done")
        probs_ready = sem("probs_ready")
        pt_done = sem("pt_done")
        pt_ready = sem("pt_ready")
        pv_done = sem("pv_done")
        attn_ready = sem("attn_ready")
        f1_done = sem("f1_done")
        ab_ready = [sem("ab_ready_act"), sem("ab_ready_dve")]
        f2_done = sem("f2_done")
        fT_ready = [sem("fT_ready_act"), sem("fT_ready_dve")]
        mixed_ready = sem("mixed_ready")
        y1_ready = sem("y1_ready")
        gg1_ready = sem("gg1_ready")
        rows_a = sem("rows_a")
        rows_b = sem("rows_b")
        rows_c = sem("rows_c")
        x1_ready = sem("x1_ready")
        x1_sumsq = sem("x1_sumsq")
        h2_ready = sem("h2_ready")
        route_consts = sem("route_consts")
        logits_done = sem("logits_done")
        logitsT_ready = sem("logitsT_ready")
        gathered = sem("gathered")
        xt_ready = sem("xt_ready")
        shifted_ready = sem("shifted_ready")
        route_exp = sem("route_exp")
        member_ready = sem("member_ready")
        ranks_done = sem("ranks_done")
        flags_ready = sem("flags_ready")
        flagsT_done = sem("flagsT_done")
        flagsT_ready = sem("flagsT_ready")
        prefix_done = sem("prefix_done")
        meta_ready = sem("meta_ready")
        p_ready = sem("p_ready")
        pw_ready = sem("pw_ready")
        gather_done = sem("gather_done")
        xg_ready = sem("xg_ready")
        st_done = sem("st_done")
        s_ready = sem("s_ready")
        gu_done = sem("gu_done")
        gu_ready = sem("gu_ready")
        gut_done = sem("gut_done")
        silu_ready = sem("silu_ready")
        act_ready = sem("act_ready")
        down_done = sem("down_done")
        y_ready = sem("y_ready")
        scat_done = sem("scat_done")
        scat_out = [sem("scat_out_even"), sem("scat_out_odd")]
        acc_sumsq = sem("acc_sumsq")
        out_ready = sem("out_ready")
        out_stored = sem("out_stored")
        o_dve = sem("o_dve")

        halves = []
        owner = []
        pair_of, use_of = [], []

        def chunk(src, n, count, pair):
            for k in range(count):
                halves.append((src, k * HK, n))
                owner.append((len(pair_of), k == count - 1))
            use_of.append(pair_of.count(pair))
            pair_of.append(pair)
            return len(pair_of) - 1
        G_IN = [chunk(w_in_v, n, 2, n % 2) for n in range(8)]
        G_GA = [chunk(w_in_v, 8 + n, 2, 2) for n in range(ND)]
        G_AO = [chunk(ao_v, n, 2, n % 2) for n in range(ND)]
        G_GF, G_FO = [], []
        for n in range(ND):
            G_GF.append(chunk(w_in_v, 12 + n, 2, 0))
            G_FO.append(chunk(fo_v, n, 1, 1))
        G_MO = [chunk(mo_v, n, 2, n % 2) for n in range(ND)]
        N_HALVES = len(halves)
        assert N_HALVES % MIX_SLOTS == 0
        MIX_USES = N_HALVES // MIX_SLOTS

        def out_count(g, t):
            return 2 * use_of[g] + t + 1

        def frees(s, upto):
            return sum(1 for r in range(s, upto + 1, MIX_SLOTS) if not owner[r][1])

        def half_used(r):
            g, last = owner[r]
            return (mm_done, g + 1) if last else (slot_free[r % MIX_SLOTS], frees(r % MIX_SLOTS, r))

        def ada_slot_used(j, s):
            early = j < 2 * ND
            if s == (ADA_SLOTS - 2 if early else ADA_SLOTS - 1):
                return ada_sum_ready, j + 1
            return ada_free[s], j + 1 - (2 * ND if s == ADA_SLOTS - 2 else 0)

        def ada_col(j):
            return (j % 2) * D + (j // 2) * CW if j < 2 * ND else j * CW

        def ada_load(eng, j, ready):
            for s in range(ADA_SLOTS):
                if j >= 1:
                    eng.wait_ge(*ada_slot_used(j - 1, s))
                eng.dma_start(ada3[s], w_ada_v[:, s * ADA_K:(s + 1) * ADA_K, ada_col(j):ada_col(j) + CW])\
                   .then_inc(ready[s], 16)

        M_H, M_Q, M_MIX, M_H2 = 0, 2 * ND, 2 * ND + 2 * (Q_CHUNKS + 1), 4 * ND + 2 * (Q_CHUNKS + 1)
        block = ctx.enter_context(nc.Block())

        def further_blocks(eng, body):
            eng.wait_ge(meta_ready, 1)
            n_blk = eng.value_load(meta[0:1, 0:1], min_val=NE, max_val=NBLK - 1)
            with eng.If(n_blk > NE):
                with eng.Fori(NE, n_blk) as i:
                    body(i)
            return n_blk

        @block.sync
        def _(sp):
            def half_load(r):
                src, k0, n = halves[r]
                s = r % MIX_SLOTS
                if r >= MIX_SLOTS:
                    sp.wait_ge(*half_used(r - MIX_SLOTS))
                sp.dma_start(ring3[s], src[:, k0:k0 + HK, n * CW:(n + 1) * CW]).then_inc(slot_ready[s], 16)

            early_half = {1: 0, 2: 2, 4: 1, 5: 3}
            sp.dma_start(x3, x_v).then_inc(x_ready, 16)
            sp.dma_start(cs, c.rearrange("b (k p) -> p (b k)", p=P), allow_slow_non_contiguous=True).then_inc(c_ready, 16)
            sp.dma_start(ident[:, :], k_ident).then_inc(mod_consts, 16)
            sp.dma_start(b_all[0:N_ADA, :], b_ada.rearrange("(j n) -> j n", n=CW)).then_inc(mod_consts, 16)
            sp.dma_start(g_pre, bc_row(g_pre_mix)).then_inc(mod_consts, 16)
            for j in range(2 * ND):
                ada_load(sp, j, ada_ready)
                if j in early_half:
                    half_load(early_half[j])
            sp.dma_start(cos3, k_cos.rearrange("(t p) d -> p t d", p=P)).then_inc(rope_consts, 16)
            sp.dma_start(sin3, k_sin.rearrange("(t p) d -> p t d", p=P)).then_inc(rope_consts, 16)
            sp.dma_start(g_qk[:, 0, :], bc_row(q_norm_g)).then_inc(rope_consts, 16)
            sp.dma_start(g_qk[:, 1, :], bc_row(k_norm_g)).then_inc(rope_consts, 16)
            sp.dma_start(dft_tok, k_dft_tok.rearrange("(t p) n -> p t n", p=P)).then_inc(dft_ready, 16)
            sp.dma_start(dft_ch, k_dft_ch.rearrange("(t p) n -> p t n", p=P)).then_inc(dft_ready, 16)
            for r in range(MIX_SLOTS, N_HALVES):
                half_load(r)

            def expert_load(e, i):
                for s in range(RING):
                    if i is None:
                        if s < MIX_SLOTS:
                            sp.wait_ge(*half_used(N_HALVES - MIX_SLOTS + s))
                        elif s == MIX_SLOTS:
                            sp.wait_ge(tr_done, M_H2)
                    elif s < 2:
                        sp.wait_ge(slot_free[s], i + frees(s, N_HALVES - 1))
                    elif s < MIX_SLOTS:
                        sp.wait_ge(gu_done, i)
                    else:
                        sp.wait_ge(down_done, 2 * i + s - MIX_SLOTS - 1)
                    if s < MIX_SLOTS:
                        src = (w_exp_gate, w_exp_up)[s % 2]
                        half = s // 2
                        sp.dma_start(ring3[s], src[e, half * HK * P:(half + 1) * HK * P, :]
                                     .rearrange("(k p) n -> p k n", p=P)).then_inc(slot_ready[s], 16)
                    else:
                        n = s - MIX_SLOTS
                        for g in range(2):
                            sp.dma_start(ring3[s][:, g * KFF:(g + 1) * KFF, :],
                                         w_exp_down[e, :, (2 * g + n) * CW:(2 * g + n + 1) * CW]
                                         .rearrange("(k p) n -> p k n", p=P)).then_inc(slot_ready[s], 16)

            expert_load(0, None)
            with sp.Fori(1, NE) as i:
                expert_load(i, i)
            sp.wait_ge(meta_ready, 1)
            n_over = sp.value_load(meta[0:1, 1:2], min_val=0, max_val=NOVER - 1)
            with sp.If(n_over > 0):
                with sp.Fori(0, n_over) as j:
                    e = sp.value_load(meta[0:1, bass.ds(j + 2, 1)], min_val=0, max_val=NE - 1)
                    expert_load(e, j + NE)
            sp.wait_ge(out_stored, 32)

        @block.gpsimd
        def _(pool):
            pool.memset(ones[:, :], 1.0).then_inc(ones_ready, 1)
            pool.memset(eps, EPS).then_inc(eps_ready, 1)
            for j in range(2 * ND, N_ADA):
                ada_load(pool, j, ada_late)
            pool.wait_ge(ada_sum_ready, N_ADA)
            for s in range(2):
                pool.wait_ge(row_stored[s], 16 * (N_ADA - 2 * ND) // 2)

            def mod_row(m):
                return mods_dram[m * ND:(m + 1) * ND, :].rearrange("(a j) n -> a (j n)", a=1)
            pool.dma_start(rows[0], bc_row(mod_row(2))).then_inc(rows_a, 16)
            pool.dma_start(rows[1], bc_row(g_post_mix)).then_inc(rows_a, 16)
            pool.dma_start(rows[2], bc_row(mod_row(4))).then_inc(rows_a, 16)
            pool.dma_start(rows[3], bc_row(g_pre_ffn)).then_inc(rows_a, 16)
            pool.wait_ge(gg1_ready, 1)
            pool.dma_start(rows[1], bc_row(mod_row(3))).then_inc(rows_b, 16)
            pool.wait_ge(mixed_ready, 2 * ND)
            pool.dma_start(wr[:, :, 0:NG], w_group_router.rearrange("(k p) n -> p k n", p=P)).then_inc(route_consts, 16)
            pool.dma_start(wr[:, :, NG:NR], w_expert_router.rearrange("(k p) n -> p k n", p=P)).then_inc(route_consts, 16)
            pool.dma_start(rb[:, 0:NG], row_of(b_group_router)).then_inc(route_consts, 16)
            pool.dma_start(rb[:, NG:NR], row_of(b_expert_router)).then_inc(route_consts, 16)
            pool.dma_start(upper, k_upper).then_inc(route_consts, 16)
            pool.dma_start(krow, bc_row(k_row)).then_inc(route_consts, 16)
            pool.wait_ge(h2_ready, 2)
            pool.dma_start(rows[2], bc_row(mod_row(5))).then_inc(rows_c, 16)
            pool.dma_start(rows[3], bc_row(g_post_ffn)).then_inc(rows_c, 16)

        acc_out = y1
        h2 = h_tok
        gained = [ring[t][:, 0:D] for t in range(TT)]
        o = [0]

        def take(n):
            o[0] += n
            return r_kvf[:, o[0] - n:o[0]]
        xg_flat = take(KD * SLOTS)
        xg = xg_flat.rearrange("p (k s) -> p k s", k=KD)
        xg4 = xg_flat.rearrange("p (g k s) -> p g k s", g=2, k=HK)
        y_sb = take(2 * CW).rearrange("p (n c) -> p n c", n=2)
        gu = take(FF)
        act_sb = take(KFF * SLOTS).rearrange("p (f s) -> p f s", f=KFF)
        silu_sb = take(KFF * SLOTS).rearrange("p (f s) -> p f s", f=KFF)
        s_mat = take(SEQ)
        p_mat = take(TT * SLOTS).rearrange("p (t s) -> p t s", t=TT)
        pw = take(TT * 2 * SLOTS).rearrange("p (t g s) -> p t g s", t=TT, g=2)
        o[0] = 0

        def tmp(n, *dims):
            o[0] += n
            return ada_w[:, o[0] - n:o[0]]
        logitsT = tmp(SEQ)
        lg = tmp(TT * NR).rearrange("p (t n) -> p t n", t=TT)
        gm = tmp(TT)
        ga = tmp(TT * NG).rearrange("p (t n) -> p t n", t=TT)
        oh_g = tmp(TT * NG).rearrange("p (t n) -> p t n", t=TT)
        gsh = tmp(TT * NG).rearrange("p (t n) -> p t n", t=TT)
        gex = tmp(TT * NG).rearrange("p (t n) -> p t n", t=TT)
        gmin = tmp(TT)
        elm = tmp(TT * NE).rearrange("p (t n) -> p t n", t=TT)
        e_tmp = tmp(TT * NE).rearrange("p (t n) -> p t n", t=TT)
        oh1 = tmp(TT * NE).rearrange("p (t n) -> p t n", t=TT)
        oh2 = tmp(TT * NE).rearrange("p (t n) -> p t n", t=TT)
        member = tmp(TT * NE).rearrange("p (t n) -> p t n", t=TT)
        comb = tmp(TT * NE).rearrange("p (t n) -> p t n", t=TT)
        rank_m = tmp(TT * NE).rearrange("p (t n) -> p t n", t=TT)
        m1, m2, i1, gw, de, w1, w2 = (tmp(TT) for _ in range(7))
        cnt = tmp(NE)
        flags = tmp(NCAND)
        flagsT = tmp(P)
        rank_c = tmp(TT * NCAND).rearrange("p (t n) -> p t n", t=TT)
        sel = tmp(NOVER * NCAND).rearrange("p (j n) -> p j n", j=NOVER)
        selx = tmp(NOVER * NCAND).rearrange("p (j n) -> p j n", j=NOVER)
        eblk = tmp(NOVER)
        nover = tmp(1)
        xt_sb = tmp(2 * CW).rearrange("p (n c) -> p n c", n=2)
        rank_b = tmp(TT * NBLK).rearrange("p (t n) -> p t n", t=TT)
        w_b = tmp(TT * NBLK).rearrange("p (t n) -> p t n", t=TT)
        assert o[0] <= 2 * D, o[0]
        k_slot = krow[:, 0:SLOTS]
        k_g4 = krow[:, 64:68]
        k_e32 = krow[:, 68:100]
        k_j8 = krow[:, 100:108]
        k_ec = krow[:, 108:108 + NCAND]

        @block.tensor
        def _(pe):
            def gemm_steps(g, lhsT):
                pair, use = pair_of[g], use_of[g]
                mine = [r for r in range(N_HALVES) if owner[r][0] == g]
                if use:
                    pe.wait_ge(mm_out[pair], 2 * use)
                for hh, r in enumerate(mine):
                    slot = r % MIX_SLOTS
                    pe.wait_ge(slot_ready[slot], 16 * (r // MIX_SLOTS + 1))
                    for k in range(HK):
                        kk = hh * HK + k
                        end = kk == len(mine) * HK - 1
                        for t in range(TT):
                            last = pe.matmul(bank[2 * pair + t][:, :], lhsT[:, kk, t * P:(t + 1) * P], ring3[slot][:, k, :],
                                             start=(kk == 0), stop=end)
                        if end:
                            last.then_inc(mm_done, 1)
                        elif k == HK - 1:
                            last.then_inc(slot_free[slot], 1)
                        yield

            def gemm(g, lhsT):
                for _ in gemm_steps(g, lhsT):
                    pass

            def transposes(m, src, ready, value):
                pe.wait_ge(ready, value)
                if m >= 2:
                    pe.wait_ge(tr_out, m - 1)
                for b in range(4):
                    last = pe.transpose(bank[6 + m % 2][:, b * P:(b + 1) * P], src[:, b * P:(b + 1) * P], ident[:, :])
                last.then_inc(tr_done, 1)

            def reduce_row(j):
                pe.wait_ge(ada_sum_ready, j + 1)
                if j < 2 * ND + 2:
                    pe.wait_ge(h_ready, 2 * ND)
                elif j in (4 * ND, 4 * ND + 1):
                    pe.wait_ge(mm_out[2], 2 * ND)
                else:
                    pe.wait_ge(ada_row_out, j - 2 * ND - 1)
                b = bank[4 + j % 2]
                cc = ada_col(j) // CW
                pe.matmul(b[0:1, :], ones[:, 0:1], accs[j % 2], start=True, stop=False)
                pe.matmul(b[0:1, :], ident[0:N_ADA, cc:cc + 1], b_all[0:N_ADA, :], start=False, stop=True)\
                  .then_inc(ada_reduced, 1)

            pe.wait_ge(ones_ready, 1)
            pe.wait_ge(mod_consts, 48)
            pe.wait_ge(silu_c_ready, 1)
            first = [gemm_steps(G_IN[a], hT) for a in range(2)]
            for n in range(ND):
                for a in range(2):
                    if n:
                        if a == 0:
                            pe.wait_ge(tr_out, M_H + 2 * n)
                        for _ in range(CW // P):
                            next(first[a])
                    j = 2 * n + a
                    if n:
                        pe.wait_ge(h_ready, 2 * n)
                    b = bank[4 + a]
                    cc = ada_col(j) // CW
                    pe.matmul(b[:, :], ident[0:N_ADA, cc:cc + 1].to_broadcast([N_ADA, P]), b_all[0:N_ADA, :],
                              start=True, stop=False)
                    pe.wait_ge(ada_ready[ADA_SLOTS - 1], 16 * (j + 1))
                    for k in range(ADA_K):
                        kk = (ADA_SLOTS - 1) * ADA_K + k
                        last = pe.matmul(b[:, :], s_col[:, kk:kk + 1].to_broadcast([P, P]), ada3[ADA_SLOTS - 1][:, k, :],
                                         start=False, stop=False)
                    last.then_inc(ada_free[ADA_SLOTS - 1], 1)
                    pe.wait_ge(ada_sum_ready, j + 1)
                    pe.matmul(b[:, :], ones[:, 0:P], accs[a], start=False, stop=True).then_inc(ada_reduced, 1)
                for t in range(TT):
                    transposes(M_H + 2 * n + t, h_tok[:, t, n * CW:(n + 1) * CW], h_ready, 2 * n + t + 1)
            pe.wait_ge(tr_out, M_Q)
            for g in G_IN:
                if g < 2:
                    for _ in first[g]:
                        pass
                else:
                    gemm(g, hT)
                reduce_row(2 * ND + g)
                if 1 <= g <= Q_CHUNKS + 1:
                    for t in range(TT):
                        transposes(M_Q + 2 * (g - 1) + t, qr[:, t, :], rope_done, 2 * (g - 1) + t + 1)
            for pair in range(2):
                pe.wait_ge(mm_out[pair], 8)

            pe.wait_ge(dft_ready, 32)
            for i in range(KF):
                if i >= 4:
                    pe.wait_ge(ab_ready[i % 2], (i - 4) // 2 + 1)
                for t in range(TT):
                    last = pe.matmul(bank[i % 4][:, :], f_sb[:, t, i * P:(i + 1) * P], dft_tok[:, t, :],
                                     start=(t == 0), stop=(t == TT - 1))
                last.then_inc(f1_done, 1)
            for i in range(KF):
                grp, cc = i // 2, i % 2
                for a in range(2):
                    pe.wait_ge(ab_ready[a], i // 2 + 1)
                if i < 4:
                    pe.wait_ge(ab_ready[i % 2], (i + 4) // 2 + 1)
                else:
                    pe.wait_ge(fT_ready[i % 2], (i - 4) // 2 + 1)
                for kc in range(2):
                    for part in range(2):
                        last = pe.matmul(bank[i % 4][:, 0:SEQ], dft_ch[:, kc, part * FG + cc * P:part * FG + (cc + 1) * P],
                                         ab[:, 2 * grp + kc, part * SEQ:(part + 1) * SEQ],
                                         start=(kc == 0 and part == 0), stop=(kc == 1 and part == 1))
                last.then_inc(f2_done, 1)

            pe.wait_ge(tr_out, M_MIX)
            for a in range(2):
                pe.wait_ge(fT_ready[a], KF // 2)

            def scores(h):
                if h >= 2:
                    pe.wait_ge(exp_done, 2 * (h - 1))
                for t in range(TT):
                    last = pe.matmul(bank[h % 2][:, t * SEQ:(t + 1) * SEQ], qT[:, h, t * P:(t + 1) * P], kT[:, h // 4, :],
                                     start=True, stop=True)
                last.then_inc(score_done, 1)

            def probs_t(h):
                pe.wait_ge(probs_ready, h + 1)
                if h >= 2:
                    pe.wait_ge(pt_ready, h - 1)
                for s in range(TT):
                    for t in range(TT):
                        last = pe.transpose(bank[2 + h % 2][:, s * SEQ + t * P:s * SEQ + (t + 1) * P],
                                            probs[h % 2][:, t, s * P:(s + 1) * P], ident[:, :])
                last.then_inc(pt_done, 1)

            def pv(h):
                pe.wait_ge(pt_ready, h + 1)
                if h >= 2:
                    pe.wait_ge(attn_ready, h - 1)
                for s in range(TT):
                    last = pe.matmul(bank[6 + h % 2][:, 0:SEQ], v_sb[:, s, (h // 4) * HD:(h // 4 + 1) * HD], pT[h % 2][:, s, :],
                                     start=(s == 0), stop=(s == TT - 1))
                last.then_inc(pv_done, 1)

            def gate_steps():
                pe.wait_ge(ada_row_out, 2 * ND)
                for g in G_GA:
                    yield from gemm_steps(g, hT)
            gates = gate_steps()

            def fill(count):
                for _ in range(count):
                    next(gates, None)

            scores(0)
            for h in range(NH):
                if h + 1 < NH:
                    scores(h + 1)
                fill(2)
                probs_t(h)
                fill(1)
                if h >= 1:
                    pv(h - 1)
                fill(1)
            pv(NH - 1)
            fill(1)

            pe.wait_ge(attn_ready, NH)
            for n in range(ND):
                gemm(G_AO[n], qT)
                reduce_row(4 * ND + n)
            for n in range(ND):
                gemm(G_GF[n], hT)
                gemm(G_FO[n], fT)
                reduce_row(5 * ND + n)
                if n:
                    for t in range(TT):
                        transposes(M_MIX + 2 * (n - 1) + t, mixed[:, t, (n - 1) * CW:n * CW], mixed_ready, 2 * (n - 1) + t + 1)
            for t in range(TT):
                transposes(M_MIX + 2 * (ND - 1) + t, mixed[:, t, (ND - 1) * CW:D], mixed_ready, 2 * (ND - 1) + t + 1)
            pe.wait_ge(tr_out, M_H2)
            for g in G_MO:
                gemm(g, mT)

            def gather():
                for n in range(2):
                    for t in range(TT):
                        for g in range(2):
                            last = pe.matmul(bank[2 + n][g * SLOTS:(g + 1) * SLOTS, :], p_mat[:, t, :],
                                             h2[:, t, (2 * g + n) * CW:(2 * g + n + 1) * CW], start=(t == 0), stop=(t == TT - 1),
                                             skip_group_check=True)
                    last.then_inc(gather_done, 1)

            def gather_t():
                for n in range(2):
                    for b in range(4):
                        last = pe.transpose(bank[6 + n][:, b * P:(b + 1) * P], xt_sb[:, n, b * P:(b + 1) * P], ident[:, :])
                    last.then_inc(gathered, 1)

            pe.wait_ge(ada_row_out, N_ADA - 2 * ND)
            for t in range(TT):
                for n in range(ND):
                    transposes(M_H2 + t * ND + n, h2[:, t, n * CW:(n + 1) * CW], h2_ready, t + 1)
                if t == 0:
                    pe.wait_ge(route_consts, 96)
                for k in range(KD):
                    if k % 4 == 0:
                        pe.wait_ge(tr_out, M_H2 + t * ND + k // 4 + 1)
                    pe.matmul(bank[4][0:NR, t * P:(t + 1) * P], wr[:, k, :], h2T[:, k, t * P:(t + 1) * P], start=(k == 0), stop=False)
                last = pe.matmul(bank[4][0:NR, t * P:(t + 1) * P], rb, ones_row[:, 0:P], start=False, stop=True)
            last.then_inc(logits_done, 1)
            pe.wait_ge(logitsT_ready, 1)
            for t in range(TT):
                last = pe.transpose(bank[5][:, 128 * (t + 2):128 * (t + 2) + NR], logitsT[0:NR, t * P:(t + 1) * P], ident[0:NR, 0:NR])
            last.then_inc(logits_done, 1)
            pe.wait_ge(member_ready, 1)
            pe.matmul(bank[5][:, 0:NE], upper, member[:, 0, :], start=True, stop=True)
            pe.matmul(bank[5][:, NE:2 * NE], ones[:, 0:P], member[:, 0, :], start=True, stop=False)
            pe.matmul(bank[5][:, NE:2 * NE], upper, member[:, 1, :], start=False, stop=True)
            pe.matmul(bank[5][:, 2 * NE:3 * NE], ones[:, 0:P], member[:, 0, :], start=True, stop=False)
            pe.matmul(bank[5][:, 2 * NE:3 * NE], ones[:, 0:P], member[:, 1, :], start=False, stop=True).then_inc(ranks_done, 1)
            pe.wait_ge(p_ready, 1)
            gather()
            pe.wait_ge(flags_ready, 1)
            pe.transpose(bank[4][0:NCAND, 128:256], flags, ident[:, :]).then_inc(flagsT_done, 1)
            pe.wait_ge(flagsT_ready, 1)
            pe.matmul(bank[4][:, 256:256 + NCAND], flagsT[0:NCAND, :], upper[0:NCAND, 0:NCAND], start=True, stop=True)\
              .then_inc(prefix_done, 1)

            def expert_block(i):
                pe.wait_ge(xg_ready, 2 * i + 2)
                for half in range(2):
                    for a in range(2):
                        pe.wait_ge(slot_ready[2 * half + a], 16 * (i + 1 + MIX_USES))
                    for k in range(HK):
                        kk = half * HK + k
                        for a in range(2):
                            last = pe.matmul(bank[0][a * SLOTS:(a + 1) * SLOTS, :], xg[:, kk, :], ring3[2 * half + a][:, k, :],
                                             start=(kk == 0), stop=(kk == KD - 1), skip_group_check=True)
                            if kk == HK - 1:
                                last.then_inc(slot_free[a], 1)
                last.then_inc(gu_done, 1)
                pe.wait_ge(p_ready, i + 2)
                gather()
                pe.wait_ge(pw_ready, i + 1)
                pe.wait_ge(scat_out[0], 2 * i + 1)
                for t in range(TT):
                    last = pe.transpose(bank[4][:, t * P:(t + 1) * P], pw[:, t, :, :].rearrange("p g s -> p (g s)"), ident[:, :])
                last.then_inc(st_done, 1)
                pe.wait_ge(gu_ready, i + 1)
                for f in range(KFF):
                    last = pe.transpose(bank[1][:, f * P:(f + 1) * P], gu[:, f * P:(f + 1) * P], ident[:, :])
                last.then_inc(gut_done, 1)
                pe.wait_ge(xt_ready, 2 * i + 4)
                pe.wait_ge(scat_out[1], 2 * i + 1)
                gather_t()
                pe.wait_ge(act_ready, i + 1)
                for n in range(2):
                    pe.wait_ge(slot_ready[MIX_SLOTS + n], 32 * (i + 1))
                    for f in range(KFF):
                        for g in range(2):
                            last = pe.matmul(bank[2 + n][g * SLOTS:(g + 1) * SLOTS, :], act_sb[:, f, :],
                                             ring3[MIX_SLOTS + n][:, g * KFF + f, :], start=(f == 0), stop=(f == KFF - 1),
                                             skip_group_check=True)
                    last.then_inc(down_done, 1)
                pe.wait_ge(s_ready, i + 1)
                pe.wait_ge(xg_ready, 2 * i + 4)
                for n in range(2):
                    pe.wait_ge(y_ready, 2 * i + n + 1)
                    for t in range(TT):
                        if n:
                            pe.wait_ge(scat_out[t], 2 * i + 2)
                        for g in range(2):
                            last = pe.matmul(bank[4 + 2 * t + g][:, :], s_mat[g * SLOTS:(g + 1) * SLOTS, t * P:(t + 1) * P],
                                             y_sb[g * SLOTS:(g + 1) * SLOTS, n, :], start=True, stop=True)
                        last.then_inc(scat_done, 1)

            pe.wait_ge(xt_ready, 2)
            gather_t()
            with pe.Fori(0, NE) as i:
                expert_block(i)
            further_blocks(pe, expert_block)

        @block.scalar
        def _(act):
            act.wait_ge(c_ready, 16)
            act.activation(s_col, cs, ACT.Silu).then_inc(silu_c_ready, 1)
            act.wait_ge(x_ready, 16)
            for t in range(TT):
                act.activation(h_tok[:, t, :], x3[:, t, :], ACT.Square, accum_out=ss[:, t:t + 1]).then_inc(sumsq_ready, 1)

            def root(dst, src, count, signal):
                act.activation(dst, src, ACT.Sqrt, bias=eps, scale=1.0 / count).then_inc(signal, 1)

            act.wait_ge(eps_ready, 1)
            act.wait_ge(sumsq_ready, TT)
            root(rstd[:, 0:TT], ss[:, 0:TT], D, root_x)

            def tr_copy(m, dst):
                act.wait_ge(tr_done, m + 1)
                act.activation(dst, bank[6 + m % 2][:, :].rearrange("p (b s) -> p b s", b=4), ACT.Copy).then_inc(tr_out, 1)

            def store_row(j):
                act.wait_ge(ada_reduced, j + 1)
                act.activation(accs[j % 2][0:1, :], bank[4 + j % 2][0:1, :], ACT.Copy).then_inc(ada_row_out, 1)
                act.wait_ge(ada_row_out, j - 2 * ND + 1)
                act.dma_start(mods_dram[j:j + 1, :], accs[j % 2][0:1, :]).then_inc(row_stored[j % 2], 16)

            for n in range(ND):
                for t in range(TT):
                    tr_copy(M_H + 2 * n + t, hT[:, 4 * n:4 * n + 4, t * P:(t + 1) * P])
            for g in range(8):
                act.wait_ge(mm_done, g + 1)
                pair = pair_of[g]
                for t in range(TT):
                    src = bank[2 * pair + t][:, :]
                    if g <= Q_CHUNKS:
                        if g:
                            act.wait_ge(rope_done, 2 * (g - 1) + t + 1)
                        for hh in range(HPC):
                            act.activation(rope_junk[:, hh * HD:(hh + 1) * HD], src[:, hh * HD:(hh + 1) * HD], ACT.Square,
                                           accum_out=rms_q[:, t * HPC + hh:t * HPC + hh + 1])
                        dst = raw[:, t, :]
                    else:
                        dst = v_sb[:, t, :] if g == Q_CHUNKS + 1 else f_sb[:, t, (g - Q_CHUNKS - 2) * CW:(g - Q_CHUNKS - 1) * CW]
                    act.activation(dst, src, ACT.Copy).then_inc(mm_out[pair], 1)
                    if g <= Q_CHUNKS:
                        act.wait_ge(mm_out[pair], out_count(g, t))
                        rq = rms_q[:, t * HPC:(t + 1) * HPC]
                        root(rq, rq, HD, root_qk)
                store_row(2 * ND + g)
                if 1 <= g <= Q_CHUNKS + 1:
                    for t in range(TT):
                        dst = qT[:, 4 * (g - 1):4 * g, t * P:(t + 1) * P] if g <= Q_CHUNKS else kT[:, :, t * P:(t + 1) * P]
                        tr_copy(M_Q + 2 * (g - 1) + t, dst)

            def attn_copy(h):
                act.wait_ge(pv_done, h + 1)
                act.activation(qT[:, h, :], bank[6 + h % 2][:, 0:SEQ], ACT.Copy).then_inc(attn_ready, 1)

            for i in range(0, KF, 2):
                act.wait_ge(f1_done, i + 1)
                act.activation(ab[:, i, :], bank[i % 4][:, :], ACT.Copy).then_inc(ab_ready[0], 1)
            for i in range(0, KF, 2):
                act.wait_ge(f2_done, i + 1)
                act.activation(fT[:, i, :], bank[i % 4][:, 0:SEQ], ACT.Copy).then_inc(fT_ready[0], 1)

            def gate_copy(n):
                act.wait_ge(mm_done, G_GA[n] + 1)
                for t in range(TT):
                    act.activation(ga_sb[:, t, n * CW:(n + 1) * CW], bank[4 + t][:, :], ACT.Copy).then_inc(mm_out[2], 1)

            for h in range(NH):
                if h % 4 == 0 and h:
                    gate_copy(h // 4 - 1)
                act.wait_ge(nmx_ready, h + 1)
                if h >= 2:
                    act.wait_ge(pt_done, h - 1)
                for t in range(TT):
                    b = 2 * (h % 2) + t
                    act.activation(probs[h % 2][:, t, :], bank[h % 2][:, t * SEQ:(t + 1) * SEQ], ACT.Exp,
                                   bias=nmx[:, b:b + 1], scale=SCALE, accum_out=rs[:, b:b + 1]).then_inc(exp_done, 1)
                if h >= 2:
                    attn_copy(h - 2)
            attn_copy(NH - 2)
            attn_copy(NH - 1)
            gate_copy(ND - 1)
            act.wait_ge(mm_out[2], 2 * ND)
            for n in range(ND):
                for t in range(TT):
                    v = ga_sb[:, t, n * CW:(n + 1) * CW]
                    act.activation(v, v, ACT.Sigmoid).then_inc(ga_ready, 1)
            for n in range(ND):
                store_row(4 * ND + n)
            for n in range(ND):
                act.wait_ge(mm_done, G_GF[n] + 1)
                for t in range(TT):
                    if n:
                        act.wait_ge(mixed_ready, 2 * (n - 1) + t + 1)
                    act.activation(gate3[:, t, :], bank[t][:, :], ACT.Sigmoid).then_inc(mm_out[0], 1)
                store_row(5 * ND + n)
                if n:
                    for t in range(TT):
                        tr_copy(M_MIX + 2 * (n - 1) + t, mT[:, 4 * (n - 1):4 * n, t * P:(t + 1) * P])
            for t in range(TT):
                tr_copy(M_MIX + 2 * (ND - 1) + t, mT[:, 4 * (ND - 1):4 * ND, t * P:(t + 1) * P])
            root(junk4[:, 0:1], eps, 1, table_ready)
            for n in range(ND):
                act.wait_ge(mm_done, G_MO[n] + 1)
                for t in range(TT):
                    b = bank[2 * (n % 2) + t][:, :]
                    y = y1[:, t, n * CW:(n + 1) * CW]
                    act.activation(y, b, ACT.Copy).then_inc(mm_out[n % 2], 1)
                    act.wait_ge(mm_out[n % 2], out_count(G_MO[n], t))
                    act.activation(bank[6 + t][:, :], y, ACT.Square, accum_out=ss[:, t * ND + n:t * ND + n + 1]).then_inc(y1_ready, 1)
            act.wait_ge(y1_ready, 2 * ND)
            for t in range(TT):
                act.activation(junk4[:, t * ND:(t + 1) * ND], ss[:, t * ND:(t + 1) * ND], ACT.Copy, accum_out=rs[:, t:t + 1]).then_inc(y1_sum, 1)
            act.wait_ge(y1_sum, TT)
            root(rstd[:, 0:TT], rs[:, 0:TT], D, root_y)
            for t in range(TT):
                act.wait_ge(x1_ready, t + 1)
                act.activation(y1[:, t, :], x3[:, t, :], ACT.Square, accum_out=rs[:, t:t + 1]).then_inc(x1_sumsq, 1)
                act.wait_ge(x1_sumsq, t + 1)
                root(rinv[:, t:t + 1], rs[:, t:t + 1], D, root_x1)
            for t in range(TT):
                for n in range(ND):
                    tr_copy(M_H2 + t * ND + n, h2T[:, 4 * n:4 * n + 4, t * P:(t + 1) * P])
            act.wait_ge(shifted_ready, 1)
            act.activation(gex, gsh, ACT.Exp).then_inc(route_exp, 1)
            act.wait_ge(shifted_ready, 2)
            act.activation(w2, de, ACT.Exp).then_inc(route_exp, 1)

            act.wait_ge(route_exp, 2)
            act.activation(junk4[:, 1:2], eps, ACT.Silu).then_inc(table_ready, 1)

            def gather_copy(v):
                for n in range(2):
                    act.wait_ge(gather_done, 2 * v + n + 1)
                    act.activation(xt_sb[:, n, :], bank[2 + n][:, :], ACT.Copy).then_inc(xt_ready, 1)

            def gather_t_copy(v):
                for n in range(2):
                    act.wait_ge(gathered, 2 * v + n + 1)
                    act.activation(xg4[:, :, 4 * n:4 * n + 4, :], bank[6 + n][:, :].rearrange("p (k g s) -> p g k s", g=2, s=SLOTS),
                                   ACT.Copy).then_inc(xg_ready, 1)

            def expert_block(i):
                gather_copy(i + 1)
                act.wait_ge(st_done, i + 1)
                act.activation(s_mat, bank[4][:, 0:SEQ], ACT.Copy).then_inc(s_ready, 1)
                act.wait_ge(gut_done, i + 1)
                act.activation(silu_sb, bank[1][:, :].rearrange("p (f s) -> p f s", f=KFF)[:, :, 0:SLOTS], ACT.Silu)\
                   .then_inc(silu_ready, 1)
                gather_t_copy(i + 1)
                for n in range(2):
                    act.wait_ge(down_done, 2 * i + n + 1)
                    act.activation(y_sb[:, n, :], bank[2 + n][:, :], ACT.Copy).then_inc(y_ready, 1)

            gather_copy(0)
            gather_t_copy(0)
            with act.Fori(0, NE) as i:
                expert_block(i)
            n_blk = further_blocks(act, expert_block)
            root(junk4[:, 2:3], eps, 1, table_ready)
            for t in range(TT):
                act.wait_ge(scat_out[t], 2 * n_blk + 1)
                act.activation(r_q[:, t * D:(t + 1) * D], acc_out[:, t, :], ACT.Square, accum_out=ss[:, t:t + 1]).then_inc(acc_sumsq, 1)
                act.wait_ge(acc_sumsq, t + 1)
                root(rstd[:, t:t + 1], ss[:, t:t + 1], D, root_out)
            for t in range(TT):
                act.wait_ge(out_ready, t + 1)
                act.dma_start(out_v[:, t, :], x3[:, t, :]).then_inc(out_stored, 16)
            act.wait_ge(out_stored, 32)

        @block.vector
        def _(dve):
            order = Order(dve, o_dve)

            def signal(ins, s, value):
                ins.then_inc(s, 1)
                dve.wait_ge(s, value)

            def ada_chunk(j):
                a = accs[j % 2]
                if j >= 2 * ND + 2:
                    dve.wait_ge(row_stored[j % 2], 16 * ((j - 2 * ND) // 2))
                elif j >= 2:
                    dve.wait_ge(ada_reduced, j - 1)
                slots = ADA_SLOTS - 1 if j < 2 * ND else ADA_SLOTS
                for s in range(slots):
                    dve.wait_ge(*((ada_ready[s], 16 * (j + 1)) if j < 2 * ND else (ada_late[s], 16 * (j + 1 - 2 * ND))))
                    for k in range(ADA_K):
                        kk = s * ADA_K + k
                        if kk == 0:
                            ins = dve.tensor_scalar(a, ada3[s][:, k, :], s_col[:, kk:kk + 1], None, ALU.mult)
                        else:
                            ins = dve.scalar_tensor_tensor(a, ada3[s][:, k, :], s_col[:, kk:kk + 1], a, ALU.mult, ALU.add)
                        if k < ADA_K - 1:
                            order(ins)
                        elif s < slots - 1:
                            signal(ins, *ada_slot_used(j, s))
                        else:
                            ins.then_inc(ada_sum_ready, 1)

            dve.wait_ge(root_x, 1)
            order(dve.reciprocal(rstd[:, 0:TT], rstd[:, 0:TT]))
            for t in range(TT):
                order(dve.tensor_scalar(h_tok[:, t, :], x3[:, t, :], rstd[:, t:t + 1], None, ALU.mult))
            dve.wait_ge(silu_c_ready, 1)
            dve.wait_ge(mod_consts, 48)
            for n in range(ND):
                ada_chunk(2 * n)
                ada_chunk(2 * n + 1)
                cols = slice(n * CW, (n + 1) * CW)
                dve.wait_ge(ada_reduced, 2 * n + 2)
                order(dve.scalar_tensor_tensor(a_row, bank[5][:, :], 1.0, g_pre[:, cols], ALU.add, ALU.mult))
                for t in range(TT):
                    order(dve.tensor_tensor(h_tok[:, t, cols], h_tok[:, t, cols], a_row, ALU.mult))
                    dve.tensor_tensor(h_tok[:, t, cols], h_tok[:, t, cols], bank[4][:, :], ALU.add).then_inc(h_ready, 1)

            dve.wait_ge(rope_consts, 64)
            for a in range(2):
                for t in range(TT):
                    order(dve.tensor_tensor(cosg[a][:, t, :], cos3[:, t, :], g_qk[:, a, :], ALU.mult))
                    sv = sin3[:, t, :].rearrange("p (a b c) -> p a b c", a=2, b=2)
                    gv = g_qk[:, a, :].rearrange("p (a b c) -> p a b c", a=2, b=2)
                    dv = sing[a][:, t, :].rearrange("p (a b c) -> p a b c", a=2, b=2)
                    for b in range(2):
                        order(dve.tensor_tensor(dv[:, :, b, :], sv[:, :, b, :], gv[:, :, 1 - b, :], ALU.mult))

            def rope(g, t):
                a = 0 if g < Q_CHUNKS else 1
                v = raw[:, t, :]
                v3 = v.rearrange("p (h d) -> p h d", h=HPC)
                dve.wait_ge(mm_out[pair_of[g]], out_count(g, t))
                if g or t:
                    dve.wait_ge(rope_done, 2 * g + t)
                dve.wait_ge(root_qk, 2 * g + t + 1)
                rq = rms_q[:, t * HPC:(t + 1) * HPC]
                order(dve.reciprocal(rq, rq))
                order(dve.tensor_tensor(v3, v3, rq.unsqueeze(2).to_broadcast([P, HPC, HD]), ALU.mult))
                if g:
                    dve.wait_ge(tr_done, M_Q + 2 * (g - 1) + t + 1)
                q3 = qr[:, t, :].rearrange("p (h d) -> p h d", h=HPC)
                order(dve.tensor_tensor(q3, v3, cosg[a][:, t, :].unsqueeze(1).to_broadcast([P, HPC, HD]), ALU.mult))
                v5 = v.rearrange("p (h a b c) -> p h a b c", h=HPC, a=2, b=2)
                r5 = rope_tmp.rearrange("p (h a b c) -> p h a b c", h=HPC, a=2, b=2)
                s4 = sing[a][:, t, :].rearrange("p (a b c) -> p a b c", a=2, b=2)
                for b in range(2):
                    order(dve.tensor_tensor(r5[:, :, :, b, :], v5[:, :, :, 1 - b, :],
                                            s4[:, :, b, :].unsqueeze(1).to_broadcast([P, HPC, 2, HD // 4]), ALU.mult))
                dve.tensor_tensor(qr[:, t, :], qr[:, t, :], rope_tmp, ALU.add).then_inc(rope_done, 1)

            for g in range(8):
                ada_chunk(2 * ND + g)
                if g <= Q_CHUNKS:
                    for t in range(TT):
                        rope(g, t)

            def row_max(h):
                b = 2 * (h % 2)
                dve.wait_ge(score_done, h + 1)
                if h >= 2:
                    dve.wait_ge(exp_done, 2 * (h - 1))
                order(dve.tensor_reduce(mx[:, b:b + 2], bank[h % 2][:, :].rearrange("p (t s) -> p t s", t=TT), AX_X, ALU.max))
                dve.tensor_scalar(nmx[:, b:b + 2], mx[:, b:b + 2], -SCALE, None, ALU.mult).then_inc(nmx_ready, 1)

            def normalise(h):
                b = 2 * (h % 2)
                dve.wait_ge(exp_done, 2 * (h + 1))
                order(dve.reciprocal(rinv[:, b:b + 2], rs[:, b:b + 2]))
                for t in range(TT):
                    last = dve.tensor_scalar(probs[h % 2][:, t, :], probs[h % 2][:, t, :], rinv[:, b + t:b + t + 1], None, ALU.mult)
                last.then_inc(probs_ready, 1)

            def pt_copy(h):
                dve.wait_ge(pt_done, h + 1)
                if h >= 2:
                    dve.wait_ge(pv_done, h - 1)
                dve.tensor_copy(pT[h % 2], bank[2 + h % 2][:, :].rearrange("p (s q) -> p s q", s=TT)).then_inc(pt_ready, 1)

            for i in range(1, KF, 2):
                dve.wait_ge(f1_done, i + 1)
                dve.tensor_copy(ab[:, i, :], bank[i % 4][:, :]).then_inc(ab_ready[1], 1)
            for i in range(1, KF, 2):
                dve.wait_ge(f2_done, i + 1)
                dve.tensor_copy(fT[:, i, :], bank[i % 4][:, 0:SEQ]).then_inc(fT_ready[1], 1)
            row_max(0)
            for h in range(NH):
                if h + 1 < NH:
                    row_max(h + 1)
                normalise(h)
                if h >= 1:
                    pt_copy(h - 1)
            pt_copy(NH - 1)
            for n in range(ND):
                ada_chunk(4 * ND + n)
                g, cols = G_AO[n], slice(n * CW, (n + 1) * CW)
                dve.wait_ge(mm_done, g + 1)
                dve.wait_ge(ga_ready, 2 * n + 2)
                for t in range(TT):
                    dve.tensor_tensor(mixed[:, t, cols], ga_sb[:, t, cols], bank[2 * pair_of[g] + t][:, :], ALU.mult)\
                       .then_inc(mm_out[pair_of[g]], 1)
            for n in range(ND):
                ada_chunk(5 * ND + n)
                g, cols = G_FO[n], slice(n * CW, (n + 1) * CW)
                dve.wait_ge(mm_done, g + 1)
                for t in range(TT):
                    dve.wait_ge(mm_out[0], out_count(G_GF[n], t))
                    signal(dve.tensor_tensor(gate3[:, t, :], gate3[:, t, :], bank[2 + t][:, :], ALU.mult), mm_out[1], out_count(g, t))
                    dve.tensor_tensor(mixed[:, t, cols], mixed[:, t, cols], gate3[:, t, :], ALU.add).then_inc(mixed_ready, 1)

            dve.wait_ge(rows_a, 64)
            signal(dve.tensor_tensor(rows[0], rows[0], rows[1], ALU.mult), gg1_ready, 1)
            order(dve.scalar_tensor_tensor(rows[2], rows[2], 1.0, rows[3], ALU.add, ALU.mult))
            for n in range(ND):
                cols = slice(n * CW, (n + 1) * CW)
                for t in range(TT):
                    dve.wait_ge(y1_ready, 2 * n + t + 1)
                    order(dve.tensor_tensor(y1[:, t, cols], y1[:, t, cols], rows[0][:, cols], ALU.mult))
            dve.wait_ge(root_y, 1)
            order(dve.reciprocal(rstd[:, 0:TT], rstd[:, 0:TT]))
            for t in range(TT):
                dve.scalar_tensor_tensor(x3[:, t, :], y1[:, t, :], rstd[:, t:t + 1], x3[:, t, :], ALU.mult, ALU.add)\
                   .then_inc(x1_ready, 1)
            dve.wait_ge(x1_ready, TT)
            dve.wait_ge(rows_b, 16)
            dve.wait_ge(mm_done, G_MO[-1] + 1)
            for t in range(TT):
                dve.wait_ge(root_x1, t + 1)
                order(dve.reciprocal(rinv[:, t:t + 1], rinv[:, t:t + 1]))
                order(dve.scalar_tensor_tensor(h2[:, t, :], x3[:, t, :], rinv[:, t:t + 1], rows[2], ALU.mult, ALU.mult))
                dve.tensor_tensor(h2[:, t, :], h2[:, t, :], rows[1], ALU.add).then_inc(h2_ready, 1)
            for t in range(TT):
                signal(dve.memset(acc_out[:, t, :], 0.0), scat_out[t], 1)

            def select(col):
                for t in range(TT):
                    last = dve.tensor_scalar(p_mat[:, t, :], k_slot, rank_b[:, t, col], None, ALU.is_equal)
                last.then_inc(p_ready, 1)

            dve.wait_ge(logits_done, 1)
            dve.tensor_copy(logitsT[0:NR, :], bank[4][0:NR, 0:SEQ]).then_inc(logitsT_ready, 1)
            dve.wait_ge(logits_done, 2)
            order(dve.tensor_copy(lg, bank[5][:, 2 * P:4 * P].rearrange("p (t n) -> p t n", t=TT)[:, :, 0:NR]))

            def bc(v, n):
                return v.unsqueeze(2).to_broadcast([P, TT, n])

            def kbc(v, n):
                return v.unsqueeze(1).to_broadcast([P, TT, n])

            def first_max(oh, vals, top, work, low, k_idx, n):
                order(dve.tensor_reduce(top, vals, AX_X, ALU.max))
                order(dve.tensor_tensor(work, vals, bc(top, n), ALU.is_equal))
                order(dve.tensor_tensor(work, work, kbc(k_idx, n), ALU.mult))
                order(dve.tensor_reduce(low, work, AX_X, ALU.min))
                order(dve.tensor_tensor(oh, kbc(k_idx, n), bc(low, n), ALU.is_equal))

            gl = lg[:, :, 0:NG]
            first_max(oh_g, gl, gm, ga, gmin, k_g4, NG)
            signal(dve.tensor_tensor(gsh, gl, bc(gm, NG), ALU.subtract), shifted_ready, 1)
            order(dve.tensor_scalar(ga, oh_g, -1.0, FAR, ALU.add, ALU.mult))
            for t in range(TT):
                order(dve.tensor_tensor(elm[:, t, :].rearrange("p (g e) -> p g e", g=NG),
                                        lg[:, t, NG:NR].rearrange("p (g e) -> p g e", g=NG),
                                        ga[:, t, :].unsqueeze(2).to_broadcast([P, NG, EG]), ALU.add))
            first_max(oh1, elm, m1, e_tmp, i1, k_e32, NE)
            order(dve.scalar_tensor_tensor(elm, oh1, -2 * FAR, elm, ALU.mult, ALU.add))
            first_max(oh2, elm, m2, e_tmp, i1, k_e32, NE)
            signal(dve.tensor_tensor(de, m2, m1, ALU.subtract), shifted_ready, 2)
            signal(dve.tensor_tensor(member, oh1, oh2, ALU.add), member_ready, 1)
            dve.wait_ge(route_exp, 2)
            order(dve.tensor_reduce(gw, gex, AX_X, ALU.add))
            order(dve.tensor_scalar(w1, w2, 1.0, None, ALU.add))
            order(dve.tensor_tensor(w1, w1, gw, ALU.mult))
            order(dve.reciprocal(w1, w1))
            order(dve.tensor_tensor(w2, w2, w1, ALU.mult))
            order(dve.tensor_tensor(comb, oh1, bc(w1, NE), ALU.mult))
            order(dve.tensor_tensor(e_tmp, oh2, bc(w2, NE), ALU.mult))
            order(dve.tensor_tensor(comb, comb, e_tmp, ALU.add))
            dve.wait_ge(ranks_done, 1)
            order(dve.scalar_tensor_tensor(rank_m, bank[5][:, 0:2 * NE].rearrange("p (t n) -> p t n", t=TT), 1.0, member,
                                           ALU.add, ALU.mult))
            order(dve.tensor_scalar(rank_m, rank_m, -1.0, None, ALU.add))
            order(dve.tensor_copy(rank_b[:, :, 0:NE], rank_m))
            select(slice(0, 1))
            order(dve.tensor_copy(w_b[:, :, 0:NE], comb))
            for b in range(BMAX):
                order(dve.tensor_scalar(rank_c[:, :, b * NE:(b + 1) * NE], rank_m, -float(CAP * (b + 1)), None, ALU.add))
                last = dve.tensor_scalar(flags[:, b * NE:(b + 1) * NE], bank[5][:, 2 * NE:3 * NE], CAP * (b + 1) + 0.5, None, ALU.is_gt)
            signal(last, flags_ready, 1)
            dve.wait_ge(flagsT_done, 1)
            dve.tensor_copy(flagsT[0:NCAND, :], bank[4][0:NCAND, 128:256]).then_inc(flagsT_ready, 1)
            order(dve.tensor_reduce(nover, flags, AX_X, ALU.add))
            dve.wait_ge(prefix_done, 1)
            order(dve.tensor_tensor(sel, bank[4][:, 256:256 + NCAND].unsqueeze(1).to_broadcast([P, NOVER, NCAND]),
                                    k_j8.unsqueeze(2).to_broadcast([P, NOVER, NCAND]), ALU.is_equal))
            order(dve.tensor_tensor(sel, sel, flags.unsqueeze(1).to_broadcast([P, NOVER, NCAND]), ALU.mult))
            for t in range(TT):
                order(dve.tensor_tensor(selx, sel, rank_c[:, t, :].unsqueeze(1).to_broadcast([P, NOVER, NCAND]), ALU.mult))
                order(dve.tensor_reduce(rank_b[:, t, NE:NBLK], selx, AX_X, ALU.add))
                for b in range(BMAX):
                    order(dve.tensor_tensor(selx[:, :, b * NE:(b + 1) * NE], sel[:, :, b * NE:(b + 1) * NE],
                                            comb[:, t, :].unsqueeze(1).to_broadcast([P, NOVER, NE]), ALU.mult))
                order(dve.tensor_reduce(w_b[:, t, NE:NBLK], selx, AX_X, ALU.add))
            order(dve.tensor_tensor(selx, sel, k_ec.unsqueeze(1).to_broadcast([P, NOVER, NCAND]), ALU.mult))
            order(dve.tensor_reduce(eblk, selx, AX_X, ALU.add))
            order(dve.tensor_scalar(meta[:, 0:1], nover, float(NE), None, ALU.add))
            order(dve.tensor_copy(meta[:, 1:2], nover))
            signal(dve.tensor_copy(meta[:, 2:2 + NOVER], eblk), meta_ready, 1)
            def expert_block(i):
                dve.wait_ge(p_ready, i + 1)
                for t in range(TT):
                    last = dve.tensor_scalar(pw[:, t, :, :], p_mat[:, t, :].unsqueeze(1).to_broadcast([P, 2, SLOTS]),
                                             w_b[:, t, bass.ds(i, 1)], None, ALU.mult)
                last.then_inc(pw_ready, 1)
                dve.wait_ge(gather_done, 2 * i + 2)
                dve.wait_ge(pw_ready, i + 1)
                select(bass.ds(i + 1, 1))
                dve.wait_ge(gu_done, i + 1)
                dve.tensor_copy(gu, bank[0][:, :]).then_inc(gu_ready, 1)
                dve.wait_ge(silu_ready, i + 1)
                dve.tensor_tensor(act_sb, silu_sb, bank[1][:, :].rearrange("p (f s) -> p f s", f=KFF)[:, :, SLOTS:2 * SLOTS],
                                  ALU.mult).then_inc(act_ready, 1)
                for n in range(2):
                    for t in range(TT):
                        dve.wait_ge(scat_done, 4 * i + 2 * n + t + 1)
                        for g in range(2):
                            cols = slice((2 * g + n) * CW, (2 * g + n + 1) * CW)
                            last = dve.tensor_tensor(acc_out[:, t, cols], acc_out[:, t, cols], bank[4 + 2 * t + g][:, :], ALU.add)
                        last.then_inc(scat_out[t], 1)
                for t in range(TT):
                    dve.wait_ge(scat_out[t], 2 * i + 3)

            dve.wait_ge(rows_c, 32)
            order(dve.tensor_tensor(rows[2], rows[2], rows[3], ALU.mult))
            with dve.Fori(0, NE) as i:
                expert_block(i)
            further_blocks(dve, expert_block)
            for t in range(TT):
                order(dve.tensor_tensor(gained[t], acc_out[:, t, :], rows[2], ALU.mult))
            for t in range(TT):
                dve.wait_ge(root_out, t + 1)
                order(dve.reciprocal(rstd[:, t:t + 1], rstd[:, t:t + 1]))
                dve.scalar_tensor_tensor(x3[:, t, :], gained[t], rstd[:, t:t + 1], x3[:, t, :], ALU.mult, ALU.add)\
                   .then_inc(out_ready, 1)


_INS = ["x", "c", "w_ada", "b_ada", "g_pre_mix", "g_post_mix", "w_in", "q_norm_g", "k_norm_g", "w_attn_out", "w_fourier_out",
        "w_mix_out", "g_pre_ffn", "g_post_ffn", "w_group_router", "b_group_router", "w_expert_router", "b_expert_router",
        "w_exp_gate", "w_exp_up", "w_exp_down"]


def shape_constants():
    import numpy as np
    grid_w, theta = 64, 10000.0
    pos = np.arange(SEQ)
    n_freq = HD // 4
    inv = theta ** (-np.arange(n_freq) / n_freq)
    row = (pos // grid_w)[:, None] * inv
    col = (pos % grid_w)[:, None] * inv
    ang = np.concatenate([row, row, col, col], axis=-1)
    sign = np.tile(np.repeat([-1.0, 1.0], n_freq), 2)
    w = 2 * np.pi * (np.outer(np.arange(SEQ), np.arange(SEQ)) % SEQ) / SEQ
    row_k = np.zeros(108 + NCAND)
    row_k[0:SLOTS] = np.where(np.arange(SLOTS) < CAP, np.arange(SLOTS), 1e6)
    row_k[64:68] = np.arange(NG) - NG
    row_k[68:100] = np.arange(NE) - NE
    row_k[100:108] = np.arange(NOVER)
    row_k[108:] = np.tile(np.arange(NE), BMAX)
    tables = {
        "k_cos": np.cos(ang), "k_sin": np.sin(ang) * sign,
        "k_dft_tok": np.concatenate([np.cos(w), np.sin(w)], axis=1) / 16,
        "k_dft_ch": np.concatenate([np.cos(w), -np.sin(w)], axis=1) / 16,
        "k_ident": np.eye(P), "k_upper": np.triu(np.ones((P, P)), 1), "k_row": row_k,
    }
    return {k: np.ascontiguousarray(v.astype(np.float32)) for k, v in tables.items()}


def kernel(**inputs):
    import numpy as np
    import concourse.bacc as bacc
    from concourse.bass_utils import run_bass_kernel_spmd

    nc = bacc.Bacc("TRN2", target_bir_lowering=False, num_devices=1)
    arrays, args = {}, []
    for name, a in [(n, inputs[n]) for n in _INS] + list(shape_constants().items()):
        a = np.ascontiguousarray(a)
        arrays[f"in_{name}"] = a
        args.append(nc.dram_tensor(f"in_{name}", a.shape, mybir.dt.from_np(a.dtype), kind="ExternalInput").ap())
    args.append(nc.dram_tensor("out_x", (1, SEQ, D), F32, kind="ExternalOutput").ap())
    build(nc, *args)
    r = run_bass_kernel_spmd(nc, [arrays], core_ids=[0])
    return r.results[0]["out_x"]
```

```python
from contextlib import ExitStack

import concourse.bass as bass
from concourse import mybir

ALU = mybir.AluOpType
ACT = mybir.ActivationFunctionType
F32 = mybir.dt.float32
F32R = mybir.dt.float32r
I32 = mybir.dt.int32
AX_X = mybir.AxisListType.X

P = 128
D = 2048
SEQ = 256
TT = SEQ // P
KD = D // P
CW = 512
ND = D // CW
HD = 128
NH = 16
NKV = 4
HPC = CW // HD
FD = 1024
FG = 256
KF = FD // P
Q_CHUNKS = NH * HD // CW
NE = 32
NG = 4
EG = NE // NG
FF = 512
KFF = FF // P
NR = NG + NE
SLOTS = 64
CAP = 64
BMAX = (SEQ - 1) // CAP
NCAND = BMAX * NE
NOVER = 8
NBLK = NE + NOVER
EPS = 1e-6
SCALE = float(HD) ** -0.5
FAR = 1e37
GU_SLOTS = 4
RING = 6
HK = 8
GK = 2
W_BUFS = HK // GK
GPH = HK // GK
ADA_SLOTS = 4
ADA_K = KD // ADA_SLOTS
N_ADA = 6 * ND


class Order:

    def __init__(self, eng, sem, base=0):
        self.eng, self.sem, self.base, self.n = eng, sem, base, 0

    def __call__(self, ins):
        ins.then_inc(self.sem, 1)
        self.n += 1
        self.eng.wait_ge(self.sem, self.base + self.n)


def build(nc, x, c, w_ada, b_ada, g_pre_mix, g_post_mix, w_in, q_norm_g, k_norm_g, w_attn_out, w_fourier_out,
          w_mix_out, g_pre_ffn, g_post_ffn, w_group_router, b_group_router, w_expert_router, b_expert_router,
          w_exp_gate, w_exp_up, w_exp_down, k_cos, k_sin, k_dft_tok, k_dft_ch, k_ident, k_upper, k_row, out):
    mods_dram = nc.dram_tensor("mods_scratch", (N_ADA, CW), F32, kind="Internal").ap()
    with ExitStack() as ctx:
        def sb(name, n, dt=F32):
            return ctx.enter_context(nc.sbuf_tensor(name, [P, n], dt))

        def sem(name):
            return ctx.enter_context(nc.semaphore(name))

        def sb_twin(name, n):
            with nc.sbuf_tensor(name, [P, n], F32) as plain:
                pass
            return plain, ctx.enter_context(nc.sbuf_tensor(name + "_parts", [P, n], F32R))

        ring = [sb(f"ring{s}", HK * CW) for s in range(2)]
        ring2, w_hi_all = sb_twin("ring2", HK * CW)
        ring3_, w_lo_all = sb_twin("ring3", HK * CW)
        ring += [ring2, ring3_] + [sb(f"ring{s}", HK * CW) for s in range(4, RING)]
        ada_w = sb("ada_w", ADA_SLOTS * ADA_K * CW)
        x_sb, x_parts = sb_twin("x_sb", TT * D)
        r_h, h_parts = sb_twin("r_h", KD * SEQ)
        r_q, q_parts = sb_twin("r_q", KD * SEQ)
        r_kvf, kvf_parts = sb_twin("r_kvf", KD * SEQ)
        gate = sb("gate", TT * CW)
        acc = sb("acc", 2 * CW)
        b_all = sb("b_all", CW)
        ident = sb("ident", P)
        ones = sb("ones", SEQ)
        ones_row = ones[0:1, :]
        cos_t = sb("cos_t", TT * HD)
        sin_t = sb("sin_t", TT * HD)
        small = sb("small", 160)
        meta = sb("meta", 16, I32)
        bank = [ctx.enter_context(nc.psum_tensor(f"bank{b}", [P, CW], F32)) for b in range(8)]

        x3 = x_sb[:, :].rearrange("p (t d) -> p t d", t=TT)
        y1 = r_q[:, :].rearrange("p (t d) -> p t d", t=TT)
        h_tok = r_q[:, :].rearrange("p (t d) -> p t d", t=TT)
        qT = r_q[:, :].rearrange("p (h s) -> p h s", h=NH)
        kT = r_kvf[:, 0:NKV * SEQ].rearrange("p (h s) -> p h s", h=NKV)
        v_sb = r_kvf[:, 1024:2048].rearrange("p (t d) -> p t d", t=TT)
        f_sb = r_kvf[:, 2048:4096].rearrange("p (t d) -> p t d", t=TT)
        fT = r_kvf[:, 2048:4096].rearrange("p (k s) -> p k s", k=KF)
        g_pre = r_kvf[:, 0:D]
        h2T = r_kvf[:, :].rearrange("p (k s) -> p k s", k=KD)
        gate3 = gate[:, :].rearrange("p (t d) -> p t d", t=TT)
        a_row = gate[:, 0:CW]
        accs = [acc[:, j * CW:(j + 1) * CW] for j in range(2)]
        cos3 = cos_t[:, :].rearrange("p (t d) -> p t d", t=TT)
        sin3 = sin_t[:, :].rearrange("p (t d) -> p t d", t=TT)
        ada3 = [ada_w[:, s * ADA_K * CW:(s + 1) * ADA_K * CW].rearrange("p (k n) -> p k n", k=ADA_K)
                for s in range(ADA_SLOTS)]
        rows = [ada_w[:, s * D:(s + 1) * D] for s in range(4)]
        ring3 = [r[:, :].rearrange("p (k n) -> p k n", k=HK) for r in ring]
        raw = ring[4][:, 0:1024].rearrange("p (t n) -> p t n", t=TT)
        qr = ring[4][:, 1024:2048].rearrange("p (t n) -> p t n", t=TT)
        rope_tmp = ring[4][:, 2048:2560]
        rope_junk = ring[4][:, 2560:2560 + CW]
        ab = ring[4][:, :].rearrange("p (i n) -> p i n", i=KF)
        dft_tok = ring[5][:, 0:1024].rearrange("p (t n) -> p t n", t=TT)
        dft_ch = ring[5][:, 1024:2048].rearrange("p (t n) -> p t n", t=TT)
        cosg = [ring[5][:, 2048 + 256 * a:2304 + 256 * a].rearrange("p (t n) -> p t n", t=TT) for a in range(2)]
        sing = [ring[5][:, 2560 + 256 * a:2816 + 256 * a].rearrange("p (t n) -> p t n", t=TT) for a in range(2)]
        g_qk = ring[5][:, 3072:3072 + 2 * HD].rearrange("p (a n) -> p a n", a=2)
        probs = [ring[5][:, 2048 + 512 * b:2560 + 512 * b].rearrange("p (t s) -> p t s", t=TT) for b in range(2)]
        pT = [ring[5][:, 3072 + 512 * b:3584 + 512 * b].rearrange("p (s q) -> p s q", s=TT) for b in range(2)]
        ga_sb = ring[4][:, :].rearrange("p (t d) -> p t d", t=TT)
        mixed = ring[5][:, :].rearrange("p (t d) -> p t d", t=TT)

        def parts(t, k):
            return t.rearrange("p (k s) -> p k s", k=k)
        hT_hi, hT_lo = parts(x_parts[:, :], KD), parts(h_parts[:, :], KD)
        fT_hi, fT_lo = parts(kvf_parts[:, 0:2048], KF), parts(kvf_parts[:, 2048:4096], KF)
        aT_hi, aT_lo = parts(x_parts[:, :], KD), parts(q_parts[:, :], KD)
        mT_hi, mT_lo = parts(h_parts[:, :], KD), parts(kvf_parts[:, :], KD)
        w_hi = [w_hi_all[:, b * GK * CW:(b + 1) * GK * CW].rearrange("p (k n) -> p k n", k=GK) for b in range(W_BUFS)]
        w_lo = [w_lo_all[:, b * GK * CW:(b + 1) * GK * CW].rearrange("p (k n) -> p k n", k=GK) for b in range(W_BUFS)]
        wr = gate[:, 0:KD * NR].rearrange("p (k n) -> p k n", k=KD)
        upper = gate[:, 576:704]
        krow = gate[:, 704:704 + k_row.shape[0]]

        cs = small[:, 0:KD]
        s_col = small[:, 16:32]
        ss = small[:, 32:40]
        rstd = small[:, 40:48]
        mx = small[:, 48:52]
        nmx = small[:, 52:56]
        rs = small[:, 56:60]
        rinv = small[:, 60:64]
        rms_q = small[:, 64:64 + TT * HPC]
        eps = small[:, 72:73]
        junk4 = small[:, 74:74 + TT * ND]
        rb = small[0:1, 96:96 + NR]

        w_ada_v = w_ada.rearrange("(k p) n -> p k n", p=P)
        w_in_v = w_in.rearrange("(k p) n -> p k n", p=P)
        ao_v = w_attn_out.rearrange("(k p) n -> p k n", p=P)
        fo_v = w_fourier_out.rearrange("(k p) n -> p k n", p=P)
        mo_v = w_mix_out.rearrange("(k p) n -> p k n", p=P)
        x_v = x.rearrange("b (t p) d -> p (b t) d", p=P)
        out_v = out.rearrange("b (t p) d -> p (b t) d", p=P)

        def bc_row(v):
            return v.rearrange("(a n) -> a n", a=1).partition_broadcast(P) if len(v.shape) == 1 else v.partition_broadcast(P)

        def row_of(v):
            return v.rearrange("(a n) -> a n", a=1)

        x_ready = sem("x_ready")
        c_ready = sem("c_ready")
        mod_consts = sem("mod_consts")
        rope_consts = sem("rope_consts")
        dft_ready = sem("dft_ready")
        ones_ready = sem("ones_ready")
        silu_c_ready = sem("silu_c_ready")
        ada_ready = [sem(f"ada_ready{s}") for s in range(ADA_SLOTS)]
        ga_ready = sem("ga_ready")
        table_ready = sem("table_ready")
        ada_late = [sem(f"ada_late{s}") for s in range(ADA_SLOTS)]
        ada_free = [sem(f"ada_free{s}") for s in range(ADA_SLOTS)]
        ada_sum_ready = sem("ada_sum_ready")
        ada_reduced = sem("ada_reduced")
        ada_row_out = sem("ada_row_out")
        row_stored = [sem(f"row_stored{s}") for s in range(2)]
        sumsq_ready = sem("sumsq_ready")
        root_x, root_qk, root_y, root_x1, root_out = (sem(f"root_{v}") for v in ("x", "qk", "y", "x1", "out"))
        eps_ready = sem("eps_ready")
        y1_sum = sem("y1_sum")
        h_ready = sem("h_ready")
        tr_done = sem("tr_done")
        tr_out = sem("tr_out")
        slot_ready = [sem(f"slot_ready{s}") for s in range(RING)]
        slot_free = [sem(f"slot_free{s}") for s in range(RING)]
        mm_done = sem("mm_done")
        mm_out = [sem(f"mm_out{s}") for s in range(3)]
        hi_ready = sem("hi_ready")
        lo_ready = sem("lo_ready")
        gran_done = sem("gran_done")
        fT_hi_ready, aT_hi_ready = sem("fT_hi_ready"), sem("aT_hi_ready")
        hT_lo_ready, fT_lo_ready, aT_lo_ready = sem("hT_lo_ready"), sem("fT_lo_ready"), sem("aT_lo_ready")
        mT_lo_ready = sem("mT_lo_ready")
        x_again = sem("x_again")
        rope_done = sem("rope_done")
        score_done = sem("score_done")
        nmx_ready = sem("nmx_ready")
        exp_done = sem("exp_done")
        probs_ready = sem("probs_ready")
        pt_done = sem("pt_done")
        pt_ready = sem("pt_ready")
        pv_done = sem("pv_done")
        attn_ready = sem("attn_ready")
        f1_done = sem("f1_done")
        ab_ready = [sem("ab_ready_act"), sem("ab_ready_dve")]
        f2_done = sem("f2_done")
        fT_ready = [sem("fT_ready_act"), sem("fT_ready_dve")]
        mixed_ready = sem("mixed_ready")
        y1_ready = sem("y1_ready")
        gg1_ready = sem("gg1_ready")
        rows_a = sem("rows_a")
        rows_b = sem("rows_b")
        rows_c = sem("rows_c")
        x1_ready = sem("x1_ready")
        x1_sumsq = sem("x1_sumsq")
        h2_ready = sem("h2_ready")
        route_consts = sem("route_consts")
        logits_done = sem("logits_done")
        logitsT_ready = sem("logitsT_ready")
        gathered = sem("gathered")
        xt_ready = sem("xt_ready")
        shifted_ready = sem("shifted_ready")
        route_exp = sem("route_exp")
        member_ready = sem("member_ready")
        ranks_done = sem("ranks_done")
        flags_ready = sem("flags_ready")
        flagsT_done = sem("flagsT_done")
        flagsT_ready = sem("flagsT_ready")
        prefix_done = sem("prefix_done")
        meta_ready = sem("meta_ready")
        p_ready = sem("p_ready")
        pw_ready = sem("pw_ready")
        gather_done = sem("gather_done")
        xg_ready = sem("xg_ready")
        st_done = sem("st_done")
        s_ready = sem("s_ready")
        gu_done = sem("gu_done")
        gu_ready = sem("gu_ready")
        gut_done = sem("gut_done")
        silu_ready = sem("silu_ready")
        act_ready = sem("act_ready")
        down_done = sem("down_done")
        y_ready = sem("y_ready")
        scat_done = sem("scat_done")
        scat_out = [sem("scat_out_even"), sem("scat_out_odd")]
        acc_sumsq = sem("acc_sumsq")
        out_ready = sem("out_ready")
        out_stored = sem("out_stored")
        o_dve = sem("o_dve")

        halves = []
        granules = []
        pair_of, use_of = [], []

        def chunk(src, n, count, pair, place=True):
            if place:
                for k in range(count):
                    halves.append((src, k * HK, n))
                    for v in range(GPH):
                        granules.append((len(halves) - 1, v * GK, len(pair_of), k == count - 1 and v == GPH - 1))
            use_of.append(pair_of.count(pair))
            pair_of.append(pair)
            return len(pair_of) - 1
        G_IN = [chunk(w_in_v, n, 2, n % 2, place=False) for n in range(2)]
        for k in range(2):
            for n in range(2):
                halves.append((w_in_v, k * HK, n))
        for p in range(ND):
            for n in range(2):
                for v in range(2):
                    granules.append((p // 2 * 2 + n, (p % 2 * 2 + v) * GK, n, p == ND - 1 and v == 1))
        G_IN += [chunk(w_in_v, n, 2, n % 2) for n in range(2, 8)]
        G_GA = [chunk(w_in_v, 8 + n, 2, 2) for n in range(ND)]
        G_GF, G_FO = [], []
        for n in range(ND):
            G_GF.append(chunk(w_in_v, 12 + n, 2, 0))
            G_FO.append(chunk(fo_v, n, 1, 1))
        G_AO = [chunk(ao_v, n, 2, n % 2) for n in range(ND)]
        G_MO = [chunk(mo_v, n, 2, n % 2) for n in range(ND)]
        N_HALVES = len(halves)
        N_GRAN = len(granules)
        MIX_USES = [N_HALVES // 2] * 2 + [0] * 2
        assert N_HALVES % 2 == 0

        def grans(g):
            return [v for v in range(N_GRAN) if granules[v][2] == g]

        def after(g):
            return grans(g)[-1] + 1

        def gran_used(q):
            if granules[q][3]:
                return mm_done, granules[q][2] + 1
            return gran_done, sum(1 for v in range(q + 1) if not granules[v][3])

        def half_split(r):
            return lo_ready, max(v for v in range(N_GRAN) if granules[v][0] == r) + 1

        def out_count(g, t):
            return 2 * use_of[g] + t + 1

        IN_ROWS = {3: [8], 5: [9], 6: [10], 7: [11]}
        N_IN_ROWS = len(IN_ROWS)
        FOURIER_ROW = 12
        HEAD_ROWS = {5: 13, 9: 14, 13: 15, NH: 16}
        FO_ROWS = {0: [17], 1: [18], 2: [19], 3: [20]}
        AO_ROWS = {0: [], 1: [21], 2: [22], 3: [23]}

        def ada_slot_used(j, s):
            early = j < 2 * ND
            if s == (ADA_SLOTS - 2 if early else ADA_SLOTS - 1):
                return ada_sum_ready, j + 1
            return ada_free[s], j + 1 - (2 * ND if s == ADA_SLOTS - 2 else 0)

        def ada_col(j):
            return (j % 2) * D + (j // 2) * CW if j < 2 * ND else j * CW

        def ada_load(eng, j, ready):
            for s in range(ADA_SLOTS):
                if j >= 1:
                    eng.wait_ge(*ada_slot_used(j - 1, s))
                eng.dma_start(ada3[s], w_ada_v[:, s * ADA_K:(s + 1) * ADA_K, ada_col(j):ada_col(j) + CW])\
                   .then_inc(ready[s], 16)

        M_H, M_Q, M_MIX, M_H2 = 0, 2 * ND, 2 * ND + 2 * (Q_CHUNKS + 1), 4 * ND + 2 * (Q_CHUNKS + 1)
        block = ctx.enter_context(nc.Block())

        def further_blocks(eng, body):
            eng.wait_ge(meta_ready, 1)
            n_blk = eng.value_load(meta[0:1, 0:1], min_val=NE, max_val=NBLK - 1)
            with eng.If(n_blk > NE):
                with eng.Fori(NE, n_blk) as i:
                    body(i)
            return n_blk

        @block.sync
        def _(sp):
            def half_load(r):
                src, k0, n = halves[r]
                if r >= 2:
                    sp.wait_ge(*half_split(r - 2))
                sp.dma_start(ring3[r % 2], src[:, k0:k0 + HK, n * CW:(n + 1) * CW]).then_inc(slot_ready[r % 2], 16)

            early_half = {0: 0, 1: 1, 4: 2, 5: 3}
            sp.dma_start(x3, x_v).then_inc(x_ready, 16)
            sp.dma_start(cs, c.rearrange("b (k p) -> p (b k)", p=P), allow_slow_non_contiguous=True).then_inc(c_ready, 16)
            sp.dma_start(ident[:, :], k_ident).then_inc(mod_consts, 16)
            sp.dma_start(b_all[0:N_ADA, :], b_ada.rearrange("(j n) -> j n", n=CW)).then_inc(mod_consts, 16)
            sp.dma_start(g_pre, bc_row(g_pre_mix)).then_inc(mod_consts, 16)
            for j in range(2 * ND):
                ada_load(sp, j, ada_ready)
                if j in early_half:
                    half_load(early_half[j])
            sp.dma_start(cos3, k_cos.rearrange("(t p) d -> p t d", p=P)).then_inc(rope_consts, 16)
            sp.dma_start(sin3, k_sin.rearrange("(t p) d -> p t d", p=P)).then_inc(rope_consts, 16)
            sp.dma_start(g_qk[:, 0, :], bc_row(q_norm_g)).then_inc(rope_consts, 16)
            sp.dma_start(g_qk[:, 1, :], bc_row(k_norm_g)).then_inc(rope_consts, 16)
            for r in range(4, N_HALVES):
                half_load(r)
                if r == granules[grans(G_MO[0])[0]][0] + 2:
                    sp.wait_ge(mm_done, G_AO[-1] + 1)
                    sp.dma_start(x3, x_v).then_inc(x_again, 16)
                if r == 8:
                    sp.dma_start(dft_tok, k_dft_tok.rearrange("(t p) n -> p t n", p=P)).then_inc(dft_ready, 16)
                    sp.dma_start(dft_ch, k_dft_ch.rearrange("(t p) n -> p t n", p=P)).then_inc(dft_ready, 16)

            def expert_load(e, i):
                for s in range(RING) if i is not None else (0, 1, 4, 5, 2, 3):
                    if i is None:
                        if s < 2:
                            sp.wait_ge(lo_ready, N_GRAN - GPH * (1 - s))
                        elif s < GU_SLOTS:
                            sp.wait_ge(mm_done, G_MO[-1] + 1)
                        elif s == GU_SLOTS:
                            sp.wait_ge(tr_done, M_H2)
                    elif s < 2:
                        sp.wait_ge(slot_free[s], i)
                    elif s < GU_SLOTS:
                        sp.wait_ge(gu_done, i)
                    else:
                        sp.wait_ge(down_done, 2 * i + s - GU_SLOTS - 1)
                    if s < GU_SLOTS:
                        src = (w_exp_gate, w_exp_up)[s % 2]
                        half = s // 2
                        sp.dma_start(ring3[s], src[e, half * HK * P:(half + 1) * HK * P, :]
                                     .rearrange("(k p) n -> p k n", p=P)).then_inc(slot_ready[s], 16)
                    else:
                        n = s - GU_SLOTS
                        for g in range(2):
                            sp.dma_start(ring3[s][:, g * KFF:(g + 1) * KFF, :],
                                         w_exp_down[e, :, (2 * g + n) * CW:(2 * g + n + 1) * CW]
                                         .rearrange("(k p) n -> p k n", p=P)).then_inc(slot_ready[s], 16)

            expert_load(0, None)
            with sp.Fori(1, NE) as i:
                expert_load(i, i)
            sp.wait_ge(meta_ready, 1)
            n_over = sp.value_load(meta[0:1, 1:2], min_val=0, max_val=NOVER - 1)
            with sp.If(n_over > 0):
                with sp.Fori(0, n_over) as j:
                    e = sp.value_load(meta[0:1, bass.ds(j + 2, 1)], min_val=0, max_val=NE - 1)
                    expert_load(e, j + NE)
            sp.wait_ge(out_stored, 64)

        @block.gpsimd
        def _(pool):
            pool.memset(ones[:, :], 1.0).then_inc(ones_ready, 1)
            pool.memset(eps, EPS).then_inc(eps_ready, 1)
            pool.wait_ge(slot_ready[1], 32)
            for j in range(2 * ND, N_ADA):
                ada_load(pool, j, ada_late)
            pool.wait_ge(ada_sum_ready, N_ADA)
            for s in range(2):
                pool.wait_ge(row_stored[s], 16 * (N_ADA - 2 * ND) // 2)

            def mod_row(m):
                return mods_dram[m * ND:(m + 1) * ND, :].rearrange("(a j) n -> a (j n)", a=1)
            pool.dma_start(rows[0], bc_row(mod_row(2))).then_inc(rows_a, 16)
            pool.dma_start(rows[1], bc_row(g_post_mix)).then_inc(rows_a, 16)
            pool.dma_start(rows[2], bc_row(mod_row(4))).then_inc(rows_a, 16)
            pool.dma_start(rows[3], bc_row(g_pre_ffn)).then_inc(rows_a, 16)
            pool.wait_ge(gg1_ready, 1)
            pool.dma_start(rows[1], bc_row(mod_row(3))).then_inc(rows_b, 16)
            pool.wait_ge(mixed_ready, 2 * ND)
            pool.dma_start(wr[:, :, 0:NG], w_group_router.rearrange("(k p) n -> p k n", p=P)).then_inc(route_consts, 16)
            pool.dma_start(wr[:, :, NG:NR], w_expert_router.rearrange("(k p) n -> p k n", p=P)).then_inc(route_consts, 16)
            pool.dma_start(rb[:, 0:NG], row_of(b_group_router)).then_inc(route_consts, 16)
            pool.dma_start(rb[:, NG:NR], row_of(b_expert_router)).then_inc(route_consts, 16)
            pool.dma_start(upper, k_upper).then_inc(route_consts, 16)
            pool.dma_start(krow, bc_row(k_row)).then_inc(route_consts, 16)
            pool.wait_ge(h2_ready, TT * ND)
            pool.dma_start(rows[2], bc_row(mod_row(5))).then_inc(rows_c, 16)
            pool.dma_start(rows[3], bc_row(g_post_ffn)).then_inc(rows_c, 16)

        acc_out = y1
        h2 = r_h[:, :].rearrange("p (t d) -> p t d", t=TT)
        gained = [ring[t][:, 0:D] for t in range(TT)]
        o = [0]

        def take(n):
            o[0] += n
            return r_kvf[:, o[0] - n:o[0]]
        xg_flat = take(KD * SLOTS)
        xg = xg_flat.rearrange("p (k s) -> p k s", k=KD)
        xg4 = xg_flat.rearrange("p (g k s) -> p g k s", g=2, k=HK)
        y_sb = take(2 * CW).rearrange("p (n c) -> p n c", n=2)
        gu = take(FF)
        act_sb = take(KFF * SLOTS).rearrange("p (f s) -> p f s", f=KFF)
        silu_sb = take(KFF * SLOTS).rearrange("p (f s) -> p f s", f=KFF)
        s_mat = take(SEQ)
        p_mat = take(TT * SLOTS).rearrange("p (t s) -> p t s", t=TT)
        pw = take(TT * 2 * SLOTS).rearrange("p (t g s) -> p t g s", t=TT, g=2)
        o[0] = 0

        def tmp(n, *dims):
            o[0] += n
            return ada_w[:, o[0] - n:o[0]]
        logitsT = tmp(SEQ)
        lg = tmp(TT * NR).rearrange("p (t n) -> p t n", t=TT)
        gm = tmp(TT)
        ga = tmp(TT * NG).rearrange("p (t n) -> p t n", t=TT)
        oh_g = tmp(TT * NG).rearrange("p (t n) -> p t n", t=TT)
        gsh = tmp(TT * NG).rearrange("p (t n) -> p t n", t=TT)
        gex = tmp(TT * NG).rearrange("p (t n) -> p t n", t=TT)
        gmin = tmp(TT)
        elm = tmp(TT * NE).rearrange("p (t n) -> p t n", t=TT)
        e_tmp = tmp(TT * NE).rearrange("p (t n) -> p t n", t=TT)
        oh1 = tmp(TT * NE).rearrange("p (t n) -> p t n", t=TT)
        oh2 = tmp(TT * NE).rearrange("p (t n) -> p t n", t=TT)
        member = tmp(TT * NE).rearrange("p (t n) -> p t n", t=TT)
        comb = tmp(TT * NE).rearrange("p (t n) -> p t n", t=TT)
        rank_m = tmp(TT * NE).rearrange("p (t n) -> p t n", t=TT)
        m1, m2, i1, gw, de, w1, w2 = (tmp(TT) for _ in range(7))
        flags = tmp(NCAND)
        flagsT = tmp(P)
        rank_c = tmp(TT * NCAND).rearrange("p (t n) -> p t n", t=TT)
        sel = tmp(NOVER * NCAND).rearrange("p (j n) -> p j n", j=NOVER)
        selx = tmp(NOVER * NCAND).rearrange("p (j n) -> p j n", j=NOVER)
        eblk = tmp(NOVER)
        nover = tmp(1)
        xt_sb = tmp(2 * CW).rearrange("p (n c) -> p n c", n=2)
        rank_b = tmp(TT * NBLK).rearrange("p (t n) -> p t n", t=TT)
        w_b = tmp(TT * NBLK).rearrange("p (t n) -> p t n", t=TT)
        assert o[0] <= 2 * D, o[0]
        k_slot = krow[:, 0:SLOTS]
        k_g4 = krow[:, 64:68]
        k_e32 = krow[:, 68:100]
        k_j8 = krow[:, 100:108]
        k_ec = krow[:, 108:108 + NCAND]

        @block.tensor
        def _(pe):
            def split_steps(g, hi, lo):
                pair, use = pair_of[g], use_of[g]
                if use:
                    pe.wait_ge(mm_out[pair], 2 * use)
                mine = grans(g)
                for i, q in enumerate(mine):
                    pe.wait_ge(lo_ready, q + 1)
                    wh, wl = w_hi[q % W_BUFS], w_lo[q % W_BUFS]
                    for k in range(GK):
                        kk = i * GK + k
                        end = q == mine[-1] and k == GK - 1
                        for t in range(TT):
                            cols = slice(t * P, (t + 1) * P)
                            b = bank[2 * pair + t][:, :]
                            pe.matmul(b, hi[:, kk, cols], wh[:, k, :], start=(kk == 0), stop=False)
                            pe.matmul(b, hi[:, kk, cols], wl[:, k, :], start=False, stop=False)
                            last = pe.matmul(b, lo[:, kk, cols], wh[:, k, :], start=False, stop=end)
                        if k == GK - 1:
                            last.then_inc(mm_done if end else gran_done, 1)
                        yield

            def split_gemm(g, hi, lo):
                for _ in split_steps(g, hi, lo):
                    pass

            def transposes(m, src, ready, value):
                pe.wait_ge(ready, value)
                if m >= 2:
                    pe.wait_ge(tr_out, m - 1)
                if 2 <= m < M_Q + 2:
                    pe.wait_ge(hT_lo_ready, m - 1)
                if M_MIX + 2 <= m < M_H2 + 2:
                    pe.wait_ge(mT_lo_ready, m - M_MIX - 1)
                for b in range(4):
                    last = pe.transpose(bank[6 + m % 2][:, b * P:(b + 1) * P], src[:, b * P:(b + 1) * P], ident[:, :])
                last.then_inc(tr_done, 1)

            def reduce_row(j):
                pe.wait_ge(ada_sum_ready, j + 1)
                if j < 2 * ND + 2:
                    pe.wait_ge(h_ready, 2 * ND)
                elif j in (17, 18):
                    pe.wait_ge(mm_out[2], 2 * ND)
                else:
                    pe.wait_ge(ada_row_out, j - 2 * ND - 1)
                b = bank[4 + j % 2]
                cc = ada_col(j) // CW
                pe.matmul(b[0:1, :], ones[:, 0:1], accs[j % 2], start=True, stop=False)
                pe.matmul(b[0:1, :], ident[0:N_ADA, cc:cc + 1], b_all[0:N_ADA, :], start=False, stop=True)\
                  .then_inc(ada_reduced, 1)

            def reduce_row_halves(j):
                pe.wait_ge(ada_sum_ready, j + 1)
                pe.wait_ge(ada_row_out, j - 2 * ND)
                cc = ada_col(j) // CW
                for b in range(2):
                    dst, cols = bank[6 + b][0:1, SEQ:2 * SEQ], slice(b * SEQ, (b + 1) * SEQ)
                    pe.matmul(dst, ones[:, 0:1], accs[j % 2][:, cols], start=True, stop=False)
                    last = pe.matmul(dst, ident[0:N_ADA, cc:cc + 1], b_all[0:N_ADA, cols], start=False, stop=True)
                last.then_inc(ada_reduced, 1)

            pe.wait_ge(ones_ready, 1)
            pe.wait_ge(mod_consts, 48)
            pe.wait_ge(silu_c_ready, 1)
            first = [split_steps(G_IN[a], hT_hi, hT_lo) for a in range(2)]
            for n in range(ND):
                for a in range(2):
                    if n:
                        if a == 0:
                            pe.wait_ge(hT_lo_ready, 2 * n)
                        for _ in range(CW // P):
                            next(first[a])
                    j = 2 * n + a
                    if n:
                        pe.wait_ge(h_ready, 2 * n)
                    b = bank[4 + a]
                    cc = ada_col(j) // CW
                    pe.matmul(b[:, :], ident[0:N_ADA, cc:cc + 1].to_broadcast([N_ADA, P]), b_all[0:N_ADA, :],
                              start=True, stop=False)
                    pe.wait_ge(ada_ready[ADA_SLOTS - 1], 16 * (j + 1))
                    for k in range(ADA_K):
                        kk = (ADA_SLOTS - 1) * ADA_K + k
                        last = pe.matmul(b[:, :], s_col[:, kk:kk + 1].to_broadcast([P, P]), ada3[ADA_SLOTS - 1][:, k, :],
                                         start=False, stop=False)
                    last.then_inc(ada_free[ADA_SLOTS - 1], 1)
                    pe.wait_ge(ada_sum_ready, j + 1)
                    pe.matmul(b[:, :], ones[:, 0:P], accs[a], start=False, stop=True).then_inc(ada_reduced, 1)
                for t in range(TT):
                    transposes(M_H + 2 * n + t, h_tok[:, t, n * CW:(n + 1) * CW], h_ready, 2 * n + t + 1)
            pe.wait_ge(hT_lo_ready, M_Q)
            for g in G_IN:
                if g < 2:
                    for _ in first[g]:
                        pass
                else:
                    split_gemm(g, hT_hi, hT_lo)
                for j in IN_ROWS.get(g, []):
                    reduce_row(j)
                if 1 <= g <= Q_CHUNKS + 1:
                    for t in range(TT):
                        transposes(M_Q + 2 * (g - 1) + t, qr[:, t, :], rope_done, 2 * (g - 1) + t + 1)
            for pair in range(2):
                pe.wait_ge(mm_out[pair], 8)

            pe.wait_ge(dft_ready, 32)
            for i in range(KF):
                if i >= 4:
                    pe.wait_ge(ab_ready[i % 2], (i - 4) // 2 + 1)
                for t in range(TT):
                    last = pe.matmul(bank[i % 4][:, :], f_sb[:, t, i * P:(i + 1) * P], dft_tok[:, t, :],
                                     start=(t == 0), stop=(t == TT - 1))
                last.then_inc(f1_done, 1)
            reduce_row(FOURIER_ROW)
            for i in range(KF):
                grp, cc = i // 2, i % 2
                for a in range(2):
                    pe.wait_ge(ab_ready[a], i // 2 + 1)
                if i < 4:
                    pe.wait_ge(ab_ready[i % 2], (i + 4) // 2 + 1)
                else:
                    pe.wait_ge(fT_ready[i % 2], (i - 4) // 2 + 1)
                for kc in range(2):
                    for part in range(2):
                        last = pe.matmul(bank[i % 4][:, 0:SEQ], dft_ch[:, kc, part * FG + cc * P:part * FG + (cc + 1) * P],
                                         ab[:, 2 * grp + kc, part * SEQ:(part + 1) * SEQ],
                                         start=(kc == 0 and part == 0), stop=(kc == 1 and part == 1))
                last.then_inc(f2_done, 1)

            pe.wait_ge(tr_out, M_MIX)
            for a in range(2):
                pe.wait_ge(fT_ready[a], KF // 2)

            def scores(h):
                if h >= 2:
                    pe.wait_ge(exp_done, 2 * (h - 1))
                for t in range(TT):
                    last = pe.matmul(bank[h % 2][:, t * SEQ:(t + 1) * SEQ], qT[:, h, t * P:(t + 1) * P], kT[:, h // 4, :],
                                     start=True, stop=True)
                last.then_inc(score_done, 1)

            def probs_t(h):
                pe.wait_ge(probs_ready, h + 1)
                if h >= 2:
                    pe.wait_ge(pt_ready, h - 1)
                for s in range(TT):
                    for t in range(TT):
                        last = pe.transpose(bank[2 + h % 2][:, s * SEQ + t * P:s * SEQ + (t + 1) * P],
                                            probs[h % 2][:, t, s * P:(s + 1) * P], ident[:, :])
                last.then_inc(pt_done, 1)

            def pv(h):
                pe.wait_ge(pt_ready, h + 1)
                if h >= 2:
                    pe.wait_ge(attn_ready, h - 1)
                for s in range(TT):
                    last = pe.matmul(bank[6 + h % 2][:, 0:SEQ], v_sb[:, s, (h // 4) * HD:(h // 4 + 1) * HD], pT[h % 2][:, s, :],
                                     start=(s == 0), stop=(s == TT - 1))
                last.then_inc(pv_done, 1)

            def gate_steps():
                pe.wait_ge(ada_row_out, N_IN_ROWS + 1)
                for g in G_GA:
                    yield from split_steps(g, hT_hi, hT_lo)
            gates = gate_steps()

            def fill(count):
                for _ in range(count):
                    next(gates, None)

            scores(0)
            for h in range(NH):
                if h + 1 < NH:
                    scores(h + 1)
                fill(2)
                probs_t(h)
                if h in HEAD_ROWS:
                    pe.wait_ge(attn_ready, h - 1)
                    reduce_row_halves(HEAD_ROWS[h])
                fill(1)
                if h in HEAD_ROWS:
                    pe.wait_ge(ada_row_out, HEAD_ROWS[h] - 2 * ND + 1)
                if h >= 1:
                    pv(h - 1)
                fill(1)
            pv(NH - 1)
            fill(1)
            pe.wait_ge(attn_ready, NH)
            reduce_row_halves(HEAD_ROWS[NH])

            for n in range(ND):
                split_gemm(G_GF[n], hT_hi, hT_lo)
                if n == 0:
                    pe.wait_ge(fT_lo_ready, 1)
                split_gemm(G_FO[n], fT_hi, fT_lo)
                for j in FO_ROWS[n]:
                    reduce_row(j)
            pe.wait_ge(aT_lo_ready, 2)
            for n in range(ND):
                split_gemm(G_AO[n], aT_hi, aT_lo)
                for j in AO_ROWS[n]:
                    reduce_row(j)
                if n:
                    for t in range(TT):
                        transposes(M_MIX + 2 * (n - 1) + t, mixed[:, t, (n - 1) * CW:n * CW], mixed_ready, 2 * (n - 1) + t + 1)
            steps = split_steps(G_MO[0], mT_hi, mT_lo)
            pe.wait_ge(mT_lo_ready, 2 * (ND - 1))
            for _ in range((ND - 1) * CW // P):
                next(steps)
            for t in range(TT):
                transposes(M_MIX + 2 * (ND - 1) + t, mixed[:, t, (ND - 1) * CW:D], mixed_ready, 2 * (ND - 1) + t + 1)
            pe.wait_ge(mT_lo_ready, 2 * ND)
            for _ in steps:
                pass
            for g in G_MO[1:]:
                split_gemm(g, mT_hi, mT_lo)

            def gather():
                for n in range(2):
                    for t in range(TT):
                        for g in range(2):
                            last = pe.matmul(bank[2 + n][g * SLOTS:(g + 1) * SLOTS, :], p_mat[:, t, :],
                                             h2[:, t, (2 * g + n) * CW:(2 * g + n + 1) * CW], start=(t == 0), stop=(t == TT - 1),
                                             skip_group_check=True)
                    last.then_inc(gather_done, 1)

            def gather_t():
                for n in range(2):
                    for b in range(4):
                        last = pe.transpose(bank[6 + n][:, b * P:(b + 1) * P], xt_sb[:, n, b * P:(b + 1) * P], ident[:, :])
                    last.then_inc(gathered, 1)

            pe.wait_ge(ada_row_out, N_ADA - 2 * ND)
            for t in range(TT):
                for n in range(ND + 1):
                    if n < ND:
                        transposes(M_H2 + t * ND + n, h2[:, t, n * CW:(n + 1) * CW], h2_ready, t * ND + n + 1)
                    if t == 0 and n == 1:
                        pe.wait_ge(route_consts, 96)
                    if n:
                        pe.wait_ge(tr_out, M_H2 + t * ND + n)
                        for k in range(4 * n - 4, 4 * n):
                            pe.matmul(bank[4][0:NR, t * P:(t + 1) * P], wr[:, k, :], h2T[:, k, t * P:(t + 1) * P],
                                      start=(k == 0), stop=False)
                last = pe.matmul(bank[4][0:NR, t * P:(t + 1) * P], rb, ones_row[:, 0:P], start=False, stop=True)
            last.then_inc(logits_done, 1)
            pe.wait_ge(logitsT_ready, 1)
            for t in range(TT):
                last = pe.transpose(bank[5][:, 128 * (t + 2):128 * (t + 2) + NR], logitsT[0:NR, t * P:(t + 1) * P], ident[0:NR, 0:NR])
            last.then_inc(logits_done, 1)
            pe.wait_ge(member_ready, 1)
            pe.matmul(bank[5][:, 0:NE], upper, member[:, 0, :], start=True, stop=True)
            pe.matmul(bank[5][:, NE:2 * NE], ones[:, 0:P], member[:, 0, :], start=True, stop=False)
            pe.matmul(bank[5][:, NE:2 * NE], upper, member[:, 1, :], start=False, stop=True)
            pe.matmul(bank[5][:, 2 * NE:3 * NE], ones[:, 0:P], member[:, 0, :], start=True, stop=False)
            pe.matmul(bank[5][:, 2 * NE:3 * NE], ones[:, 0:P], member[:, 1, :], start=False, stop=True).then_inc(ranks_done, 1)
            pe.wait_ge(p_ready, 1)
            gather()
            pe.wait_ge(flags_ready, 1)
            pe.transpose(bank[4][0:NCAND, 128:256], flags, ident[:, :]).then_inc(flagsT_done, 1)
            pe.wait_ge(flagsT_ready, 1)
            pe.matmul(bank[4][:, 256:256 + NCAND], flagsT[0:NCAND, :], upper[0:NCAND, 0:NCAND], start=True, stop=True)\
              .then_inc(prefix_done, 1)

            def expert_block(i):
                pe.wait_ge(xg_ready, 2 * i + 2)
                for half in range(2):
                    for a in range(2):
                        pe.wait_ge(slot_ready[2 * half + a], 16 * (i + 1 + MIX_USES[2 * half + a]))
                    for k in range(HK):
                        kk = half * HK + k
                        for a in range(2):
                            last = pe.matmul(bank[0][a * SLOTS:(a + 1) * SLOTS, :], xg[:, kk, :], ring3[2 * half + a][:, k, :],
                                             start=(kk == 0), stop=(kk == KD - 1), skip_group_check=True)
                            if kk == HK - 1:
                                last.then_inc(slot_free[a], 1)
                last.then_inc(gu_done, 1)
                pe.wait_ge(p_ready, i + 2)
                gather()
                pe.wait_ge(pw_ready, i + 1)
                pe.wait_ge(scat_out[0], 2 * i + 1)
                for t in range(TT):
                    last = pe.transpose(bank[4][:, t * P:(t + 1) * P], pw[:, t, :, :].rearrange("p g s -> p (g s)"), ident[:, :])
                last.then_inc(st_done, 1)
                pe.wait_ge(gu_ready, i + 1)
                for f in range(KFF):
                    last = pe.transpose(bank[1][:, f * P:(f + 1) * P], gu[:, f * P:(f + 1) * P], ident[:, :])
                last.then_inc(gut_done, 1)
                pe.wait_ge(xt_ready, 2 * i + 4)
                pe.wait_ge(scat_out[1], 2 * i + 1)
                gather_t()
                pe.wait_ge(act_ready, i + 1)
                for n in range(2):
                    pe.wait_ge(slot_ready[GU_SLOTS + n], 32 * (i + 1))
                    for f in range(KFF):
                        for g in range(2):
                            last = pe.matmul(bank[2 + n][g * SLOTS:(g + 1) * SLOTS, :], act_sb[:, f, :],
                                             ring3[GU_SLOTS + n][:, g * KFF + f, :], start=(f == 0), stop=(f == KFF - 1),
                                             skip_group_check=True)
                    last.then_inc(down_done, 1)
                pe.wait_ge(s_ready, i + 1)
                pe.wait_ge(xg_ready, 2 * i + 4)
                for n in range(2):
                    pe.wait_ge(y_ready, 2 * i + n + 1)
                    for t in range(TT):
                        if n:
                            pe.wait_ge(scat_out[t], 2 * i + 2)
                        for g in range(2):
                            last = pe.matmul(bank[4 + 2 * t + g][:, :], s_mat[g * SLOTS:(g + 1) * SLOTS, t * P:(t + 1) * P],
                                             y_sb[g * SLOTS:(g + 1) * SLOTS, n, :], start=True, stop=True)
                        last.then_inc(scat_done, 1)

            pe.wait_ge(xt_ready, 2)
            gather_t()
            with pe.Fori(0, NE) as i:
                expert_block(i)
            further_blocks(pe, expert_block)

        @block.scalar
        def _(act):
            act.wait_ge(c_ready, 16)
            act.activation(s_col, cs, ACT.Silu).then_inc(silu_c_ready, 1)
            act.wait_ge(x_ready, 16)
            for t in range(TT):
                act.activation(h_tok[:, t, :], x3[:, t, :], ACT.Square, accum_out=ss[:, t:t + 1]).then_inc(sumsq_ready, 1)

            def root(dst, src, count, signal):
                act.activation(dst, src, ACT.Sqrt, bias=eps, scale=1.0 / count).then_inc(signal, 1)

            act.wait_ge(eps_ready, 1)
            act.wait_ge(sumsq_ready, TT)
            root(rstd[:, 0:TT], ss[:, 0:TT], D, root_x)

            def tr_copy(m, dst):
                act.wait_ge(tr_done, m + 1)
                act.activation(dst, bank[6 + m % 2][:, :].rearrange("p (b s) -> p b s", b=4), ACT.Copy).then_inc(tr_out, 1)

            def store_row(j):
                act.wait_ge(ada_reduced, j + 1)
                act.activation(accs[j % 2][0:1, :], bank[4 + j % 2][0:1, :], ACT.Copy).then_inc(ada_row_out, 1)
                act.wait_ge(ada_row_out, j - 2 * ND + 1)
                act.dma_start(mods_dram[j:j + 1, :], accs[j % 2][0:1, :]).then_inc(row_stored[j % 2], 16)

            splits = [0]
            ahead = W_BUFS - 1

            def split_upto(q):
                while splits[0] < min(q, N_GRAN):
                    v = splits[0]
                    r, k = granules[v][:2]
                    act.wait_ge(slot_ready[r % 2], 16 * (r // 2 + 1))
                    if v >= W_BUFS:
                        act.wait_ge(*gran_used(v - W_BUFS))
                    act.activation(w_hi[v % W_BUFS], ring3[r % 2][:, k:k + GK, :], ACT.Copy).then_inc(hi_ready, 1)
                    splits[0] += 1

            def store_row_halves(j):
                act.wait_ge(ada_reduced, j + 1)
                for b in range(2):
                    last = act.activation(accs[j % 2][0:1, b * SEQ:(b + 1) * SEQ], bank[6 + b][0:1, SEQ:2 * SEQ], ACT.Copy)
                last.then_inc(ada_row_out, 1)
                act.wait_ge(ada_row_out, j - 2 * ND + 1)
                act.dma_start(mods_dram[j:j + 1, :], accs[j % 2][0:1, :]).then_inc(row_stored[j % 2], 16)

            for n in range(ND):
                for t in range(TT):
                    tr_copy(M_H + 2 * n + t, hT_hi[:, 4 * n:4 * n + 4, t * P:(t + 1) * P])
                split_upto(W_BUFS * (n + 1))
            for g in range(8):
                split_upto(after(g) + ahead)
                act.wait_ge(mm_done, g + 1)
                pair = pair_of[g]
                for t in range(TT):
                    src = bank[2 * pair + t][:, :]
                    if g <= Q_CHUNKS:
                        if g:
                            act.wait_ge(rope_done, 2 * (g - 1) + t + 1)
                        for hh in range(HPC):
                            act.activation(rope_junk[:, hh * HD:(hh + 1) * HD], src[:, hh * HD:(hh + 1) * HD], ACT.Square,
                                           accum_out=rms_q[:, t * HPC + hh:t * HPC + hh + 1])
                        dst = raw[:, t, :]
                    else:
                        dst = v_sb[:, t, :] if g == Q_CHUNKS + 1 else f_sb[:, t, (g - Q_CHUNKS - 2) * CW:(g - Q_CHUNKS - 1) * CW]
                    act.activation(dst, src, ACT.Copy).then_inc(mm_out[pair], 1)
                    if g <= Q_CHUNKS:
                        act.wait_ge(mm_out[pair], out_count(g, t))
                        rq = rms_q[:, t * HPC:(t + 1) * HPC]
                        root(rq, rq, HD, root_qk)
                for j in IN_ROWS.get(g, []):
                    store_row(j)
                if 1 <= g <= Q_CHUNKS + 1:
                    for t in range(TT):
                        dst = qT[:, 4 * (g - 1):4 * g, t * P:(t + 1) * P] if g <= Q_CHUNKS else kT[:, :, t * P:(t + 1) * P]
                        tr_copy(M_Q + 2 * (g - 1) + t, dst)

            def attn_copy(h):
                act.wait_ge(pv_done, h + 1)
                act.activation(qT[:, h, :], bank[6 + h % 2][:, 0:SEQ], ACT.Copy).then_inc(attn_ready, 1)

            for i in range(0, KF, 2):
                act.wait_ge(f1_done, i + 1)
                act.activation(ab[:, i, :], bank[i % 4][:, :], ACT.Copy).then_inc(ab_ready[0], 1)
            store_row(FOURIER_ROW)
            for i in range(0, KF, 2):
                act.wait_ge(f2_done, i + 1)
                act.activation(fT[:, i, :], bank[i % 4][:, 0:SEQ], ACT.Copy).then_inc(fT_ready[0], 1)

            def gate_copy(n):
                act.wait_ge(mm_done, G_GA[n] + 1)
                for t in range(TT):
                    act.activation(ga_sb[:, t, n * CW:(n + 1) * CW], bank[4 + t][:, :], ACT.Copy).then_inc(mm_out[2], 1)

            for h in range(NH):
                if h % 4 == 0 and h:
                    gate_copy(h // 4 - 1)
                act.wait_ge(nmx_ready, h + 1)
                if h >= 2:
                    act.wait_ge(pt_done, h - 1)
                for t in range(TT):
                    b = 2 * (h % 2) + t
                    act.activation(probs[h % 2][:, t, :], bank[h % 2][:, t * SEQ:(t + 1) * SEQ], ACT.Exp,
                                   bias=nmx[:, b:b + 1], scale=SCALE, accum_out=rs[:, b:b + 1]).then_inc(exp_done, 1)
                split_upto(grans(G_GA[0])[0] + 2 * h + 4)
                if h >= 2:
                    attn_copy(h - 2)
                if h in HEAD_ROWS:
                    store_row_halves(HEAD_ROWS[h])
            attn_copy(NH - 2)
            attn_copy(NH - 1)
            gate_copy(ND - 1)

            split_upto(after(G_GA[-1]) + ahead)
            act.activation(fT_hi, fT, ACT.Copy).then_inc(fT_hi_ready, 1)
            store_row_halves(HEAD_ROWS[NH])
            act.wait_ge(mm_out[2], 2 * ND)
            for n in range(ND):
                for t in range(TT):
                    v = ga_sb[:, t, n * CW:(n + 1) * CW]
                    act.activation(v, v, ACT.Sigmoid).then_inc(ga_ready, 1)
            for n in range(ND):
                split_upto(after(G_GF[n]) + ahead)
                act.wait_ge(mm_done, G_GF[n] + 1)
                for t in range(TT):
                    if n:
                        act.wait_ge(mm_out[1], out_count(G_FO[n - 1], t))
                    act.activation(gate3[:, t, :], bank[t][:, :], ACT.Sigmoid).then_inc(mm_out[0], 1)
                if n == ND - 1:
                    for p in range(2):
                        act.activation(aT_hi[:, 8 * p:8 * p + 8, :], qT[:, 8 * p:8 * p + 8, :], ACT.Copy).then_inc(aT_hi_ready, 1)
                split_upto(after(G_FO[n]) + ahead)
                for j in FO_ROWS[n]:
                    store_row(j)

            def mixed_copy(n):
                for t in range(TT):
                    tr_copy(M_MIX + 2 * n + t, mT_hi[:, 4 * n:4 * n + 4, t * P:(t + 1) * P])

            for n in range(ND):
                split_upto(after(G_AO[n]) + ahead)
                for j in AO_ROWS[n]:
                    store_row(j)
                if n:
                    mixed_copy(n - 1)
            split_upto(after(G_MO[0]))
            mixed_copy(ND - 1)
            root(junk4[:, 0:1], eps, 1, table_ready)
            for n in range(ND):
                split_upto(after(G_MO[n]) + ahead)
                act.wait_ge(mm_done, G_MO[n] + 1)
                for t in range(TT):
                    b = bank[2 * (n % 2) + t][:, :]
                    y = y1[:, t, n * CW:(n + 1) * CW]
                    act.activation(y, b, ACT.Copy).then_inc(mm_out[n % 2], 1)
                    act.wait_ge(mm_out[n % 2], out_count(G_MO[n], t))
                    act.activation(bank[6 + t][:, :], y, ACT.Square, accum_out=ss[:, t * ND + n:t * ND + n + 1]).then_inc(y1_ready, 1)
            act.wait_ge(y1_ready, 2 * ND)
            for t in range(TT):
                act.activation(junk4[:, t * ND:(t + 1) * ND], ss[:, t * ND:(t + 1) * ND], ACT.Copy, accum_out=rs[:, t:t + 1]).then_inc(y1_sum, 1)
            act.wait_ge(y1_sum, TT)
            root(rstd[:, 0:TT], rs[:, 0:TT], D, root_y)
            for t in range(TT):
                act.wait_ge(x1_ready, t + 1)
                act.activation(y1[:, t, :], x3[:, t, :], ACT.Square, accum_out=rs[:, t:t + 1]).then_inc(x1_sumsq, 1)
                act.wait_ge(x1_sumsq, t + 1)
                root(rinv[:, t:t + 1], rs[:, t:t + 1], D, root_x1)
            for t in range(TT):
                for n in range(ND):
                    tr_copy(M_H2 + t * ND + n, h2T[:, 4 * n:4 * n + 4, t * P:(t + 1) * P])
            act.wait_ge(shifted_ready, 1)
            act.activation(gex, gsh, ACT.Exp).then_inc(route_exp, 1)
            act.wait_ge(shifted_ready, 2)
            act.activation(w2, de, ACT.Exp).then_inc(route_exp, 1)

            act.wait_ge(route_exp, 2)
            act.activation(junk4[:, 1:2], eps, ACT.Silu).then_inc(table_ready, 1)

            def gather_copy(v):
                for n in range(2):
                    act.wait_ge(gather_done, 2 * v + n + 1)
                    act.activation(xt_sb[:, n, :], bank[2 + n][:, :], ACT.Copy).then_inc(xt_ready, 1)

            def gather_t_copy(v):
                for n in range(2):
                    act.wait_ge(gathered, 2 * v + n + 1)
                    act.activation(xg4[:, :, 4 * n:4 * n + 4, :], bank[6 + n][:, :].rearrange("p (k g s) -> p g k s", g=2, s=SLOTS),
                                   ACT.Copy).then_inc(xg_ready, 1)

            def expert_block(i):
                gather_copy(i + 1)
                act.wait_ge(st_done, i + 1)
                act.activation(s_mat, bank[4][:, 0:SEQ], ACT.Copy).then_inc(s_ready, 1)
                act.wait_ge(gut_done, i + 1)
                act.activation(silu_sb, bank[1][:, :].rearrange("p (f s) -> p f s", f=KFF)[:, :, 0:SLOTS], ACT.Silu)\
                   .then_inc(silu_ready, 1)
                gather_t_copy(i + 1)
                for n in range(2):
                    act.wait_ge(down_done, 2 * i + n + 1)
                    act.activation(y_sb[:, n, :], bank[2 + n][:, :], ACT.Copy).then_inc(y_ready, 1)

            gather_copy(0)
            gather_t_copy(0)
            with act.Fori(0, NE) as i:
                expert_block(i)
            n_blk = further_blocks(act, expert_block)
            root(junk4[:, 2:3], eps, 1, table_ready)
            for t in range(TT):
                act.wait_ge(scat_out[t], 2 * n_blk + 1)
                act.activation(r_h[:, t * D:(t + 1) * D], acc_out[:, t, :], ACT.Square, accum_out=ss[:, t:t + 1]).then_inc(acc_sumsq, 1)
                act.wait_ge(acc_sumsq, t + 1)
                root(rstd[:, t:t + 1], ss[:, t:t + 1], D, root_out)
            for t in range(TT):
                for hf in range(2):
                    cols = slice(hf * D // 2, (hf + 1) * D // 2)
                    act.wait_ge(out_ready, 2 * t + hf + 1)
                    act.dma_start(out_v[:, t, cols], x3[:, t, cols]).then_inc(out_stored, 16)
            act.wait_ge(out_stored, 64)

        @block.vector
        def _(dve):
            order = Order(dve, o_dve)

            def signal(ins, s, value):
                ins.then_inc(s, 1)
                dve.wait_ge(s, value)

            def ada_steps(j):
                a = accs[j % 2]
                if j >= 2 * ND + 2:
                    dve.wait_ge(row_stored[j % 2], 16 * ((j - 2 * ND) // 2))
                elif j >= 2:
                    dve.wait_ge(ada_reduced, j - 1)
                slots = ADA_SLOTS - 1 if j < 2 * ND else ADA_SLOTS
                for s in range(slots):
                    dve.wait_ge(*((ada_ready[s], 16 * (j + 1)) if j < 2 * ND else (ada_late[s], 16 * (j + 1 - 2 * ND))))
                    for k in range(ADA_K):
                        kk = s * ADA_K + k
                        if kk == 0:
                            ins = dve.tensor_scalar(a, ada3[s][:, k, :], s_col[:, kk:kk + 1], None, ALU.mult)
                        else:
                            ins = dve.scalar_tensor_tensor(a, ada3[s][:, k, :], s_col[:, kk:kk + 1], a, ALU.mult, ALU.add)
                        if k < ADA_K - 1:
                            order(ins)
                        elif s < slots - 1:
                            signal(ins, *ada_slot_used(j, s))
                        else:
                            ins.then_inc(ada_sum_ready, 1)
                        if k % 2:
                            yield

            def ada_chunk(j):
                for _ in ada_steps(j):
                    pass

            def all_rows():
                for j in range(2 * ND, N_ADA):
                    yield from ada_steps(j)
            rows_left = all_rows()
            splits = [0]
            ahead = W_BUFS - 1
            NO_ROWS, IN_RATE, S_RATE = (0, 1), (2, 3), (7, 10)

            def split_upto(q, rate=NO_ROWS):
                while splits[0] < min(q, N_GRAN):
                    v = splits[0]
                    r, k = granules[v][:2]
                    dve.wait_ge(hi_ready, v + 1)
                    dve.tensor_tensor(w_lo[v % W_BUFS], ring3[r % 2][:, k:k + GK, :], w_hi[v % W_BUFS].bitcast(F32), ALU.subtract)\
                       .then_inc(lo_ready, 1)
                    splits[0] += 1
                    if (v - START[rate]) % rate[1] < rate[0] and v >= START[rate]:
                        next(rows_left, None)
            START = {NO_ROWS: N_GRAN, IN_RATE: after(1), S_RATE: after(G_GA[-1])}

            def parts_low(m, dst, hi, ready):
                dve.wait_ge(tr_out, m + 1)
                dve.tensor_tensor(dst, bank[6 + m % 2][:, :].rearrange("p (b s) -> p b s", b=4), hi.bitcast(F32), ALU.subtract)\
                   .then_inc(ready, 1)

            dve.wait_ge(root_x, 1)
            order(dve.reciprocal(rstd[:, 0:TT], rstd[:, 0:TT]))
            for t in range(TT):
                order(dve.tensor_scalar(h_tok[:, t, :], x3[:, t, :], rstd[:, t:t + 1], None, ALU.mult))
            dve.wait_ge(silu_c_ready, 1)
            dve.wait_ge(mod_consts, 48)
            for n in range(ND):
                ada_chunk(2 * n)
                ada_chunk(2 * n + 1)
                cols = slice(n * CW, (n + 1) * CW)
                dve.wait_ge(ada_reduced, 2 * n + 2)
                order(dve.scalar_tensor_tensor(a_row, bank[5][:, :], 1.0, g_pre[:, cols], ALU.add, ALU.mult))
                for t in range(TT):
                    order(dve.tensor_tensor(h_tok[:, t, cols], h_tok[:, t, cols], a_row, ALU.mult))
                    dve.tensor_tensor(h_tok[:, t, cols], h_tok[:, t, cols], bank[4][:, :], ALU.add).then_inc(h_ready, 1)
                for t in range(TT):
                    dst, hi = (v[:, 4 * n:4 * n + 4, t * P:(t + 1) * P] for v in (hT_lo, hT_hi))
                    parts_low(M_H + 2 * n + t, dst, hi, hT_lo_ready)
                split_upto(W_BUFS * (n + 1))

            dve.wait_ge(rope_consts, 64)
            for a in range(2):
                for t in range(TT):
                    order(dve.tensor_tensor(cosg[a][:, t, :], cos3[:, t, :], g_qk[:, a, :], ALU.mult))
                    sv = sin3[:, t, :].rearrange("p (a b c) -> p a b c", a=2, b=2)
                    gv = g_qk[:, a, :].rearrange("p (a b c) -> p a b c", a=2, b=2)
                    dv = sing[a][:, t, :].rearrange("p (a b c) -> p a b c", a=2, b=2)
                    for b in range(2):
                        order(dve.tensor_tensor(dv[:, :, b, :], sv[:, :, b, :], gv[:, :, 1 - b, :], ALU.mult))

            def rope(g, t):
                a = 0 if g < Q_CHUNKS else 1
                v = raw[:, t, :]
                v3 = v.rearrange("p (h d) -> p h d", h=HPC)
                dve.wait_ge(mm_out[pair_of[g]], out_count(g, t))
                if g or t:
                    dve.wait_ge(rope_done, 2 * g + t)
                dve.wait_ge(root_qk, 2 * g + t + 1)
                rq = rms_q[:, t * HPC:(t + 1) * HPC]
                order(dve.reciprocal(rq, rq))
                order(dve.tensor_tensor(v3, v3, rq.unsqueeze(2).to_broadcast([P, HPC, HD]), ALU.mult))
                if g:
                    dve.wait_ge(tr_done, M_Q + 2 * (g - 1) + t + 1)
                q3 = qr[:, t, :].rearrange("p (h d) -> p h d", h=HPC)
                order(dve.tensor_tensor(q3, v3, cosg[a][:, t, :].unsqueeze(1).to_broadcast([P, HPC, HD]), ALU.mult))
                v5 = v.rearrange("p (h a b c) -> p h a b c", h=HPC, a=2, b=2)
                r5 = rope_tmp.rearrange("p (h a b c) -> p h a b c", h=HPC, a=2, b=2)
                s4 = sing[a][:, t, :].rearrange("p (a b c) -> p a b c", a=2, b=2)
                for b in range(2):
                    order(dve.tensor_tensor(r5[:, :, :, b, :], v5[:, :, :, 1 - b, :],
                                            s4[:, :, b, :].unsqueeze(1).to_broadcast([P, HPC, 2, HD // 4]), ALU.mult))
                dve.tensor_tensor(qr[:, t, :], qr[:, t, :], rope_tmp, ALU.add).then_inc(rope_done, 1)

            for g in range(8):
                split_upto(after(g) + ahead, IN_RATE)
                if g <= Q_CHUNKS:
                    for t in range(TT):
                        rope(g, t)

            for _ in range(KD // 2):
                next(rows_left)

            def row_max(h):
                b = 2 * (h % 2)
                dve.wait_ge(score_done, h + 1)
                if h >= 2:
                    dve.wait_ge(exp_done, 2 * (h - 1))
                order(dve.tensor_reduce(mx[:, b:b + 2], bank[h % 2][:, :].rearrange("p (t s) -> p t s", t=TT), AX_X, ALU.max))
                dve.tensor_scalar(nmx[:, b:b + 2], mx[:, b:b + 2], -SCALE, None, ALU.mult).then_inc(nmx_ready, 1)

            def normalise(h):
                b = 2 * (h % 2)
                dve.wait_ge(exp_done, 2 * (h + 1))
                order(dve.reciprocal(rinv[:, b:b + 2], rs[:, b:b + 2]))
                for t in range(TT):
                    last = dve.tensor_scalar(probs[h % 2][:, t, :], probs[h % 2][:, t, :], rinv[:, b + t:b + t + 1], None, ALU.mult)
                last.then_inc(probs_ready, 1)

            def pt_copy(h):
                dve.wait_ge(pt_done, h + 1)
                if h >= 2:
                    dve.wait_ge(pv_done, h - 1)
                dve.tensor_copy(pT[h % 2], bank[2 + h % 2][:, :].rearrange("p (s q) -> p s q", s=TT)).then_inc(pt_ready, 1)

            for i in range(1, KF, 2):
                dve.wait_ge(f1_done, i + 1)
                dve.tensor_copy(ab[:, i, :], bank[i % 4][:, :]).then_inc(ab_ready[1], 1)
            for i in range(1, KF, 2):
                dve.wait_ge(f2_done, i + 1)
                dve.tensor_copy(fT[:, i, :], bank[i % 4][:, 0:SEQ]).then_inc(fT_ready[1], 1)

            row_max(0)
            for h in range(NH):
                if h + 1 < NH:
                    row_max(h + 1)
                normalise(h)
                if h >= 1:
                    pt_copy(h - 1)
                split_upto(grans(G_GA[0])[0] + 2 * h + 4)
                for _ in range(2):
                    next(rows_left)
            pt_copy(NH - 1)

            split_upto(after(G_GA[-1]) + ahead, S_RATE)
            dve.wait_ge(fT_hi_ready, 1)
            dve.tensor_tensor(fT_lo, fT, fT_hi.bitcast(F32), ALU.subtract).then_inc(fT_lo_ready, 1)
            for n in range(ND):
                if n == ND - 1:
                    split_upto(after(G_GF[n]) + ahead, S_RATE)
                    for p in range(2):
                        dve.wait_ge(aT_hi_ready, p + 1)
                        dve.tensor_tensor(aT_lo[:, 8 * p:8 * p + 8, :], qT[:, 8 * p:8 * p + 8, :],
                                          aT_hi[:, 8 * p:8 * p + 8, :].bitcast(F32), ALU.subtract).then_inc(aT_lo_ready, 1)
                split_upto(after(G_FO[n]) + ahead, S_RATE)
                g, cols = G_FO[n], slice(n * CW, (n + 1) * CW)
                dve.wait_ge(mm_done, g + 1)
                for t in range(TT):
                    dve.wait_ge(mm_out[0], out_count(G_GF[n], t))
                    dve.tensor_tensor(mixed[:, t, cols], gate3[:, t, :], bank[2 + t][:, :], ALU.mult).then_inc(mm_out[1], 1)

            def mixed_low(n):
                for t in range(TT):
                    dst, hi = (v[:, 4 * n:4 * n + 4, t * P:(t + 1) * P] for v in (mT_lo, mT_hi))
                    parts_low(M_MIX + 2 * n + t, dst, hi, mT_lo_ready)

            dve.wait_ge(ga_ready, 2 * ND)
            for n in range(ND):
                g, cols = G_AO[n], slice(n * CW, (n + 1) * CW)
                split_upto(after(g) + ahead, S_RATE)
                dve.wait_ge(mm_done, g + 1)
                for t in range(TT):
                    signal(dve.tensor_tensor(ga_sb[:, t, cols], ga_sb[:, t, cols], bank[2 * pair_of[g] + t][:, :], ALU.mult),
                           mm_out[pair_of[g]], out_count(g, t))
                    dve.tensor_tensor(mixed[:, t, cols], mixed[:, t, cols], ga_sb[:, t, cols], ALU.add).then_inc(mixed_ready, 1)
                if n:
                    mixed_low(n - 1)
            split_upto(after(G_MO[0]), S_RATE)
            mixed_low(ND - 1)

            split_upto(after(G_MO[0]) + ahead)
            dve.wait_ge(rows_a, 64)
            signal(dve.tensor_tensor(rows[0], rows[0], rows[1], ALU.mult), gg1_ready, 1)
            order(dve.scalar_tensor_tensor(rows[2], rows[2], 1.0, rows[3], ALU.add, ALU.mult))
            for n in range(ND):
                cols = slice(n * CW, (n + 1) * CW)
                split_upto(after(G_MO[n]) + ahead)
                for t in range(TT):
                    dve.wait_ge(y1_ready, 2 * n + t + 1)
                    order(dve.tensor_tensor(y1[:, t, cols], y1[:, t, cols], rows[0][:, cols], ALU.mult))
            dve.wait_ge(x_again, 16)
            dve.wait_ge(root_y, 1)
            order(dve.reciprocal(rstd[:, 0:TT], rstd[:, 0:TT]))
            for t in range(TT):
                dve.scalar_tensor_tensor(x3[:, t, :], y1[:, t, :], rstd[:, t:t + 1], x3[:, t, :], ALU.mult, ALU.add)\
                   .then_inc(x1_ready, 1)
            dve.wait_ge(x1_ready, TT)
            dve.wait_ge(rows_b, 16)
            dve.wait_ge(mm_done, G_MO[-1] + 1)
            for t in range(TT):
                dve.wait_ge(root_x1, t + 1)
                order(dve.reciprocal(rinv[:, t:t + 1], rinv[:, t:t + 1]))
                for n in range(ND):
                    cols = slice(n * CW, (n + 1) * CW)
                    order(dve.scalar_tensor_tensor(h2[:, t, cols], x3[:, t, cols], rinv[:, t:t + 1], rows[2][:, cols],
                                                   ALU.mult, ALU.mult))
                    dve.tensor_tensor(h2[:, t, cols], h2[:, t, cols], rows[1][:, cols], ALU.add).then_inc(h2_ready, 1)
            for t in range(TT):
                signal(dve.memset(acc_out[:, t, :], 0.0), scat_out[t], 1)

            def select(col):
                for t in range(TT):
                    last = dve.tensor_scalar(p_mat[:, t, :], k_slot, rank_b[:, t, col], None, ALU.is_equal)
                last.then_inc(p_ready, 1)

            dve.wait_ge(logits_done, 1)
            dve.tensor_copy(logitsT[0:NR, :], bank[4][0:NR, 0:SEQ]).then_inc(logitsT_ready, 1)
            dve.wait_ge(logits_done, 2)
            order(dve.tensor_copy(lg, bank[5][:, 2 * P:4 * P].rearrange("p (t n) -> p t n", t=TT)[:, :, 0:NR]))

            def bc(v, n):
                return v.unsqueeze(2).to_broadcast([P, TT, n])

            def kbc(v, n):
                return v.unsqueeze(1).to_broadcast([P, TT, n])

            def first_max(oh, vals, top, work, low, k_idx, n):
                order(dve.tensor_reduce(top, vals, AX_X, ALU.max))
                order(dve.tensor_tensor(work, vals, bc(top, n), ALU.is_equal))
                order(dve.tensor_tensor(work, work, kbc(k_idx, n), ALU.mult))
                order(dve.tensor_reduce(low, work, AX_X, ALU.min))
                order(dve.tensor_tensor(oh, kbc(k_idx, n), bc(low, n), ALU.is_equal))

            gl = lg[:, :, 0:NG]
            first_max(oh_g, gl, gm, ga, gmin, k_g4, NG)
            signal(dve.tensor_tensor(gsh, gl, bc(gm, NG), ALU.subtract), shifted_ready, 1)
            order(dve.tensor_scalar(ga, oh_g, -1.0, FAR, ALU.add, ALU.mult))
            for t in range(TT):
                order(dve.tensor_tensor(elm[:, t, :].rearrange("p (g e) -> p g e", g=NG),
                                        lg[:, t, NG:NR].rearrange("p (g e) -> p g e", g=NG),
                                        ga[:, t, :].unsqueeze(2).to_broadcast([P, NG, EG]), ALU.add))
            first_max(oh1, elm, m1, e_tmp, i1, k_e32, NE)
            order(dve.scalar_tensor_tensor(elm, oh1, -2 * FAR, elm, ALU.mult, ALU.add))
            first_max(oh2, elm, m2, e_tmp, i1, k_e32, NE)
            signal(dve.tensor_tensor(de, m2, m1, ALU.subtract), shifted_ready, 2)
            signal(dve.tensor_tensor(member, oh1, oh2, ALU.add), member_ready, 1)
            dve.wait_ge(route_exp, 2)
            order(dve.tensor_reduce(gw, gex, AX_X, ALU.add))
            order(dve.tensor_scalar(w1, w2, 1.0, None, ALU.add))
            order(dve.tensor_tensor(w1, w1, gw, ALU.mult))
            order(dve.reciprocal(w1, w1))
            order(dve.tensor_tensor(w2, w2, w1, ALU.mult))
            order(dve.tensor_tensor(comb, oh1, bc(w1, NE), ALU.mult))
            order(dve.tensor_tensor(e_tmp, oh2, bc(w2, NE), ALU.mult))
            order(dve.tensor_tensor(comb, comb, e_tmp, ALU.add))
            dve.wait_ge(ranks_done, 1)
            order(dve.scalar_tensor_tensor(rank_m, bank[5][:, 0:2 * NE].rearrange("p (t n) -> p t n", t=TT), 1.0, member,
                                           ALU.add, ALU.mult))
            order(dve.tensor_scalar(rank_m, rank_m, -1.0, None, ALU.add))
            order(dve.tensor_copy(rank_b[:, :, 0:NE], rank_m))
            select(slice(0, 1))
            order(dve.tensor_copy(w_b[:, :, 0:NE], comb))
            for b in range(BMAX):
                order(dve.tensor_scalar(rank_c[:, :, b * NE:(b + 1) * NE], rank_m, -float(CAP * (b + 1)), None, ALU.add))
                last = dve.tensor_scalar(flags[:, b * NE:(b + 1) * NE], bank[5][:, 2 * NE:3 * NE], CAP * (b + 1) + 0.5, None, ALU.is_gt)
            signal(last, flags_ready, 1)
            dve.wait_ge(flagsT_done, 1)
            dve.tensor_copy(flagsT[0:NCAND, :], bank[4][0:NCAND, 128:256]).then_inc(flagsT_ready, 1)
            order(dve.tensor_reduce(nover, flags, AX_X, ALU.add))
            dve.wait_ge(prefix_done, 1)
            order(dve.tensor_tensor(sel, bank[4][:, 256:256 + NCAND].unsqueeze(1).to_broadcast([P, NOVER, NCAND]),
                                    k_j8.unsqueeze(2).to_broadcast([P, NOVER, NCAND]), ALU.is_equal))
            order(dve.tensor_tensor(sel, sel, flags.unsqueeze(1).to_broadcast([P, NOVER, NCAND]), ALU.mult))
            for t in range(TT):
                order(dve.tensor_tensor(selx, sel, rank_c[:, t, :].unsqueeze(1).to_broadcast([P, NOVER, NCAND]), ALU.mult))
                order(dve.tensor_reduce(rank_b[:, t, NE:NBLK], selx, AX_X, ALU.add))
                for b in range(BMAX):
                    order(dve.tensor_tensor(selx[:, :, b * NE:(b + 1) * NE], sel[:, :, b * NE:(b + 1) * NE],
                                            comb[:, t, :].unsqueeze(1).to_broadcast([P, NOVER, NE]), ALU.mult))
                order(dve.tensor_reduce(w_b[:, t, NE:NBLK], selx, AX_X, ALU.add))
            order(dve.tensor_tensor(selx, sel, k_ec.unsqueeze(1).to_broadcast([P, NOVER, NCAND]), ALU.mult))
            order(dve.tensor_reduce(eblk, selx, AX_X, ALU.add))
            order(dve.tensor_scalar(meta[:, 0:1], nover, float(NE), None, ALU.add))
            order(dve.tensor_copy(meta[:, 1:2], nover))
            signal(dve.tensor_copy(meta[:, 2:2 + NOVER], eblk), meta_ready, 1)
            def expert_block(i):
                dve.wait_ge(p_ready, i + 1)
                for t in range(TT):
                    last = dve.tensor_scalar(pw[:, t, :, :], p_mat[:, t, :].unsqueeze(1).to_broadcast([P, 2, SLOTS]),
                                             w_b[:, t, bass.ds(i, 1)], None, ALU.mult)
                last.then_inc(pw_ready, 1)
                dve.wait_ge(gather_done, 2 * i + 2)
                dve.wait_ge(pw_ready, i + 1)
                select(bass.ds(i + 1, 1))
                dve.wait_ge(gu_done, i + 1)
                dve.tensor_copy(gu, bank[0][:, :]).then_inc(gu_ready, 1)
                dve.wait_ge(silu_ready, i + 1)
                dve.tensor_tensor(act_sb, silu_sb, bank[1][:, :].rearrange("p (f s) -> p f s", f=KFF)[:, :, SLOTS:2 * SLOTS],
                                  ALU.mult).then_inc(act_ready, 1)
                for n in range(2):
                    for t in range(TT):
                        dve.wait_ge(scat_done, 4 * i + 2 * n + t + 1)
                        for g in range(2):
                            cols = slice((2 * g + n) * CW, (2 * g + n + 1) * CW)
                            last = dve.tensor_tensor(acc_out[:, t, cols], acc_out[:, t, cols], bank[4 + 2 * t + g][:, :], ALU.add)
                        last.then_inc(scat_out[t], 1)
                for t in range(TT):
                    dve.wait_ge(scat_out[t], 2 * i + 3)

            dve.wait_ge(rows_c, 32)
            order(dve.tensor_tensor(rows[2], rows[2], rows[3], ALU.mult))
            with dve.Fori(0, NE) as i:
                expert_block(i)
            further_blocks(dve, expert_block)
            for t in range(TT):
                order(dve.tensor_tensor(gained[t], acc_out[:, t, :], rows[2], ALU.mult))
            for t in range(TT):
                dve.wait_ge(root_out, t + 1)
                order(dve.reciprocal(rstd[:, t:t + 1], rstd[:, t:t + 1]))
                for hf in range(2):
                    cols = slice(hf * D // 2, (hf + 1) * D // 2)
                    dve.scalar_tensor_tensor(x3[:, t, cols], gained[t][:, cols], rstd[:, t:t + 1], x3[:, t, cols],
                                             ALU.mult, ALU.add).then_inc(out_ready, 1)


_INS = ["x", "c", "w_ada", "b_ada", "g_pre_mix", "g_post_mix", "w_in", "q_norm_g", "k_norm_g", "w_attn_out", "w_fourier_out",
        "w_mix_out", "g_pre_ffn", "g_post_ffn", "w_group_router", "b_group_router", "w_expert_router", "b_expert_router",
        "w_exp_gate", "w_exp_up", "w_exp_down"]


def shape_constants():
    import numpy as np
    grid_w, theta = 64, 10000.0
    pos = np.arange(SEQ)
    n_freq = HD // 4
    inv = theta ** (-np.arange(n_freq) / n_freq)
    row = (pos // grid_w)[:, None] * inv
    col = (pos % grid_w)[:, None] * inv
    ang = np.concatenate([row, row, col, col], axis=-1)
    sign = np.tile(np.repeat([-1.0, 1.0], n_freq), 2)
    w = 2 * np.pi * (np.outer(np.arange(SEQ), np.arange(SEQ)) % SEQ) / SEQ
    row_k = np.zeros(108 + NCAND)
    row_k[0:SLOTS] = np.where(np.arange(SLOTS) < CAP, np.arange(SLOTS), 1e6)
    row_k[64:68] = np.arange(NG) - NG
    row_k[68:100] = np.arange(NE) - NE
    row_k[100:108] = np.arange(NOVER)
    row_k[108:] = np.tile(np.arange(NE), BMAX)
    tables = {
        "k_cos": np.cos(ang), "k_sin": np.sin(ang) * sign,
        "k_dft_tok": np.concatenate([np.cos(w), np.sin(w)], axis=1) / 16,
        "k_dft_ch": np.concatenate([np.cos(w), -np.sin(w)], axis=1) / 16,
        "k_ident": np.eye(P), "k_upper": np.triu(np.ones((P, P)), 1), "k_row": row_k,
    }
    return {k: np.ascontiguousarray(v.astype(np.float32)) for k, v in tables.items()}


def kernel(**inputs):
    import numpy as np
    import concourse.bacc as bacc
    from concourse.bass_utils import run_bass_kernel_spmd

    nc = bacc.Bacc("TRN2", target_bir_lowering=False, num_devices=1)
    arrays, args = {}, []
    for name, a in [(n, inputs[n]) for n in _INS] + list(shape_constants().items()):
        a = np.ascontiguousarray(a)
        arrays[f"in_{name}"] = a
        args.append(nc.dram_tensor(f"in_{name}", a.shape, mybir.dt.from_np(a.dtype), kind="ExternalInput").ap())
    args.append(nc.dram_tensor("out_x", (1, SEQ, D), F32, kind="ExternalOutput").ap())
    build(nc, *args)
    r = run_bass_kernel_spmd(nc, [arrays], core_ids=[0])
    return r.results[0]["out_x"]
```
